# Optimizing a Trainium2 kernel written in Bass

```python
import math
import jax, jax.numpy as jnp
from jax import lax
import numpy as np

D_MODEL = 1024
BATCH = 1
SEQ = 256
DEPTH = 2

MEM_LEN = 256
EPS = 1e-6
DA_HEADS = 4
DA_HEAD_DIM = 64
DA_WIDTH = DA_HEADS * 2 * DA_HEAD_DIM
ROT_DIM = DA_HEAD_DIM // 4
ROPE_THETA = 500000.0
Q_BLOCK = 128
POOL_WINDOWS = (2, 4, 8, 16)
POOL_GROUPS = 4
POOL_GROUP_CH = 128
POOL_WIDTH = POOL_GROUPS * POOL_GROUP_CH
CHUNK = 128
SG_GROUPS = 4
SG_WIDTH = 512
SG_GROUP_CH = SG_WIDTH // SG_GROUPS
N_BRANCH = 3
BRANCH_WIDTH = 512
X_HEADS = 4
X_HEAD_DIM = D_MODEL // X_HEADS
PEER_HEADS = 8
N_KEYS = 128
N_EXPERTS = N_KEYS * N_KEYS
PEER_TOPK = 16
PEER_QDIM = 256
PEER_HALF = PEER_QDIM // 2
PEER_BLOCK = 128
IN_WIDTH = 3 * DA_WIDTH + POOL_WIDTH + 2 * SG_WIDTH + N_BRANCH * D_MODEL

kernel_name = "hybrid_diffattn_pool_sgmlp_peer"

def rmsnorm(x, g):
    xf = x.astype(jnp.float32)
    y = xf * lax.rsqrt(jnp.mean(xf * xf, axis=-1, keepdims=True) + EPS)
    return (y * g.astype(jnp.float32)).astype(x.dtype)

def layernorm(x, g, b):
    xf = x.astype(jnp.float32)
    mu = jnp.mean(xf, axis=-1, keepdims=True)
    var = jnp.mean(jnp.square(xf - mu), axis=-1, keepdims=True)
    y = (xf - mu) * lax.rsqrt(var + EPS) * g.astype(jnp.float32) + b.astype(jnp.float32)
    return y.astype(x.dtype)

def rope_tables(positions):
    inv = ROPE_THETA ** (-jnp.arange(0, ROT_DIM, 2, dtype=jnp.float32) / ROT_DIM)
    ang = positions.astype(jnp.float32)[..., None] * inv
    return jnp.cos(ang), jnp.sin(ang)

def apply_partial_rope(x, cos, sin):
    half = ROT_DIM // 2
    xf = x[..., :ROT_DIM].astype(jnp.float32)
    x1, x2 = xf[..., :half], xf[..., half:]
    c, s = cos[:, :, None, :], sin[:, :, None, :]
    rot = jnp.concatenate([x1 * c - x2 * s, x1 * s + x2 * c], axis=-1).astype(x.dtype)
    return jnp.concatenate([rot, x[..., ROT_DIM:]], axis=-1)

def diff_attention(q, k, v, cos, sin, lam_qk, subln_g, lam_init):
    B, S, _ = q.shape
    H, DH = DA_HEADS, DA_HEAD_DIM
    q = apply_partial_rope(q.reshape(B, S, H * 2, DH), cos, sin).reshape(B, S, H, 2, DH)
    k = apply_partial_rope(k.reshape(B, S, H * 2, DH), cos, sin).reshape(B, S, H, 2, DH)
    v = v.reshape(B, S, H, 2 * DH)
    lq = lam_qk.astype(jnp.float32)
    lam = jnp.exp(jnp.sum(lq[0] * lq[1])) - jnp.exp(jnp.sum(lq[2] * lq[3])) + lam_init
    nb = S // Q_BLOCK
    qb = q.reshape(B, nb, Q_BLOCK, H, 2, DH).transpose(1, 0, 3, 4, 2, 5)
    kt = k.transpose(0, 2, 3, 1, 4)
    vt = v.transpose(0, 2, 1, 3)
    key_pos = jnp.arange(S)
    scale = DH ** -0.5

    def block(args):
        qblk, start = args
        s = jnp.einsum('bhmqd,bhmkd->bhmqk', qblk, kt).astype(jnp.float32) * scale
        causal = key_pos[None, :] <= (start + jnp.arange(Q_BLOCK))[:, None]
        p = jax.nn.softmax(jnp.where(causal, s, -jnp.inf), axis=-1)
        a = p[:, :, 0] - lam * p[:, :, 1]
        return jnp.einsum('bhqk,bhkd->bhqd', a.astype(vt.dtype), vt)

    o = lax.map(block, (qb, jnp.arange(nb) * Q_BLOCK))
    o = o.transpose(1, 0, 3, 2, 4).reshape(B, S, H, 2 * DH)
    o = rmsnorm(o, subln_g) * (1.0 - lam_init)
    return o.reshape(B, S, H * 2 * DH)

def multiscale_pool(p, w_pool, pool_scale):
    B, S, _ = p.shape
    pg = p.reshape(B, S, POOL_GROUPS, POOL_GROUP_CH).astype(jnp.float32)
    cs = jnp.concatenate([jnp.zeros_like(pg[:, :1]), lax.cumsum(pg, axis=1)], axis=1)
    t = jnp.arange(S)
    groups = []
    for g, w in enumerate(POOL_WINDOWS):
        cg = cs[:, :, g]
        lo = jnp.maximum(t + 1 - w, 0)
        cnt = jnp.minimum(t + 1, w).astype(jnp.float32)
        mean = (cg[:, 1:] - cg[:, lo]) / cnt[None, :, None]
        groups.append(mean - pg[:, :, g])
    d = jnp.stack(groups, axis=2).astype(p.dtype)
    y = jnp.einsum('bsgc,gce->bsge', d, w_pool)
    return y.reshape(B, S, POOL_WIDTH) * pool_scale

def chunk_spatial_gate(u, v, ln_g, ln_b, w_s, b_s):
    B, S, _ = v.shape
    vn = layernorm(v, ln_g, ln_b).reshape(B, S // CHUNK, CHUNK, SG_GROUPS, SG_GROUP_CH)
    ws = w_s * jnp.tril(jnp.ones((CHUNK, CHUNK), w_s.dtype))
    mixed = jnp.einsum('gts,bnsgc->bntgc', ws, vn) + b_s.T[None, None, :, :, None]
    return u * mixed.reshape(B, S, SG_WIDTH)

def memory_cross_attention(h, m, w_q, w_kv, w_o):
    B, S, _ = h.shape
    M = m.shape[1]
    q = (h @ w_q).reshape(B, S, X_HEADS, X_HEAD_DIM)
    kv = (m @ w_kv).reshape(B, M, 2, X_HEADS, X_HEAD_DIM)
    s = jnp.einsum('bshd,bmhd->bhsm', q, kv[:, :, 0]).astype(jnp.float32) * (X_HEAD_DIM ** -0.5)
    p = jax.nn.softmax(s, axis=-1).astype(h.dtype)
    o = jnp.einsum('bhsm,bmhd->bshd', p, kv[:, :, 1])
    return o.reshape(B, S, D_MODEL) @ w_o

def peer_ffn(x, w_pq, sub_keys, peer_u, peer_v):
    B, S, D = x.shape
    q = jnp.einsum('bsd,dhk->bshk', x, w_pq).reshape(B, S, PEER_HEADS, 2, PEER_HALF)
    sc = jnp.einsum('bshpk,hpnk->bshpn', q, sub_keys).astype(jnp.float32)
    s_top, i_top = lax.top_k(sc, PEER_TOPK)
    cand = (s_top[..., 0, :, None] + s_top[..., 1, None, :]).reshape(B, S, PEER_HEADS, PEER_TOPK * PEER_TOPK)
    cand_idx = (i_top[..., 0, :, None] * N_KEYS + i_top[..., 1, None, :]).reshape(B, S, PEER_HEADS, PEER_TOPK * PEER_TOPK)
    f_s, f_pos = lax.top_k(cand, PEER_TOPK)
    e_idx = jnp.take_along_axis(cand_idx, f_pos, axis=-1)
    gates = jax.nn.softmax(f_s, axis=-1).astype(x.dtype)
    T = B * S
    nblk = T // PEER_BLOCK
    xt = x.reshape(nblk, PEER_BLOCK, D)
    it = e_idx.reshape(nblk, PEER_BLOCK, PEER_HEADS * PEER_TOPK)
    gt = gates.reshape(nblk, PEER_BLOCK, PEER_HEADS * PEER_TOPK)

    def blk(args):
        xb, ib, gb = args
        ub = peer_u[ib]
        a = jax.nn.gelu(jnp.einsum('td,ted->te', xb, ub), approximate=False)
        vb = peer_v[ib]
        return jnp.einsum('te,ted->td', a * gb, vb)

    return lax.map(blk, (xt, it, gt)).reshape(B, S, D)

def setup_inputs(seed: int = 0) -> dict:
    key = jax.random.key(seed)
    ks = jax.random.split(key, 32)
    L, D = DEPTH, D_MODEL

    def nrm(k, shape, scale):
        return jax.random.normal(k, shape, jnp.float32) * scale

    def gain(k, shape):
        return 1.0 + 0.05 * jax.random.normal(k, shape, jnp.float32)

    start = jax.random.randint(ks[2], (BATCH, 1), 0, 1024, dtype=jnp.int32)
    positions = (start + jnp.arange(SEQ, dtype=jnp.int32)[None, :]).astype(jnp.int32)
    return {
        'x': nrm(ks[0], (BATCH, SEQ, D), 1.0),
        'mem': nrm(ks[1], (BATCH, MEM_LEN, D), 1.0),
        'positions': positions,
        'g_mix': gain(ks[3], (L, D)),
        'w_in': nrm(ks[4], (L, D, IN_WIDTH), D ** -0.5),
        'lam_qk': nrm(ks[5], (L, 4, DA_HEAD_DIM), 0.1),
        'subln_g': gain(ks[6], (L, 2 * DA_HEAD_DIM)),
        'w_pool': nrm(ks[7], (L, POOL_GROUPS, POOL_GROUP_CH, POOL_GROUP_CH), POOL_GROUP_CH ** -0.5),
        'pool_scale': gain(ks[8], (L, POOL_WIDTH)),
        'sg_ln_g': gain(ks[9], (L, SG_WIDTH)),
        'sg_ln_b': nrm(ks[10], (L, SG_WIDTH), 0.02),
        'w_spatial': nrm(ks[11], (L, SG_GROUPS, CHUNK, CHUNK), 0.5 * CHUNK ** -0.5),
        'b_spatial': gain(ks[12], (L, SG_GROUPS, CHUNK)),
        'w_branch': nrm(ks[13], (L, N_BRANCH, BRANCH_WIDTH, D), BRANCH_WIDTH ** -0.5),
        'w_out': nrm(ks[14], (L, D, D), D ** -0.5),
        'g_cross': gain(ks[15], (L, D)),
        'g_mem': gain(ks[16], (L, D)),
        'w_xq': nrm(ks[17], (L, D, D), D ** -0.5),
        'w_xkv': nrm(ks[18], (L, D, 2 * D), D ** -0.5),
        'w_xo': nrm(ks[19], (L, D, D), D ** -0.5),
        'g_ffn': gain(ks[20], (L, D)),
        'w_pq': nrm(ks[21], (L, D, PEER_HEADS, PEER_QDIM), D ** -0.5),
        'sub_keys': nrm(ks[22], (L, PEER_HEADS, 2, N_KEYS, PEER_HALF), PEER_HALF ** -0.5),
        'peer_u': nrm(ks[23], (L, N_EXPERTS, D), D ** -0.5),
        'peer_v': nrm(ks[24], (L, N_EXPERTS, D), 0.2),
        'g_final': gain(ks[25], (D,)),
    }

def reference(x, mem, positions, g_mix, w_in, lam_qk, subln_g, w_pool, pool_scale, sg_ln_g, sg_ln_b, w_spatial, b_spatial, w_branch, w_out, g_cross, g_mem, w_xq, w_xkv, w_xo, g_ffn, w_pq, sub_keys, peer_u, peer_v, g_final):
    B, S, D = x.shape
    cos, sin = rope_tables(positions)
    sizes = (DA_WIDTH, DA_WIDTH, DA_WIDTH, POOL_WIDTH, SG_WIDTH, SG_WIDTH)
    pts = []
    acc = 0
    for sz in sizes:
        acc += sz
        pts.append(acc)
    for l in range(DEPTH):
        lam_init = 0.8 - 0.6 * math.exp(-0.3 * l)
        xn = rmsnorm(x, g_mix[l])
        z = xn @ w_in[l]
        q_a, k_a, v_a, p_in, u_in, v_in, gate_in = jnp.split(z, pts, axis=-1)
        a_out = diff_attention(q_a, k_a, v_a, cos, sin, lam_qk[l], subln_g[l], lam_init)
        p_out = multiscale_pool(p_in, w_pool[l], pool_scale[l])
        s_out = chunk_spatial_gate(u_in, v_in, sg_ln_g[l], sg_ln_b[l], w_spatial[l], b_spatial[l])
        branches = jnp.stack([a_out, p_out, s_out], axis=2)
        proj = jnp.einsum('bsnc,ncd->bsnd', branches, w_branch[l])
        gates = jax.nn.sigmoid(gate_in.reshape(B, S, N_BRANCH, D))
        merged = jnp.sum(gates * proj, axis=2)
        x = x + merged @ w_out[l]
        x = x + memory_cross_attention(rmsnorm(x, g_cross[l]), rmsnorm(mem, g_mem[l]), w_xq[l], w_xkv[l], w_xo[l])
        x = x + peer_ffn(rmsnorm(x, g_ffn[l]), w_pq[l], sub_keys[l], peer_u[l], peer_v[l])
    return rmsnorm(x, g_final)


_drawn_inputs = setup_inputs


def setup_inputs(seed=0):
    import zlib

    import numpy as np

    out = dict(_drawn_inputs(seed))
    spreads = {}
    factors = {'sg_ln_g': 3.927, 'sg_ln_b': 7.756, 'g_cross': 5.57, 'g_mem': 4.469, 'g_ffn': 2.997}
    for name, (base, spread) in spreads.items():
        noise = np.random.default_rng([zlib.crc32(name.encode()), seed]).standard_normal(out[name].shape)
        drawn = base * np.exp(spread * noise) if base else spread * noise
        out[name] = __import__('jax').numpy.asarray(drawn.astype(out[name].dtype))
    for name, factor in factors.items():
        out[name] = (out[name] * factor).astype(out[name].dtype)
    return out
```

```python
from contextlib import ExitStack

import numpy as np

import concourse.bass as bass
from concourse import mybir

F32 = mybir.dt.float32
BF16 = mybir.dt.bfloat16
I32 = mybir.dt.int32
U32 = mybir.dt.uint32
ALU = mybir.AluOpType
ACT = mybir.ActivationFunctionType
AX = mybir.AxisListType.X
ds = bass.ds

P = 128
L = 2
D = 1024
T = 256
NB = T // P
KC = D // P
EPS = 1e-6
DA_HEADS = 4
DA_DIM = 64
ROT = 16
HALF = ROT // 2
ROPE_THETA = 500000.0
WINDOWS = (2, 4, 8, 16)
X_HEADS = 4
X_SCALE = float(D // X_HEADS) ** -0.5
DA_SCALE = float(DA_DIM) ** -0.5
HEADS = 8
NK = 128
TOPK = 16
BW = 512
MASKED = -1e30
LOWEST = -3e38

PANEL = 4096
Z_PANEL, GATE_PANEL, KV_PANEL, BRANCH_PANEL, OUT_PANEL, XQ_PANEL, XO_PANEL, PQ_PANEL, KEY_PANEL = \
    0, 6, 12, 16, 19, 21, 23, 25, 29
PANELS = 30
PSLOTS = 3

PARAMS = {}
_at = 0
for _name, _n in (("g_mix", 8), ("g_cross", 8), ("g_mem", 8), ("g_ffn", 8), ("pool_scale", 4), ("b_spatial", 4),
                  ("lam_init", 1), ("one_less", 1), ("lam_qk", 256), ("subln_g", 128), ("sg_ln_g", 512),
                  ("sg_ln_b", 512), ("g_ffn_row", 1024), ("w_spatial", 512), ("w_pool", 512)):
    PARAMS[_name] = (_at, _at + _n)
    _at += _n
PARAM_COLS = _at

CONSTS = {}
_at = 0
for _name, _n in (("ident", 128), ("mask", 256), ("pool", 4 * 384), ("triu", 128), ("iota", 16), ("inv", 8),
                  ("expert_base", L)):
    CONSTS[_name] = (_at, _at + _n)
    _at += _n
CONST_COLS = _at

PROJ = ([f"z{p}{b}" for p in range(6) for b in range(2)] + ["pd0", "pd1", "g00", "g01", "g10", "g11", "av0"]
        + ["g20", "g21", "sm0", "sm1", "g30", "g31", "av1", "py0", "py1", "g40", "g41", "g50", "g51"]
        + [f"km{i}" for i in range(4)] + [f"vm{i}" for i in range(4)]
        + [f"br{n}{b}{h}" for n in range(3) for b in range(2) for h in range(2)]
        + [f"wo{i}" for i in range(4)] + [f"xq{i}" for i in range(4)] + [f"co{i}" for i in range(4)]
        + [f"xo{i}" for i in range(4)] + [f"pq{i}" for i in range(8)] + [f"sc{i}" for i in range(8)])
TRANS = [k + str(i) for k, n in (("nA", 4), ("qk", 4), ("a", 4), ("o", 2), ("s", 2), ("m", 4), ("nC", 4),
                                 ("e", 4), ("nF", 4)) for i in range(n)]
PU, TU = len(PROJ), len(TRANS)
assert PU % 4 == 0 and TU % 2 == 0
MEM_TU = 4
LAST_OF_PANEL = ([f"z{k}1" for k in range(6)] + [f"g{k}1" for k in range(6)] + ["km1", "km3", "vm1", "vm3"]
                 + [f"br{n}11" for n in range(3)] + ["wo1", "wo3", "xq1", "xq3", "xo1", "xo3"]
                 + [f"pq{2 * k + 1}" for k in range(4)] + ["sc7"])
assert len(LAST_OF_PANEL) == PANELS

SLOTS = 8
STEPS = NB * HEADS
TILES = STEPS * TOPK
TOPS = STEPS + 1


def trunk(nc, x_in, mem_in, pos_in, stream, params_in, consts_in, g_final, experts, out):
    ctx = ExitStack()
    with ctx:
        def sb(name, shape, dt=F32):
            return ctx.enter_context(nc.sbuf_tensor(name, shape, dt))

        def sem(name):
            return ctx.enter_context(nc.semaphore(name))

        x = sb("x", [P, NB, D])
        xn = sb("xn", [P, NB, D])
        actT = sb("actT", [P, KC, T])
        memT0 = sb("memT0", [P, KC, T])
        params = sb("params", [P, PARAM_COLS])
        consts = sb("consts", [P, CONST_COLS])
        panels = sb("panels", [P, PSLOTS, PANEL])
        shared = sb("shared", [P, SLOTS, 2 * D])
        flat = shared[:, :, :].rearrange("p a b -> p (a b)")
        z = flat[:, 0:6144].rearrange("p (b n) -> p b n", b=NB)
        gates = flat[:, 6144:12288].rearrange("p (b n) -> p b n", b=NB)
        kmT = flat[:, 12288:14336].rearrange("p (c t) -> p c t", c=KC)
        vm = flat[:, 14336:16384].rearrange("p (b n) -> p b n", b=NB)
        peer_qT = flat[:, 0:4096].rearrange("p (h t) -> p h t", h=2 * HEADS)
        work = sb("work", [P, 9216])
        memT = work[:, 0:2048].rearrange("p (c t) -> p c t", c=KC)
        probsT = work[:, 2048:4096]
        aT = probsT.rearrange("p (b h k q) -> p b h k q", b=NB, h=4, k=NB)
        eT = probsT.rearrange("p (h m t) -> p h m t", h=X_HEADS, m=NB)
        brT = work[:, 4096:7168].rearrange("p (n c t) -> p n c t", n=3, c=4)
        qkT = brT[:, 0:2, :, :]
        poolT = brT[:, 2, :, :]
        xqT = work[:, 4096:6144].rearrange("p (c t) -> p c t", c=KC)
        probs = work[:, 7168:9216].rearrange("p (u i k) -> p u i k", u=2, i=4)
        rot = work[:, 7168:8192].rearrange("p (k b n) -> p k b n", k=4, b=NB)
        gated = work[:, 7168:8192].rearrange("p (k n) -> p k n", k=2)
        scores = work[:, 0:4352].rearrange("p (h n) -> p h n", h=TOPS)
        head_sc = work[:, 4352:4608].rearrange("p (a n) -> p a n", a=2)
        head_less = work[:, 4608:4864].rearrange("p (a n) -> p a n", a=2)
        cand = work[:, 4864:5120]
        cand_less = work[:, 5120:5376]
        pick = work[:, 5376:5888].rearrange("p (a k i) -> p a k i", a=2, k=TOPK)
        products = work[:, 5888:6912]
        x_now = work[:, 6912:7936]
        diag = work[:, 7936:8960].rearrange("p (s n) -> p s n", s=SLOTS)

        zeros = sb("zeros", [P, 512], BF16)
        half = sb("half", [P, 8])
        pos_i = sb("pos_i", [P, NB], I32)
        pos_f = sb("pos_f", [P, NB])
        ang = sb("ang", [P, 4, NB, HALF])
        trig = sb("trig", [P, 2, NB, HALF])
        sq = sb("sq", [P, 2])
        var = sb("var", [P, 5, 8])
        rstd = sb("rstd", [P, 5, 8])
        lam = sb("lam", [P, 4])
        bn = sb("bn", [P, NB, 6])
        mv = sb("mv", [P, NB, 2])
        neg_max = sb("neg_max", [P, 2, 4])
        row_sum = sb("row_sum", [P, 2, 4])
        row_inv = sb("row_inv", [P, 2, 4])
        top = sb("top", [P, 2, TOPK])
        top_ix = sb("top_ix", [P, 2, TOPK], U32)
        top_ixf = sb("top_ixf", [P, 2, TOPK])
        best = sb("best", [P, 2, TOPK])
        best_neg = sb("best_neg", [P, 2])
        pos = sb("pos", [P, TOPK], U32)
        pos_ab = sb("pos_ab", [P, 2, TOPK], U32)
        chosen = sb("chosen", [P, 2, TOPK])
        expert = sb("expert", [P, 2, TOPK], I32)
        base = sb("base", [P, 1])
        gate_e = sb("gate_e", [P, 2, TOPK])
        gate_s = sb("gate_s", [P, 2])
        gate_r = sb("gate_r", [P, 2])
        gate = sb("gate", [P, 2, TOPK])
        dots = sb("dots", [P, 2, TOPK])
        gelu = sb("gelu", [P, 2, TOPK])
        weight = sb("weight", [P, 2, TOPK])

        def par(name):
            a, b = PARAMS[name]
            return params[:, a:b]

        def const(name):
            a, b = CONSTS[name]
            return consts[:, a:b]

        ident = const("ident")
        pool_m = const("pool").rearrange("p (g n) -> p g n", g=4)
        w_spatialT = par("w_spatial").rearrange("p (g t) -> p g t", g=4)
        w_pool = par("w_pool").rearrange("p (g e) -> p g e", g=4)

        mm = [ctx.enter_context(nc.psum_tensor(f"mm{i}", [P, 512], F32)) for i in range(4)]
        pair = ctx.enter_context(nc.psum_tensor("pair", [P, 1024], F32))
        tp = [ctx.enter_context(nc.psum_tensor(f"tp{i}", [P, 512], F32)) for i in range(2)]

        loaded = sem("loaded")
        params_in_s = sem("params_landed")
        params_free = sem("params_free")
        panel_in = [sem(f"panel_in{i}") for i in range(PSLOTS)]
        proj_done = sem("proj_done")
        proj_out = [sem(f"proj_out{i}") for i in range(4)]
        tp_done = sem("tp_done")
        tp_out = [sem(f"tp_out{i}") for i in range(2)]
        att_done = sem("att_done")
        att_out = sem("att_out")
        x_ready = sem("x_ready")
        xn_ready = sem("xn_ready")
        sq_ready = sem("sq_ready")
        var_ready = sem("var_ready")
        rstd_ready = sem("rstd_ready")
        trig_in = sem("trig_in")
        trig_done = sem("trig_done")
        memT_ready = sem("memT_ready")
        lam_in = sem("lam_in")
        lam_exp = sem("lam_exp")
        rope_ready = sem("rope_ready")
        max_ready = sem("max_ready")
        exp_done = sem("exp_done")
        probs_ready = sem("probs_ready")
        vn_ready = sem("vn_ready")
        on_ready = sem("on_ready")
        zeros_ready = sem("zeros_ready")
        got = [sem(f"got{i}") for i in range(SLOTS)]
        tile_used = sem("tile_used")
        expert_ready = sem("expert_ready")
        best_ready = sem("best_ready")
        gate_exp = sem("gate_exp")
        gate_ready = sem("gate_ready")
        dots_ready = sem("dots_ready")
        diag_ready = sem("diag_ready")
        acc_free = sem("acc_free")
        stored = sem("stored")

        def wait_proj_done(e, l, unit):
            e.wait_ge(proj_done, l * PU + (PU + PROJ.index(unit) + 1))

        def wait_proj_out(e, l, unit):
            i = PROJ.index(unit)
            e.wait_ge(proj_out[i % 4], l * (PU // 4) + i // 4 + 2)

        def wait_tp_done(e, l, unit):
            e.wait_ge(tp_done, l * TU + TRANS.index(unit) + 1 + MEM_TU)

        def wait_tp_out(e, l, unit):
            i = TRANS.index(unit)
            e.wait_ge(tp_out[i % 2], l * (TU // 2) + i // 2 + 2 + MEM_TU // 2)

        def bank(unit):
            return mm[PROJ.index(unit) % 4]

        def tbank(unit):
            return tp[TRANS.index(unit) % 2]

        def freed(unit):
            return proj_out[PROJ.index(unit) % 4]

        def tfreed(unit):
            return tp_out[TRANS.index(unit) % 2]

        block = ctx.enter_context(nc.Block())

        @block.sync
        def _(e):
            e.dma_start(x[:, :, :], x_in.rearrange("a (b p) d -> p (a b) d", p=P)).then_inc(loaded, 16)
            e.dma_start(xn[:, :, :], mem_in.rearrange("a (b p) d -> p (a b) d", p=P)).then_inc(loaded, 16)
            e.dma_start(consts[:, :], consts_in).then_inc(loaded, 16)
            e.dma_start(pos_i[:, :], pos_in.rearrange("a (b p) -> p (a b)", p=P),
                        allow_slow_non_contiguous=True).then_inc(loaded, 16)
            with e.Fori(0, L) as l:
                e.wait_ge(params_free, l + 1)
                e.dma_start(params[:, :], params_in[ds(l, 1)].rearrange("a p n -> p (a n)")).then_inc(params_in_s, 16)
                for k in range(PANELS):
                    if k >= PSLOTS:
                        wait_proj_done(e, l, LAST_OF_PANEL[k - PSLOTS])
                    else:
                        wait_proj_done(e, l - 1, LAST_OF_PANEL[k - PSLOTS])
                    e.dma_start(panels[:, k % PSLOTS, :], stream[ds(l * PANELS + k, 1)]
                                .rearrange("a p n -> p (a n)")).then_inc(panel_in[k % PSLOTS], 16)
            e.wait_ge(params_free, L + 1)
            e.dma_start(params[:, 0:D], g_final).then_inc(params_in_s, 16)
            e.wait_ge(xn_ready, 1 + 3 * L + 1)
            e.dma_start(out.rearrange("a (b p) d -> p (a b) d", p=P), xn[:, :, :]).then_inc(stored, 16)
            e.wait_ge(stored, 16)

        @block.tensor
        def _(e):
            def panel(l, k):
                e.wait_ge(panel_in[k % PSLOTS], (l * (PANELS // PSLOTS) + k // PSLOTS + 1) * 16)
                return panels[:, k % PSLOTS, :]

            def open_unit(l, unit):
                i = PROJ.index(unit)
                e.wait_ge(proj_out[i % 4], l * (PU // 4) + i // 4 + 1)
                return mm[i % 4]

            def open_tp(l, unit):
                i = TRANS.index(unit)
                e.wait_ge(tp_out[i % 2], l * (TU // 2) + i // 2 + 1 + MEM_TU // 2)
                return tp[i % 2]

            def turn_rows(l, kind, src):
                for u in range(4):
                    ps = open_tp(l, f"{kind}{u}")
                    for c in range(2):
                        for b in range(NB):
                            o = c * T + b * P
                            ins = e.transpose(ps[:, o:o + P], src[:, b, (2 * u + c) * P:(2 * u + c + 1) * P], ident)
                    ins.then_inc(tp_done, 1)

            def rows_times(l, unit, b, lhs, w):
                ps = open_unit(l, unit)
                n = w.shape[1]
                for c in range(n):
                    ins = e.matmul(ps[:, :], lhs[:, c, b * P:(b + 1) * P], w[:, c, :], start=c == 0, stop=c == n - 1)
                ins.then_inc(proj_done, 1)

            def columns_times(l, unit, w, cols, rhs):
                ps = open_unit(l, unit)
                for k in range(2):
                    for c in range(KC):
                        ins = e.matmul(ps[:, k * T:(k + 1) * T], w[:, c, cols + k * P:cols + (k + 1) * P],
                                       rhs[:, c, :], start=c == 0, stop=c == KC - 1)
                ins.then_inc(proj_done, 1)

            def full_panel(l, k, units, lhs):
                w = panel(l, k).rearrange("p (c n) -> p c n", c=KC)
                for b, unit in enumerate(units):
                    rows_times(l, unit, b, lhs, w)

            def column_panel(l, k, units, rhs):
                w = panel(l, k).rearrange("p (c n) -> p c n", c=KC)
                for h, unit in enumerate(units):
                    columns_times(l, unit, w, h * T, rhs)

            def gate_panel(l, k):
                full_panel(l, GATE_PANEL + k, (f"g{k}0", f"g{k}1"), actT)

            def scores_unit(l, u):
                b, h0 = u // 2, 2 * (u % 2)
                e.wait_ge(att_out, l * 6 + u + 1)
                for m in range(2):
                    for k in range(2):
                        o = (2 * m + k) * 256
                        ins = e.matmul(pair[:, o:o + P * (b + 1)],
                                       qkT[64 * m:64 * m + 64, 0, h0 + k, b * P:(b + 1) * P],
                                       qkT[64 * m:64 * m + 64, 1, h0 + k, 0:P * (b + 1)], start=True, stop=True)
                ins.then_inc(att_done, 1)

            def turn_probs(l, u):
                b = u // 2
                ps = open_tp(l, f"a{u}")
                e.wait_ge(probs_ready, l * 6 + u + 1)
                for k in range(2):
                    for kb in range(b + 1):
                        o = (k * (b + 1) + kb) * P
                        ins = e.transpose(ps[:, o:o + P], probs[:, u % 2, k, kb * P:(kb + 1) * P], ident)
                ins.then_inc(tp_done, 1)

            def probs_times_v(l, b):
                ps = open_unit(l, f"av{b}")
                for h in range(DA_HEADS):
                    for kb in range(b + 1):
                        ins = e.matmul(ps[:, h * P:(h + 1) * P], aT[:, b, h, kb, :],
                                       z[:, kb, 1024 + h * P:1024 + (h + 1) * P], start=kb == 0, stop=kb == b)
                ins.then_inc(proj_done, 1)

            e.wait_ge(zeros_ready, 1)
            e.sem_inc(proj_done, PU)
            e.sem_inc(tile_used, SLOTS)
            e.wait_ge(xn_ready, 1)
            for u in range(MEM_TU):
                e.wait_ge(tp_out[u % 2], u // 2 + 1)
                for c in range(2):
                    for b in range(NB):
                        o = c * T + b * P
                        ins = e.transpose(tp[u % 2][:, o:o + P], xn[:, b, (2 * u + c) * P:(2 * u + c + 1) * P], ident)
                ins.then_inc(tp_done, 1)

            with e.Fori(0, L) as l:
                e.wait_ge(xn_ready, l * 3 + 2)
                turn_rows(l, "nA", xn)
                wait_tp_out(e, l, "nA2")
                wait_tp_out(e, l, "nA3")
                for k in range(6):
                    full_panel(l, Z_PANEL + k, (f"z{k}0", f"z{k}1"), actT)
                e.wait_ge(rope_ready, l + 1)
                for u in range(4):
                    ps = open_tp(l, f"qk{u}")
                    for k in range(2):
                        for b in range(NB):
                            n = (u // 2) * BW + (2 * (u % 2) + k) * P
                            o = k * T + b * P
                            ins = e.transpose(ps[:, o:o + P], z[:, b, n:n + P], ident)
                    ins.then_inc(tp_done, 1)
                wait_proj_out(e, l, "z31")
                wait_tp_out(e, l, "qk2")
                wait_tp_out(e, l, "qk3")
                scores_unit(l, 0)
                for u in range(2):
                    ps = open_unit(l, f"pd{u}")
                    for k in range(2):
                        g = 2 * u + k
                        c = 1536 + g * P
                        e.matmul(ps[:, k * T:(k + 1) * T], z[:, 0, c:c + P], pool_m[:, g, 0:T], start=True, stop=False)
                        ins = e.matmul(ps[:, k * T + P:(k + 1) * T], z[:, 1, c:c + P], pool_m[:, g, T:T + P],
                                       start=False, stop=True)
                    ins.then_inc(proj_done, 1)
                gate_panel(l, 0)
                scores_unit(l, 1)
                turn_probs(l, 0)
                gate_panel(l, 1)
                scores_unit(l, 2)
                turn_probs(l, 1)
                wait_tp_out(e, l, "a0")
                wait_tp_out(e, l, "a1")
                probs_times_v(l, 0)
                gate_panel(l, 2)
                scores_unit(l, 3)
                turn_probs(l, 2)
                e.wait_ge(vn_ready, l + 1)
                for b in range(NB):
                    ps = open_unit(l, f"sm{b}")
                    for g in range(4):
                        ins = e.matmul(ps[:, g * P:(g + 1) * P], w_spatialT[:, g, :],
                                       z[:, b, 2560 + g * P:2560 + (g + 1) * P], start=True, stop=True)
                    ins.then_inc(proj_done, 1)
                gate_panel(l, 3)
                turn_probs(l, 3)
                wait_tp_out(e, l, "a2")
                wait_tp_out(e, l, "a3")
                probs_times_v(l, 1)
                wait_proj_out(e, l, "pd0")
                wait_proj_out(e, l, "pd1")
                for u in range(2):
                    ps = open_unit(l, f"py{u}")
                    for k in range(2):
                        ins = e.matmul(ps[:, k * T:(k + 1) * T], w_pool[:, 2 * u + k, :], poolT[:, 2 * u + k, :],
                                       start=True, stop=True)
                    ins.then_inc(proj_done, 1)
                gate_panel(l, 4)
                gate_panel(l, 5)
                e.wait_ge(memT_ready, l + 1)
                for k in range(2):
                    column_panel(l, KV_PANEL + k, (f"km{2 * k}", f"km{2 * k + 1}"), memT)
                for k in range(2):
                    full_panel(l, KV_PANEL + 2 + k, (f"vm{2 * k}", f"vm{2 * k + 1}"), memT)
                e.wait_ge(on_ready, l + 1)
                wait_proj_out(e, l, "sm0")
                wait_proj_out(e, l, "sm1")
                for kind, c0 in (("o", 0), ("s", BW)):
                    for u in range(2):
                        ps = open_tp(l, f"{kind}{u}")
                        for k in range(2):
                            for b in range(NB):
                                n = c0 + (2 * u + k) * P
                                o = k * T + b * P
                                ins = e.transpose(ps[:, o:o + P], xn[:, b, n:n + P], ident)
                        ins.then_inc(tp_done, 1)
                for unit in ("o0", "o1", "s0", "s1"):
                    wait_tp_out(e, l, unit)
                wait_proj_out(e, l, "py0")
                wait_proj_out(e, l, "py1")
                for n in range(3):
                    w = panel(l, BRANCH_PANEL + n).rearrange("p (c n) -> p c n", c=4)
                    for b in range(NB):
                        for h in range(2):
                            rows_times(l, f"br{n}{b}{h}", b, brT[:, n, :, :], w[:, :, h * BW:(h + 1) * BW])
                for unit in ("br200", "br201", "br210", "br211"):
                    wait_proj_out(e, l, unit)
                turn_rows(l, "m", xn)
                wait_tp_out(e, l, "m2")
                wait_tp_out(e, l, "m3")
                for k in range(2):
                    full_panel(l, OUT_PANEL + k, (f"wo{2 * k}", f"wo{2 * k + 1}"), actT)
                e.wait_ge(xn_ready, l * 3 + 3)
                turn_rows(l, "nC", xn)
                wait_tp_out(e, l, "nC2")
                wait_tp_out(e, l, "nC3")
                for k in range(2):
                    column_panel(l, XQ_PANEL + k, (f"xq{2 * k}", f"xq{2 * k + 1}"), actT)
                for i in range(4):
                    wait_proj_out(e, l, f"xq{i}")
                    wait_proj_out(e, l, f"km{i}")
                for b in range(NB):
                    e.wait_ge(att_out, l * 6 + 4 + b + 1)
                    for h in range(X_HEADS):
                        for k in range(2):
                            ins = e.matmul(pair[:, h * T:(h + 1) * T], xqT[:, 2 * h + k, b * P:(b + 1) * P],
                                           kmT[:, 2 * h + k, :], start=k == 0, stop=k == 1)
                    ins.then_inc(att_done, 1)
                for u in range(4):
                    b, h0 = u // 2, 2 * (u % 2)
                    ps = open_tp(l, f"e{u}")
                    e.wait_ge(probs_ready, l * 6 + 4 + b + 1)
                    for k in range(2):
                        for m in range(NB):
                            o = (k * NB + m) * P
                            ins = e.transpose(ps[:, o:o + P], probs[:, b, h0 + k, m * P:(m + 1) * P], ident)
                    ins.then_inc(tp_done, 1)
                wait_tp_out(e, l, "e2")
                wait_tp_out(e, l, "e3")
                for i in range(4):
                    wait_proj_out(e, l, f"vm{i}")
                for u in range(4):
                    ps = open_unit(l, f"co{u}")
                    for k in range(2):
                        c = 2 * u + k
                        for m in range(NB):
                            ins = e.matmul(ps[:, k * T:(k + 1) * T], vm[:, m, c * P:(c + 1) * P], eT[:, c // 2, m, :],
                                           start=m == 0, stop=m == NB - 1)
                    ins.then_inc(proj_done, 1)
                for i in range(4):
                    wait_proj_out(e, l, f"co{i}")
                for k in range(2):
                    full_panel(l, XO_PANEL + k, (f"xo{2 * k}", f"xo{2 * k + 1}"), actT)
                e.wait_ge(xn_ready, l * 3 + 4)
                turn_rows(l, "nF", xn)
                wait_tp_out(e, l, "nF2")
                wait_tp_out(e, l, "nF3")
                for k in range(4):
                    column_panel(l, PQ_PANEL + k, (f"pq{2 * k}", f"pq{2 * k + 1}"), actT)
                for i in range(4, 8):
                    wait_proj_out(e, l, f"pq{i}")
                keys = panel(l, KEY_PANEL)
                for b in range(NB):
                    for q in range(4):
                        ps = open_unit(l, f"sc{4 * b + q}")
                        for k in range(4):
                            hp = 4 * q + k
                            ins = e.matmul(ps[:, k * NK:(k + 1) * NK], peer_qT[:, hp, b * P:(b + 1) * P],
                                           keys[:, hp * NK:(hp + 1) * NK], start=True, stop=True)
                        ins.then_inc(proj_done, 1)
                with e.Fori(0, NB) as b:
                    e.wait_ge(acc_free, l * NB + b + 1)
                    for h in range(2):
                        e.matmul(pair[:, h * BW:(h + 1) * BW], zeros[:, 0:P], zeros[:, :], start=True, stop=False,
                                 skip_group_check=True)
                    with e.Fori(0, HEADS // 2) as hh:
                        for s in range(2):
                            for j in range(TOPK):
                                e.wait_ge(diag_ready, l * TILES + b * (TILES // NB) + hh * (2 * TOPK)
                                          + s * TOPK + j + 1)
                                for h in range(2):
                                    ins = e.matmul(pair[:, h * BW:(h + 1) * BW], diag[:, j % SLOTS, :],
                                                   shared[:, j % SLOTS, D + h * BW:D + (h + 1) * BW],
                                                   start=False, stop=False, skip_group_check=True)
                                ins.then_inc(tile_used, 1)

        @block.vector
        def _(e):
            def norm(l, r, wait_square=True):
                e.tensor_tensor_reduce(xn[:, 0, :], x[:, 0, :], x[:, 0, :], 1.0, 0.0, ALU.mult, ALU.add, sq[:, 0:1])
                e.drain()
                e.wait_ge(sq_ready, l * 3 + r + 1)
                e.tensor_scalar(var[:, r, 0:2], sq[:, :], 1.0 / D, EPS, ALU.mult, ALU.add).then_inc(var_ready, 1)
                e.wait_ge(rstd_ready, l * 5 + (0, 3, 4)[r] + 2)
                for b in range(NB):
                    ins = e.tensor_scalar(xn[:, b, :], x[:, b, :], rstd[:, r, b:b + 1], None, ALU.mult)
                return ins

            def turn_out(l, unit, dst, gain=None):
                wait_tp_done(e, l, unit)
                ps = tbank(unit)
                c = 2 * (TRANS.index(unit) % 4)
                if gain is None:
                    e.tensor_copy(dst, ps[:, :]).then_inc(tfreed(unit), 1)
                    return
                for k in range(2):
                    g = gain if isinstance(gain, float) else gain[:, c + k:c + k + 1]
                    ins = e.tensor_scalar(dst[:, c + k, :], ps[:, k * T:(k + 1) * T], g, None, ALU.mult)
                ins.then_inc(tfreed(unit), 1)

            def masked_max(l, u):
                b, n = u // 2, P * (u // 2 + 1)
                e.wait_ge(att_done, l * 6 + u + 1)
                mask = const("mask")[:, T - n:T].unsqueeze(1).broadcast_to([P, 4, n])
                src = pair[:, :].rearrange("p (i k) -> p i k", i=4)[:, :, 0:n]
                e.scalar_tensor_tensor(probs[:, u % 2, :, 0:n], src, DA_SCALE, mask, ALU.mult, ALU.add) \
                    .then_inc(att_out, 1)
                e.drain()
                e.tensor_reduce(neg_max[:, u % 2, :], probs[:, u % 2, :, 0:n], AX, ALU.max, negate=True) \
                    .then_inc(max_ready, 1)

            def difference(l, u):
                n = P * (u // 2 + 1)
                v = u % 2
                e.wait_ge(exp_done, l * 6 + u + 1)
                e.reciprocal(row_inv[:, v, :], row_sum[:, v, :])
                e.drain()
                e.tensor_scalar(row_inv[:, v, 2:4], row_inv[:, v, 2:4], lam[:, 0:1], None, ALU.mult)
                e.drain()
                for k in range(2):
                    e.tensor_scalar(probs[:, v, 2 + k, 0:n], probs[:, v, 2 + k, 0:n], row_inv[:, v, 2 + k:3 + k],
                                    None, ALU.mult)
                e.drain()
                for k in range(2):
                    ins = e.scalar_tensor_tensor(probs[:, v, k, 0:n], probs[:, v, k, 0:n], row_inv[:, v, k:k + 1],
                                                 probs[:, v, 2 + k, 0:n], ALU.mult, ALU.add)
                ins.then_inc(probs_ready, 1)

            def cross_max(l, b):
                e.wait_ge(att_done, l * 6 + 4 + b + 1)
                e.tensor_reduce(neg_max[:, b, :], pair[:, :].rearrange("p (i k) -> p i k", i=4), AX, ALU.max,
                                negate=True)
                e.drain()
                e.tensor_scalar(neg_max[:, b, :], neg_max[:, b, :], X_SCALE, None, ALU.mult).then_inc(max_ready, 1)

            def cross_probs(l, b):
                e.wait_ge(exp_done, l * 6 + 4 + b + 1)
                e.reciprocal(row_inv[:, b, :], row_sum[:, b, :])
                e.drain()
                e.tensor_tensor(probs[:, b, :, :], probs[:, b, :, :],
                                row_inv[:, b, :].unsqueeze(2).broadcast_to([P, 4, T]), ALU.mult) \
                    .then_inc(probs_ready, 1)

            def add_rows(l, unit, b, cols):
                wait_proj_done(e, l, unit)
                dst = x[:, b, cols * BW:(cols + 1) * BW]
                return e.tensor_tensor(dst, bank(unit)[:, :], dst, ALU.add)

            def top_halves(i):
                e.tensor_copy(head_sc[:, :, :], scores[:, ds(i, 1), :].rearrange("p a (h n) -> p (a h) n", h=2))
                e.drain()
                for a in range(2):
                    e.max(top[:, a, 0:8], head_sc[:, a, :])
                e.drain()

            def top_halves_rest():
                for a in range(2):
                    e.max_index(top_ix[:, a, 0:8], top[:, a, 0:8], head_sc[:, a, :])
                    e.match_replace(head_less[:, a, :], top[:, a, 0:8], head_sc[:, a, :], LOWEST)
                e.drain()

            def top_halves_second():
                for a in range(2):
                    e.max(top[:, a, 8:16], head_less[:, a, :])
                e.drain()
                for a in range(2):
                    e.max_index(top_ix[:, a, 8:16], top[:, a, 8:16], head_less[:, a, :])
                e.tensor_tensor(cand.rearrange("p (i j) -> p i j", i=TOPK),
                                top[:, 0, :].unsqueeze(2).broadcast_to([P, TOPK, TOPK]),
                                top[:, 1, :].unsqueeze(1).broadcast_to([P, TOPK, TOPK]), ALU.add)
                e.drain()

            def top_pairs(par_):
                e.tensor_copy(top_ixf[:, :, :], top_ix[:, :, :])
                e.max(best[:, par_, 0:8], cand)
                e.drain()
                e.max_index(pos[:, 0:8], best[:, par_, 0:8], cand)
                e.match_replace(cand_less, best[:, par_, 0:8], cand, LOWEST)
                e.tensor_scalar(best_neg[:, par_:par_ + 1], best[:, par_, 0:1], -1.0, None, ALU.mult)
                e.drain()

            def top_pairs_second(par_):
                e.max(best[:, par_, 8:16], cand_less).then_inc(best_ready, 1)
                e.drain()
                e.max_index(pos[:, 8:16], best[:, par_, 8:16], cand_less)
                e.drain()
                e.tensor_single_scalar(pos_ab[:, 0, :], pos[:, :], 4, ALU.logical_shift_right)
                e.tensor_single_scalar(pos_ab[:, 1, :], pos[:, :], TOPK - 1, ALU.bitwise_and)
                e.drain()

            def top_lookup():
                iota = const("iota").unsqueeze(1).unsqueeze(1).broadcast_to([P, 2, TOPK, TOPK])
                e.tensor_tensor(pick[:, :, :, :], pos_ab[:, :, :].unsqueeze(3).broadcast_to([P, 2, TOPK, TOPK]), iota,
                                ALU.is_equal)
                e.drain()
                e.tensor_tensor(pick[:, :, :, :], pick[:, :, :, :],
                                top_ixf[:, :, :].unsqueeze(2).broadcast_to([P, 2, TOPK, TOPK]), ALU.mult)
                e.drain()

            def top_experts(par_):
                e.tensor_reduce(chosen[:, :, :], pick[:, :, :, :], AX, ALU.add)
                e.drain()
                e.scalar_tensor_tensor(chosen[:, 0, :], chosen[:, 0, :], float(NK), chosen[:, 1, :], ALU.mult, ALU.add)
                e.drain()
                e.tensor_scalar(expert[:, par_, :], chosen[:, 0, :], base[:, :], None, ALU.add) \
                    .then_inc(expert_ready, 1)

            def head_gates(l, i, par_):
                e.wait_ge(gate_exp, l * TOPS + i + 1)
                e.reciprocal(gate_r[:, par_:par_ + 1], gate_s[:, par_:par_ + 1])
                e.drain()
                e.tensor_scalar(gate[:, par_, :], gate_e[:, par_, :], gate_r[:, par_:par_ + 1], None, ALU.mult) \
                    .then_inc(gate_ready, 1)

            e.memset(zeros[:, :], 0.0).then_inc(zeros_ready, 1)
            e.memset(half[:, :], -0.5)
            e.wait_ge(loaded, 64)
            for s in (*proj_out, *tp_out, att_out, acc_free, params_free, x_ready):
                e.sem_inc(s, 1)
            e.tensor_copy(pos_f[:, :], pos_i[:, :])
            e.drain()
            e.tensor_tensor(ang[:, 0, :, :], pos_f[:, :].unsqueeze(2).broadcast_to([P, NB, HALF]),
                            const("inv").unsqueeze(1).broadcast_to([P, NB, HALF]), ALU.mult)
            e.drain()
            two_pi = 2 * np.pi
            parts, rest = [], two_pi
            for bits in (5, 14, 23):
                v = np.floor(rest * 2.0 ** bits) / 2.0 ** bits
                parts.append(float(v))
                rest -= v
            parts.append(float(rest))
            nearest = 1.5 * 2.0 ** 23
            e.tensor_scalar(ang[:, 1, :, :], ang[:, 0, :, :], 1.0 / two_pi, nearest, ALU.mult, ALU.add)
            e.drain()
            e.tensor_scalar(ang[:, 1, :, :], ang[:, 1, :, :], nearest, None, ALU.subtract)
            e.drain()
            for v in parts:
                e.scalar_tensor_tensor(ang[:, 0, :, :], ang[:, 1, :, :], -v, ang[:, 0, :, :], ALU.mult, ALU.add)
                e.drain()
            e.tensor_scalar(ang[:, 3, :, :], ang[:, 0, :, :], 3.1415925, -3.1415925, ALU.min, ALU.max)
            e.drain()
            e.scalar_tensor_tensor(ang[:, 2, :, :], ang[:, 3, :, :], -1.0, ang[:, 3, :, :], ALU.mult, ALU.min)
            e.drain()
            e.tensor_scalar(ang[:, 2, :, :], ang[:, 2, :, :], float(np.pi / 2), None, ALU.add).then_inc(trig_in, 1)
            for b in range(NB):
                e.tensor_tensor_reduce(memT0[:, 4 * b:4 * b + 4, :].rearrange("p c t -> p (c t)"), xn[:, b, :],
                                       xn[:, b, :], 1.0, 0.0, ALU.mult, ALU.add, sq[:, b:b + 1])
            e.drain()
            e.tensor_scalar(var[:, 0, 0:2], sq[:, :], 1.0 / D, EPS, ALU.mult, ALU.add).then_inc(var_ready, 1)
            e.wait_ge(rstd_ready, 1)
            for b in range(NB):
                ins = e.tensor_scalar(xn[:, b, :], xn[:, b, :], rstd[:, 0, b:b + 1], None, ALU.mult)
            ins.then_inc(xn_ready, 1)
            for u in (0, 2):
                e.wait_ge(tp_done, u + 1)
                e.tensor_copy(memT0[:, 2 * u:2 * u + 2, :].rearrange("p c t -> p (c t)"), tp[0][:, :]) \
                    .then_inc(tp_out[0], 1)
            e.wait_ge(tp_done, MEM_TU)

            with e.Fori(0, L) as l:
                norm(l, 0).then_inc(xn_ready, 1)
                e.wait_ge(params_in_s, l * 16 + 16)
                turn_out(l, "nA0", actT, par("g_mix"))
                turn_out(l, "nA2", actT, par("g_mix"))
                lq = par("lam_qk")
                for k in range(2):
                    e.tensor_tensor_reduce(rot[:, k, 0, 0:64], lq[:, 128 * k:128 * k + 64],
                                           lq[:, 128 * k + 64:128 * k + 128], 1.0, 0.0, ALU.mult, ALU.add,
                                           lam[:, k:k + 1])
                e.drain()
                e.sem_inc(lam_in, 1)
                e.wait_ge(trig_done, 1)
                wait_proj_out(e, l, "z10")
                wait_proj_out(e, l, "z11")
                heads = [z[:, b, 0:1024].rearrange("p (h d) -> p h d", d=DA_DIM) for b in range(NB)]
                r = [rot[:, k, :, :].rearrange("p b (h d) -> p b h d", d=HALF) for k in range(4)]
                for b in range(NB):
                    for k, (a, t) in enumerate(((0, 0), (HALF, 1), (0, 1), (HALF, 0))):
                        e.tensor_tensor(r[k][:, b], heads[b][:, :, a:a + HALF],
                                        trig[:, t, b, :].unsqueeze(1).broadcast_to([P, 16, HALF]), ALU.mult)
                e.drain()
                for b in range(NB):
                    e.tensor_tensor(heads[b][:, :, 0:HALF], r[0][:, b], r[1][:, b], ALU.subtract)
                    ins = e.tensor_tensor(heads[b][:, :, HALF:ROT], r[2][:, b], r[3][:, b], ALU.add)
                ins.then_inc(rope_ready, 1)
                wait_proj_out(e, l, "z50")
                wait_proj_out(e, l, "z51")
                for b in range(NB):
                    e.bn_stats(bn[:, b, :], z[:, b, 2560:3072])
                e.drain()
                for b in range(NB):
                    e.bn_aggr(mv[:, b, :], bn[:, b, :])
                e.drain()
                e.tensor_scalar(var[:, 3, 0:2], mv[:, :, 1], EPS, None, ALU.add).then_inc(var_ready, 1)
                turn_out(l, "qk0", qkT[:, 0, 0:2, :].rearrange("p c t -> p (c t)"))
                turn_out(l, "qk2", qkT[:, 1, 0:2, :].rearrange("p c t -> p (c t)"))
                e.wait_ge(lam_exp, l + 1)
                e.tensor_tensor(lam[:, 0:1], lam[:, 3:4], lam[:, 2:3], ALU.subtract)
                e.drain()
                e.tensor_tensor(lam[:, 0:1], lam[:, 0:1], par("lam_init"), ALU.subtract)
                masked_max(l, 0)
                e.wait_ge(rstd_ready, l * 5 + 3)
                for b in range(NB):
                    e.tensor_scalar(z[:, b, 2560:3072], z[:, b, 2560:3072], mv[:, b, 0:1], rstd[:, 3, b:b + 1],
                                    ALU.subtract, ALU.mult)
                e.drain()
                for b in range(NB):
                    e.tensor_tensor(z[:, b, 2560:3072], z[:, b, 2560:3072], par("sg_ln_g"), ALU.mult)
                e.drain()
                for b in range(NB):
                    e.tensor_tensor(z[:, b, 2560:3072], z[:, b, 2560:3072], par("sg_ln_b"), ALU.add)
                e.tensor_tensor(w_spatialT, w_spatialT, const("triu").unsqueeze(1).broadcast_to([P, 4, P]),
                                ALU.mult).then_inc(vn_ready, 1)
                difference(l, 0)
                masked_max(l, 1)
                wait_tp_done(e, l, "a0")
                e.tensor_copy(aT[:, 0, 0:2, 0, :], tbank("a0")[:, 0:256].rearrange("p (h q) -> p h q", h=2)) \
                    .then_inc(tfreed("a0"), 1)
                difference(l, 1)
                masked_max(l, 2)
                difference(l, 2)
                masked_max(l, 3)
                difference(l, 3)
                wait_tp_done(e, l, "a2")
                e.tensor_copy(aT[:, 1, 0:2, :, :].rearrange("p h k q -> p (h k q)"), tbank("a2")[:, :]) \
                    .then_inc(tfreed("a2"), 1)
                for b in range(NB):
                    wait_proj_done(e, l, f"sm{b}")
                    for g in range(4):
                        ins = e.scalar_tensor_tensor(xn[:, b, BW + g * P:BW + (g + 1) * P],
                                                     bank(f"sm{b}")[:, g * P:(g + 1) * P],
                                                     par("b_spatial")[:, g:g + 1],
                                                     z[:, b, 2048 + g * P:2048 + (g + 1) * P], ALU.add, ALU.mult)
                    ins.then_inc(freed(f"sm{b}"), 1)
                for b in range(NB):
                    wait_proj_out(e, l, f"av{b}")
                    e.tensor_tensor(gated[:, b, :], xn[:, b, 0:BW], xn[:, b, 0:BW], ALU.mult)
                    e.drain()
                    e.tensor_reduce(var[:, 4, 4 * b:4 * b + 4], gated[:, b, :].rearrange("p (h d) -> p h d", h=4), AX,
                                    ALU.add)
                e.drain()
                e.tensor_scalar(var[:, 4, :], var[:, 4, :], 1.0 / P, EPS, ALU.mult, ALU.add).then_inc(var_ready, 1)
                e.wait_ge(rstd_ready, l * 5 + 4)
                e.tensor_scalar(rstd[:, 4, :], rstd[:, 4, :], par("one_less"), None, ALU.mult)
                e.drain()
                heads_o = [xn[:, b, 0:BW].rearrange("p (h d) -> p h d", h=4) for b in range(NB)]
                for b in range(NB):
                    e.tensor_tensor(heads_o[b], heads_o[b],
                                    rstd[:, 4, 4 * b:4 * b + 4].unsqueeze(2).broadcast_to([P, 4, P]), ALU.mult)
                e.drain()
                for b in range(NB):
                    ins = e.tensor_tensor(heads_o[b], heads_o[b],
                                          par("subln_g").unsqueeze(1).broadcast_to([P, 4, P]), ALU.mult)
                ins.then_inc(on_ready, 1)
                turn_out(l, "o0", brT[:, 0, 0:2, :].rearrange("p c t -> p (c t)"))
                turn_out(l, "s0", brT[:, 2, 0:2, :].rearrange("p c t -> p (c t)"))
                for n in range(3):
                    for b in range(NB):
                        for h in range(2):
                            unit = f"br{n}{b}{h}"
                            if n == 0 and b == 0 and h == 0:
                                wait_tp_done(e, l, "s1")
                            wait_proj_done(e, l, unit)
                            g = gates[:, b, n * D + h * BW:n * D + (h + 1) * BW]
                            dst = xn[:, b, h * BW:(h + 1) * BW]
                            if n == 0:
                                e.scalar_tensor_tensor(dst, g, 1.0, bank(unit)[:, :], ALU.add, ALU.mult) \
                                    .then_inc(freed(unit), 1)
                            else:
                                e.scalar_tensor_tensor(gated[:, h, :], g, 1.0, bank(unit)[:, :], ALU.add, ALU.mult)
                                e.drain()
                                e.tensor_tensor(dst, dst, gated[:, h, :], ALU.add).then_inc(freed(unit), 1)
                turn_out(l, "m0", actT, 0.5)
                turn_out(l, "m2", actT, 0.5)
                for k in range(2):
                    for b in range(NB):
                        ins = add_rows(l, f"wo{2 * k + b}", b, k)
                        ins.then_inc(freed(f"wo{2 * k + b}"), 1)
                e.drain()
                e.sem_inc(x_ready, 1)
                wait_tp_done(e, l, "m3")
                norm(l, 1).then_inc(xn_ready, 1)
                turn_out(l, "nC0", actT, par("g_cross"))
                turn_out(l, "nC2", actT, par("g_cross"))
                cross_max(l, 0)
                cross_max(l, 1)
                cross_probs(l, 0)
                cross_probs(l, 1)
                for u in (0, 2):
                    wait_tp_done(e, l, f"e{u}")
                    b = u // 2
                    e.tensor_copy(eT[:, 0:2, :, b * P:(b + 1) * P],
                                  tbank(f"e{u}")[:, :].rearrange("p (h m t) -> p h m t", h=2, m=NB)) \
                        .then_inc(tfreed(f"e{u}"), 1)
                for k in range(2):
                    for b in range(NB):
                        ins = add_rows(l, f"xo{2 * k + b}", b, k)
                        ins.then_inc(freed(f"xo{2 * k + b}"), 1)
                e.drain()
                e.sem_inc(x_ready, 1)
                norm(l, 2).then_inc(xn_ready, 1)
                turn_out(l, "nF0", actT, par("g_ffn"))
                turn_out(l, "nF2", actT, par("g_ffn"))
                wait_tp_done(e, l, "nF3")
                for b in range(NB):
                    e.tensor_tensor(xn[:, b, :], xn[:, b, :], par("g_ffn_row"), ALU.mult)
                e.drain()
                wait_proj_out(e, l, "pq0")
                e.sem_inc(params_free, 1)
                e.tensor_copy(base[:, :], const("expert_base")[:, ds(l, 1)])
                e.memset(scores[:, STEPS:TOPS, :], 0.0)
                for i in range(4):
                    wait_proj_out(e, l, f"sc{i}")
                top_halves(0)
                top_halves_rest()
                top_halves_second()
                top_pairs(0)
                top_pairs_second(0)
                top_lookup()
                top_experts(0)
                head_gates(l, 0, 0)
                for i in range(4, 8):
                    wait_proj_out(e, l, f"sc{i}")
                e.nop(nofuse=True)
                with e.Fori(0, NB) as b:
                    e.tensor_copy(x_now.unsqueeze(1), xn[:, ds(b, 1), :])
                    e.drain()
                    with e.Fori(0, HEADS // 2) as hh:
                        for s in range(2):
                            i = b * HEADS + hh * 2 + s
                            for j in range(TOPK):
                                e.drain()
                                e.wait_ge(got[j % SLOTS], ((l * STEPS + i) * (TOPK // SLOTS) + j // SLOTS + 1) * 16)
                                ins = e.tensor_tensor_reduce(products, x_now, shared[:, j % SLOTS, 0:D], 1.0, 0.0,
                                                             ALU.mult, ALU.add, dots[:, s, j:j + 1])
                                if j % 4 == 3:
                                    ins.then_inc(dots_ready, 1)
                                if j == 0:
                                    top_halves(i + 1)
                                if j == 1:
                                    top_halves_rest()
                                if j == 2:
                                    top_halves_second()
                                if j == 3:
                                    top_pairs(1 - s)
                                if j == 4:
                                    top_pairs_second(1 - s)
                                if j == 5:
                                    top_lookup()
                                if j == 6:
                                    top_experts(1 - s)
                                if j == 14:
                                    head_gates(l, i + 1, 1 - s)
                    e.wait_ge(tile_used, SLOTS + l * TILES + b * (TILES // NB) + TILES // NB)
                    e.tensor_tensor(x[:, ds(b, 1), :], x[:, ds(b, 1), :], pair[:, :].unsqueeze(1), ALU.add)
                    e.drain()
                    e.sem_inc(x_ready, 1)
                    e.sem_inc(acc_free, 1)

            norm(L, 0)
            e.drain()
            e.wait_ge(params_in_s, L * 16 + 16)
            for b in range(NB):
                ins = e.tensor_tensor(xn[:, b, :], xn[:, b, :], params[:, 0:D], ALU.mult)
            ins.then_inc(xn_ready, 1)

        @block.scalar
        def _(e):
            def square(l, r):
                e.wait_ge(x_ready, l * 4 + r + 1)
                e.activation(xn[:, 1, :], x[:, 1, :], ACT.Square, accum_out=sq[:, 1:2]).then_inc(sq_ready, 1)

            def out_unit(l, unit, dst, func=ACT.Copy, scale=1.0):
                wait_proj_done(e, l, unit)
                e.activation(dst, bank(unit)[:, :], func, scale=scale).then_inc(freed(unit), 1)

            def turn_out(l, unit, dst, gain=None):
                wait_tp_done(e, l, unit)
                ps = tbank(unit)
                c = 2 * (TRANS.index(unit) % 4)
                if gain is None:
                    e.activation(dst, ps[:, :], ACT.Copy).then_inc(tfreed(unit), 1)
                    return
                for k in range(2):
                    g = gain if isinstance(gain, float) else gain[:, c + k:c + k + 1]
                    ins = e.activation(dst[:, c + k, :], ps[:, k * T:(k + 1) * T], ACT.Copy, scale=g)
                ins.then_inc(tfreed(unit), 1)

            def gates_out(l, k):
                for b in range(NB):
                    out_unit(l, f"g{k}{b}", gates[:, b, k * BW:(k + 1) * BW], ACT.Tanh, 0.5)

            def exps(l, u):
                n = P * (u // 2 + 1)
                e.wait_ge(max_ready, l * 6 + u + 1)
                for i in range(4):
                    ins = e.activation(probs[:, u % 2, i, 0:n], probs[:, u % 2, i, 0:n], ACT.Exp,
                                       bias=neg_max[:, u % 2, i:i + 1], accum_out=row_sum[:, u % 2, i:i + 1])
                ins.then_inc(exp_done, 1)

            def gate_exps(l, i, par_):
                e.wait_ge(best_ready, l * TOPS + i + 1)
                e.activation(gate_e[:, par_, :], best[:, par_, :], ACT.Exp, bias=best_neg[:, par_:par_ + 1],
                             accum_out=gate_s[:, par_:par_ + 1]).then_inc(gate_exp, 1)

            e.wait_ge(trig_in, 1)
            e.activation(trig[:, 0, :, :], ang[:, 2, :, :], ACT.Sin)
            e.activation(trig[:, 1, :, :], ang[:, 3, :, :], ACT.Sin).then_inc(trig_done, 1)
            for u in (1, 3):
                e.wait_ge(tp_done, u + 1)
                e.activation(memT0[:, 2 * u:2 * u + 2, :].rearrange("p c t -> p (c t)"), tp[1][:, :], ACT.Copy) \
                    .then_inc(tp_out[1], 1)

            with e.Fori(0, L) as l:
                square(l, 0)
                e.wait_ge(params_in_s, l * 16 + 16)
                turn_out(l, "nA1", actT, par("g_mix"))
                turn_out(l, "nA3", actT, par("g_mix"))
                for k in range(6):
                    for b in range(NB):
                        out_unit(l, f"z{k}{b}", z[:, b, k * BW:(k + 1) * BW])
                e.wait_ge(lam_in, l + 1)
                e.activation(lam[:, 2:4], lam[:, 0:2], ACT.Exp).then_inc(lam_exp, 1)
                turn_out(l, "qk1", qkT[:, 0, 2:4, :].rearrange("p c t -> p (c t)"))
                turn_out(l, "qk3", qkT[:, 1, 2:4, :].rearrange("p c t -> p (c t)"))
                exps(l, 0)
                for u in range(2):
                    out_unit(l, f"pd{u}", poolT[:, 2 * u:2 * u + 2, :].rearrange("p c t -> p (c t)"))
                gates_out(l, 0)
                exps(l, 1)
                gates_out(l, 1)
                exps(l, 2)
                wait_tp_done(e, l, "a1")
                e.activation(aT[:, 0, 2:4, 0, :], tbank("a1")[:, 0:256].rearrange("p (h q) -> p h q", h=2), ACT.Copy) \
                    .then_inc(tfreed("a1"), 1)
                out_unit(l, "av0", xn[:, 0, 0:BW])
                gates_out(l, 2)
                exps(l, 3)
                gates_out(l, 3)
                wait_tp_done(e, l, "a3")
                e.activation(aT[:, 1, 2:4, :, :].rearrange("p h k q -> p (h k q)"), tbank("a3")[:, :], ACT.Copy) \
                    .then_inc(tfreed("a3"), 1)
                out_unit(l, "av1", xn[:, 1, 0:BW])
                for u in range(2):
                    unit = f"py{u}"
                    wait_proj_done(e, l, unit)
                    for k in range(2):
                        g = 2 * u + k
                        ins = e.activation(brT[:, 1, g, :], bank(unit)[:, k * T:(k + 1) * T], ACT.Copy,
                                           scale=par("pool_scale")[:, g:g + 1])
                    ins.then_inc(freed(unit), 1)
                gates_out(l, 4)
                gates_out(l, 5)
                for i in range(4):
                    out_unit(l, f"km{i}", kmT[:, 2 * i:2 * i + 2, :].rearrange("p c t -> p (c t)"))
                for i in range(4):
                    out_unit(l, f"vm{i}", vm[:, i % 2, (i // 2) * BW:(i // 2 + 1) * BW])
                turn_out(l, "o1", brT[:, 0, 2:4, :].rearrange("p c t -> p (c t)"))
                turn_out(l, "s1", brT[:, 2, 2:4, :].rearrange("p c t -> p (c t)"))
                turn_out(l, "m1", actT, 0.5)
                turn_out(l, "m3", actT, 0.5)
                square(l, 1)
                turn_out(l, "nC1", actT, par("g_cross"))
                turn_out(l, "nC3", actT, par("g_cross"))
                for i in range(4):
                    out_unit(l, f"xq{i}", xqT[:, 2 * i:2 * i + 2, :].rearrange("p c t -> p (c t)"))
                for b in range(NB):
                    e.wait_ge(max_ready, l * 6 + 4 + b + 1)
                    for h in range(X_HEADS):
                        ins = e.activation(probs[:, b, h, :], pair[:, h * T:(h + 1) * T], ACT.Exp,
                                           bias=neg_max[:, b, h:h + 1], scale=X_SCALE,
                                           accum_out=row_sum[:, b, h:h + 1])
                    ins.then_inc(exp_done, 1)
                    e.drain()
                    e.sem_inc(att_out, 1)
                for u in (1, 3):
                    wait_tp_done(e, l, f"e{u}")
                    b = u // 2
                    e.activation(eT[:, 2:4, :, b * P:(b + 1) * P],
                                 tbank(f"e{u}")[:, :].rearrange("p (h m t) -> p h m t", h=2, m=NB), ACT.Copy) \
                        .then_inc(tfreed(f"e{u}"), 1)
                for i in range(4):
                    out_unit(l, f"co{i}", actT[:, 2 * i:2 * i + 2, :].rearrange("p c t -> p (c t)"))
                square(l, 2)
                turn_out(l, "nF1", actT, par("g_ffn"))
                turn_out(l, "nF3", actT, par("g_ffn"))
                for i in range(8):
                    out_unit(l, f"pq{i}", peer_qT[:, 2 * i:2 * i + 2, :].rearrange("p c t -> p (c t)"))
                for i in range(8):
                    out_unit(l, f"sc{i}", scores[:, 2 * i:2 * i + 2, :].rearrange("p h n -> p (h n)"))
                gate_exps(l, 0, 0)
                with e.Fori(0, NB) as b:
                    with e.Fori(0, HEADS // 2) as hh:
                        for s in range(2):
                            i = b * HEADS + hh * 2 + s
                            e.wait_ge(gate_ready, l * TOPS + i + 1)
                            for g in range(4):
                                e.wait_ge(dots_ready, (l * STEPS + i) * 4 + g + 1)
                                e.activation(gelu[:, s, 4 * g:4 * g + 4], dots[:, s, 4 * g:4 * g + 4], ACT.Gelu)
                                e.drain()
                                for j in range(4 * g, 4 * g + 4):
                                    e.activation(weight[:, s, j:j + 1], gelu[:, s, j:j + 1], ACT.Copy,
                                                 scale=gate[:, s, j:j + 1])
                                e.drain()
                                for j in range(4 * g, 4 * g + 4):
                                    e.wait_ge(tile_used, (l * STEPS + i) * TOPK + j + 1)
                                    e.activation(diag[:, j % SLOTS, :], ident, ACT.Copy,
                                                 scale=weight[:, s, j:j + 1]).then_inc(diag_ready, 1)
                                if g == 2:
                                    gate_exps(l, i + 1, 1 - s)
            square(L, 0)

        @block.gpsimd
        def _(e):
            def root(k, r, n):
                e.wait_ge(var_ready, k)
                e.tensor_tensor(rstd[:, r, 0:n], var[:, r, 0:n], half[:, 0:n], ALU.pow).then_inc(rstd_ready, 1)

            root(1, 0, 2)
            with e.Fori(0, L) as l:
                root(l * 5 + 2, 0, 2)
                e.wait_ge(xn_ready, l * 3 + 2)
                e.wait_ge(params_in_s, l * 16 + 16)
                for u in range(2):
                    e.wait_ge(tp_out[u], MEM_TU // 2 + 1)
                e.nop(nofuse=True)
                for c in range(KC):
                    ins = e.tensor_scalar(memT[:, c, :], memT0[:, c, :], par("g_mem")[:, c:c + 1], None, ALU.mult)
                ins.then_inc(memT_ready, 1)
                root(l * 5 + 3, 3, 2)
                root(l * 5 + 4, 4, 8)
                root(l * 5 + 5, 1, 2)
                root(l * 5 + 6, 2, 2)
                wait_proj_done(e, l, "sc7")
                e.nop(nofuse=True)
                with e.Fori(0, NB) as b:
                    with e.Fori(0, HEADS // 2) as hh:
                        for s in range(2):
                            i = b * HEADS + hh * 2 + s
                            e.wait_ge(expert_ready, l * TOPS + i + 1)
                            e.nop(nofuse=True)
                            for j in range(TOPK):
                                e.wait_ge(tile_used, (l * STEPS + i) * TOPK + j + 1)
                                e.nop(nofuse=True)
                                e.indirect_dma_start(shared[:, j % SLOTS, :], None, experts,
                                                     bass.IndirectOffsetOnAxis(expert[:, s, j:j + 1], 0)) \
                                    .then_inc(got[j % SLOTS], 16)
            root(L * 5 + 2, 0, 2)


def _constants():
    c = np.zeros((P, CONST_COLS), np.float32)

    def put(name, v):
        c[:, CONSTS[name][0]:CONSTS[name][1]] = v

    put("ident", np.eye(P))
    q, k = np.arange(P)[:, None], np.arange(P)[None, :]
    put("mask", np.concatenate([np.zeros((P, P)), np.where(k <= q, 0.0, MASKED)], 1))
    put("triu", q <= k)
    s, t = np.arange(T)[:, None], np.arange(T)[None, :]
    cols = []
    for w in WINDOWS:
        m = ((s <= t) & (s > t - w)) / np.minimum(t + 1, w) - (s == t)
        cols.append(np.concatenate([m[0:P, :], m[P:T, P:T]], 1))
    put("pool", np.concatenate(cols, 1))
    put("iota", np.arange(TOPK)[None, :])
    put("inv", (np.float32(ROPE_THETA) ** (-np.arange(0, ROT, 2, dtype=np.float32) / np.float32(ROT)))[None, :])
    put("expert_base", (np.arange(L) * NK * NK)[None, :])
    return c


def _panels(w):
    rows, cols = w.shape
    chunks = rows // P
    width = PANEL // chunks
    return w.reshape(chunks, P, cols // width, width).transpose(2, 1, 0, 3).reshape(cols // width, P, PANEL)


def _stream(a, l):
    keys = a["sub_keys"][l].transpose(3, 0, 1, 2).reshape(1, P, 2 * HEADS * NK)
    keys = np.concatenate([keys, np.zeros_like(keys)], 2)
    branch = [_panels(a["w_branch"][l, n]) for n in range(3)]
    return np.concatenate([_panels(a["w_in"][l]), _panels(a["w_xkv"][l]), *branch, _panels(a["w_out"][l]),
                           _panels(a["w_xq"][l]), _panels(a["w_xo"][l]), _panels(a["w_pq"][l].reshape(D, -1)), keys])


def _params(a, l):
    p = np.zeros((P, PARAM_COLS), np.float32)

    def put(name, v):
        p[:, PARAMS[name][0]:PARAMS[name][1]] = v

    for name in ("g_mix", "g_cross", "g_mem", "g_ffn"):
        put(name, a[name][l].reshape(KC, P).T)
    put("pool_scale", a["pool_scale"][l].reshape(4, P).T)
    put("b_spatial", a["b_spatial"][l].T)
    start = 0.8 - 0.6 * np.exp(-0.3 * l)
    put("lam_init", start)
    put("one_less", 1.0 - start)
    put("lam_qk", a["lam_qk"][l].reshape(1, -1))
    for name in ("subln_g", "sg_ln_g", "sg_ln_b"):
        put(name, a[name][l][None, :])
    put("g_ffn_row", a["g_ffn"][l][None, :])
    put("w_spatial", a["w_spatial"][l].transpose(2, 0, 1).reshape(P, -1))
    put("w_pool", a["w_pool"][l].transpose(1, 0, 2).reshape(P, -1))
    return p


def kernel(**inputs):
    import concourse.bacc as _bacc
    from concourse.bass_utils import run_bass_kernel_spmd as _run

    a = {k: np.asarray(v) for k, v in inputs.items()}
    arrays = {
        "x_in": a["x"],
        "mem_in": a["mem"],
        "pos_in": a["positions"],
        "stream": np.concatenate([_stream(a, l) for l in range(L)]),
        "params_in": np.stack([_params(a, l) for l in range(L)]),
        "consts_in": _constants(),
        "g_final": np.broadcast_to(a["g_final"][None, :], (P, D)),
        "experts": np.concatenate([a["peer_u"], a["peer_v"]], 2).reshape(L * NK * NK, 2 * D),
    }
    arrays = {k: np.ascontiguousarray(v) for k, v in arrays.items()}
    nc = _bacc.Bacc("TRN2", target_bir_lowering=False, num_devices=1)
    args = [nc.dram_tensor(k, v.shape, mybir.dt.from_np(v.dtype), kind="ExternalInput").ap() for k, v in arrays.items()]
    out = nc.dram_tensor("out", a["x"].shape, F32, kind="ExternalOutput").ap()
    trunk(nc, *args, out)
    r = _run(nc, [arrays], core_ids=[0])
    return r.results[0]["out"]
```

```python
from contextlib import ExitStack

import numpy as np

import concourse.bass as bass
from concourse import mybir

F32 = mybir.dt.float32
F32R = mybir.dt.float32r
BF16 = mybir.dt.bfloat16
I32 = mybir.dt.int32
U32 = mybir.dt.uint32
ALU = mybir.AluOpType
ACT = mybir.ActivationFunctionType
AX = mybir.AxisListType.X
ds = bass.ds

P = 128
L = 2
D = 1024
T = 256
NB = T // P
KC = D // P
EPS = 1e-6
DA_HEADS = 4
DA_DIM = 64
ROT = 16
HALF = ROT // 2
ROPE_THETA = 500000.0
WINDOWS = (2, 4, 8, 16)
X_HEADS = 4
X_SCALE = float(D // X_HEADS) ** -0.5
DA_SCALE = float(DA_DIM) ** -0.5
HEADS = 8
NK = 128
TOPK = 16
BW = 512
MASKED = -1e30
LOWEST = -3e38

PANEL = 4096
Z_PANEL, GATE_PANEL, BRANCH_PANEL, OUT_PANEL, K_PANEL, XQ_PANEL, V_PANEL, XO_PANEL, PQ_PANEL = \
    0, 6, 12, 15, 17, 19, 21, 23, 25
PANELS = 29
PSLOTS = 2
PIECE = 512
PIECES = PANEL // PIECE
SPLITS = PANELS * PIECES
WSLOTS = 4
AHEAD = WSLOTS - 1
BRANCH_ORDER = (1, 2, 0)

PARAMS = {}
_at = 0
for _name, _n in (("g_mix", 8), ("g_cross", 8), ("g_mem", 8), ("g_ffn", 8), ("pool_scale", 4), ("b_spatial", 4),
                  ("lam_init", 1), ("one_less", 1), ("lam_qk", 256), ("subln_g", 128), ("sg_ln_g", 512),
                  ("sg_ln_b", 512), ("g_ffn_row", 1024), ("w_spatial", 512), ("w_pool", 512)):
    PARAMS[_name] = (_at, _at + _n)
    _at += _n
PARAM_COLS = _at
GAIN_COLS = PARAMS["lam_qk"][0]

CONSTS = {}
_at = 0
for _name, _n in (("ident", 128), ("iota", 16), ("inv", 8), ("expert_base", L), ("mask", 256),
                  ("pool", 4 * 384), ("triu", 128)):
    CONSTS[_name] = (_at, _at + _n)
    _at += _n
CONST_COLS = _at
SMALL_CONSTS = CONSTS["mask"][0]

LATE_SCORES = (1, 2, 3, 5, 6, 7)

PROJ = ([f"z{p}{b}" for p in range(6) for b in range(2)]
        + ["pd0", "pd1", "g00", "g01", "g10", "g11", "g20", "g21", "av0", "sm0", "sm1", "g30", "g31", "g40", "g41",
           "av1", "py0", "py1", "g50", "g51"]
        + [f"br{n}{h}{b}" for n in BRANCH_ORDER for h in range(2) for b in range(2)]
        + [f"wo{i}" for i in range(4)] + [f"km{i}" for i in range(4)] + [f"xq{i}" for i in range(4)]
        + [f"vm{i}" for i in range(4)] + [f"co{i}" for i in range(4)] + [f"xo{i}" for i in range(4)]
        + ["pq0", "pq1", "sc0", "sc4"] + [f"pq{i}" for i in range(2, 8)] + [f"sc{i}" for i in LATE_SCORES])
TRANS = [k + str(i) for k, n in (("nA", 4), ("qk", 4), ("a", 4), ("s", 2), ("o", 2), ("mT", 4), ("m", 4),
                                 ("nC", 4), ("e", 4), ("nF", 4)) for i in range(n)]
TURNED = [k + str(i) for k, n in (("nA", 4), ("py", 2), ("s", 2), ("o", 2), ("mT", 4), ("m", 4), ("nC", 4),
                                  ("co", 4), ("nF", 4)) for i in range(n)]
PU, TU, HU = len(PROJ), len(TRANS), len(TURNED)
assert PU % 4 == 0 and TU % 2 == 0

ROOTS = 6
GROUP = 2
SLOTS = 8
STEPS = NB * HEADS
TILES = STEPS * TOPK
TOPS = STEPS + 1


def trunk(nc, x_in, mem_in, pos_in, stream, keys_in, params_in, consts_in, g_final, experts, out):
    ctx = ExitStack()
    with ctx:
        def sb(name, shape, dt=F32):
            return ctx.enter_context(nc.sbuf_tensor(name, shape, dt))

        def sem(name):
            return ctx.enter_context(nc.semaphore(name))

        x = sb("x", [P, NB, D])
        xn = sb("xn", [P, NB, D])
        params = sb("params", [P, PARAM_COLS])
        consts = sb("consts", [P, CONST_COLS])
        panels = sb("panels", [P, PSLOTS, PANEL])

        Z0, G0, W0, A0, S0, B0, END = 0, 6144, 12288, 19456, 23552, 27648, 33792
        base_bytes = nc.sbuf_base
        base_bytes += -base_bytes % 32
        arena = sb("arena", [P, END + 8])
        flat = arena[:, 0:END]

        def split_tensor(name, shape, column):
            return nc.alloc_sbuf_tensor_at(name, shape, F32R, offset=base_bytes + 4 * column)

        act_hi = split_tensor("act_hi", [P, KC, T], A0)
        act_lo = split_tensor("act_lo", [P, KC, T], A0 + 2048)
        w_hi = split_tensor("w_hi", [P, WSLOTS, PIECE], S0)
        w_lo = split_tensor("w_lo", [P, WSLOTS, PIECE], S0 + 2048)
        br_hi = split_tensor("br_hi", [P, 12, T], B0)
        br_lo = split_tensor("br_lo", [P, 12, T], B0 + 3072)

        def cols(start, n):
            return flat[:, start:start + n]

        z = cols(Z0, 6144).rearrange("p (b n) -> p b n", b=NB)
        kmT = cols(Z0, 2048).rearrange("p (c t) -> p c t", c=KC)
        vm = cols(Z0 + 2048, 2048).rearrange("p (b n) -> p b n", b=NB)
        gates = cols(G0, 6144).rearrange("p (b n) -> p b n", b=NB)
        qkT = cols(W0, 2048).rearrange("p (a h t) -> p a h t", a=2, h=4)
        mem_rows = cols(W0, 2048).rearrange("p (b n) -> p b n", b=NB)
        xqT = cols(W0, 2048).rearrange("p (c t) -> p c t", c=KC)
        poolT = cols(W0 + 2048, 1024).rearrange("p (c t) -> p c t", c=4)
        probsT = cols(W0 + 3072, 2048)
        merged = probsT.rearrange("p (b n) -> p b n", b=NB)
        aT = probsT.rearrange("p (b h k q) -> p b h k q", b=NB, h=4, k=NB)
        eT = probsT.rearrange("p (h m t) -> p h m t", h=X_HEADS, m=NB)
        probs = cols(W0 + 5120, 2048).rearrange("p (u i k) -> p u i k", u=2, i=4)
        rot = cols(W0 + 5120, 1024).rearrange("p (k b n) -> p k b n", k=4, b=NB)
        gated = cols(W0 + 5120, 1024).rearrange("p (k n) -> p k n", k=2)
        tiles = [cols(2048 * i, 2048) for i in range(5)] + [cols(A0 + 2048 * i, 2048) for i in range(2)] \
            + [cols(2048 * 5, 2048)]
        keys = cols(2048 * 5, 2048)
        peer_qT = cols(W0, 4096).rearrange("p (h t) -> p h t", h=2 * HEADS)
        products = cols(W0 + 4096, 1024)
        x_now = cols(W0 + 5120, 1024)
        diag = cols(W0 + 6144, 1024).rearrange("p (s n) -> p s n", s=SLOTS)
        scores = cols(B0, 4352).rearrange("p (h n) -> p h n", h=TOPS)
        head_sc = cols(B0 + 4352, 256).rearrange("p (a n) -> p a n", a=2)
        head_less = cols(B0 + 4608, 256).rearrange("p (a n) -> p a n", a=2)
        cand = cols(B0 + 4864, 256)
        cand_less = cols(B0 + 5120, 256)
        pick = cols(B0 + 5376, 512).rearrange("p (a k i) -> p a k i", a=2, k=TOPK)

        zeros = sb("zeros", [P, 512], BF16)
        half = sb("half", [P, 8])
        pos_i = sb("pos_i", [P, NB], I32)
        pos_f = sb("pos_f", [P, NB])
        ang = sb("ang", [P, 4, NB, HALF])
        trig = sb("trig", [P, 2, NB, HALF])
        sq = sb("sq", [P, 2])
        var = sb("var", [P, 6, 8])
        rstd = sb("rstd", [P, 6, 8])
        lam = sb("lam", [P, 4])
        mem_sq = sb("mem_sq", [P, NB])
        bn = sb("bn", [P, NB, 6])
        mv = sb("mv", [P, NB, 2])
        neg_max = sb("neg_max", [P, 2, 4])
        row_sum = sb("row_sum", [P, 2, 4])
        row_inv = sb("row_inv", [P, 2, 4])
        top = sb("top", [P, 2, TOPK])
        top_ix = sb("top_ix", [P, 2, TOPK], U32)
        top_ixf = sb("top_ixf", [P, 2, TOPK])
        best = sb("best", [P, 2, TOPK])
        best_neg = sb("best_neg", [P, 2])
        pos = sb("pos", [P, TOPK], U32)
        pos_ab = sb("pos_ab", [P, 2, TOPK], U32)
        chosen = sb("chosen", [P, 2, TOPK])
        expert = sb("expert", [P, 2, TOPK], I32)
        base = sb("base", [P, 1])
        gate_e = sb("gate_e", [P, 2, TOPK])
        gate_s = sb("gate_s", [P, 2])
        gate_r = sb("gate_r", [P, 2])
        gate = sb("gate", [P, 2, TOPK])
        dots = sb("dots", [P, 2, TOPK])
        gelu = sb("gelu", [P, 2, TOPK])
        weight = sb("weight", [P, 2, TOPK])

        def par(name):
            a, b = PARAMS[name]
            return params[:, a:b]

        def const(name):
            a, b = CONSTS[name]
            return consts[:, a:b]

        ident = const("ident")
        pool_m = const("pool").rearrange("p (g n) -> p g n", g=4)
        w_spatialT = par("w_spatial").rearrange("p (g t) -> p g t", g=4)
        w_pool = par("w_pool").rearrange("p (g e) -> p g e", g=4)

        mm = [ctx.enter_context(nc.psum_tensor(f"mm{i}", [P, 512], F32)) for i in range(4)]
        pair = ctx.enter_context(nc.psum_tensor("pair", [P, 1024], F32))
        tp = [ctx.enter_context(nc.psum_tensor(f"tp{i}", [P, 512], F32)) for i in range(2)]

        x_in_s = sem("x_landed")
        pos_in_s = sem("pos_landed")
        consts_in_s = sem("consts_landed")
        wide_in_s = sem("wide_consts_landed")
        gains_in_s = sem("gains_landed")
        params_in_s = sem("params_landed")
        keys_in_s = sem("keys_landed")
        mem_sq_ready = sem("mem_sq_ready")
        params_free = sem("params_free")
        mem_in_s = sem("mem_landed")
        mem_ready = sem("mem_ready")
        w_hi_ready = sem("w_hi_ready")
        w_lo_ready = sem("w_lo_ready")
        piece_started = sem("piece_started")
        hi_ready = sem("hi_ready")
        panel_in = [sem(f"panel_in{i}") for i in range(PSLOTS)]
        proj_done = sem("proj_done")
        proj_out = [sem(f"proj_out{i}") for i in range(4)]
        tp_done = sem("tp_done")
        tp_out = [sem(f"tp_out{i}") for i in range(2)]
        att_done = sem("att_done")
        att_out = sem("att_out")
        x_ready = sem("x_ready")
        xn_ready = sem("xn_ready")
        sq_ready = sem("sq_ready")
        var_ready = sem("var_ready")
        rstd_ready = sem("rstd_ready")
        trig_in = sem("trig_in")
        trig_done = sem("trig_done")
        lam_in = sem("lam_in")
        lam_exp = sem("lam_exp")
        rope_ready = sem("rope_ready")
        max_ready = sem("max_ready")
        exp_done = sem("exp_done")
        probs_ready = sem("probs_ready")
        vn_ready = sem("vn_ready")
        on_ready = sem("on_ready")
        zeros_ready = sem("zeros_ready")
        got = [sem(f"got{i}") for i in range(SLOTS)]
        tile_used = sem("tile_used")
        expert_ready = sem("expert_ready")
        best_ready = sem("best_ready")
        gate_exp = sem("gate_exp")
        gate_ready = sem("gate_ready")
        dots_ready = sem("dots_ready")
        diag_ready = sem("diag_ready")
        acc_free = sem("acc_free")
        stored = sem("stored")

        def wait_proj_done(e, l, unit):
            e.wait_ge(proj_done, l * PU + (PU + PROJ.index(unit) + 1))

        def wait_proj_out(e, l, unit):
            i = PROJ.index(unit)
            e.wait_ge(proj_out[i % 4], l * (PU // 4) + i // 4 + 2)

        def wait_tp_done(e, l, unit):
            e.wait_ge(tp_done, l * TU + TRANS.index(unit) + 1)

        def wait_tp_out(e, l, unit):
            i = TRANS.index(unit)
            e.wait_ge(tp_out[i % 2], l * (TU // 2) + i // 2 + 2)

        def wait_panel(e, l, k):
            e.wait_ge(panel_in[k % PSLOTS], (l * len(range(k % PSLOTS, PANELS, PSLOTS)) + k // PSLOTS + 1) * 16)

        def turned(unit):
            kind, i = unit[:-1], int(unit[-1])
            hi, lo = (act_hi, act_lo) if kind in ("nA", "m", "nC", "co", "nF") else (br_hi, br_lo)
            c = {"o": 0, "py": 4, "s": 8}.get(kind, 0) + 2 * i
            return hi[:, c:c + 2, :], lo[:, c:c + 2, :]

        def gains(unit):
            kind, c = unit[:-1], 2 * int(unit[-1])
            name = {"nA": "g_mix", "nC": "g_cross", "nF": "g_ffn", "mT": "g_mem", "py": "pool_scale"}.get(kind)
            if name is None:
                return 0.5 if kind == "m" else None
            return [par(name)[:, c + k:c + k + 1] for k in range(2)]

        def source(e, l, unit):
            if unit in PROJ:
                wait_proj_done(e, l, unit)
                return bank(unit), freed(unit)
            wait_tp_done(e, l, unit)
            return tbank(unit), tfreed(unit)

        def bank(unit):
            return mm[PROJ.index(unit) % 4]

        def tbank(unit):
            return tp[TRANS.index(unit) % 2]

        def freed(unit):
            return proj_out[PROJ.index(unit) % 4]

        def tfreed(unit):
            return tp_out[TRANS.index(unit) % 2]

        block = ctx.enter_context(nc.Block())

        @block.sync
        def _(e):
            e.dma_start(consts[:, 0:SMALL_CONSTS], consts_in[:, 0:SMALL_CONSTS]).then_inc(consts_in_s, 16)
            e.dma_start(pos_i[:, :], pos_in.rearrange("a (b p) -> p (a b)", p=P),
                        allow_slow_non_contiguous=True).then_inc(pos_in_s, 16)
            e.dma_start(x[:, :, :], x_in.rearrange("a (b p) d -> p (a b) d", p=P)).then_inc(x_in_s, 16)

            def load_params(l, a, b, landed):
                e.dma_start(params[:, a:b], params_in[ds(l, 1), :, a:b].rearrange("a p n -> p (a n)")) \
                    .then_inc(landed, 16)

            with e.Fori(0, L) as l:
                e.wait_ge(params_free, l + 1)
                load_params(l, 0, GAIN_COLS, gains_in_s)
                for k in range(PANELS):
                    e.wait_ge(w_lo_ready, l * SPLITS + (SPLITS + PIECES * max(k - 1, 0)))
                    e.dma_start(panels[:, k % PSLOTS, :], stream[ds(l * PANELS + k, 1)]
                                .rearrange("a p n -> p (a n)")).then_inc(panel_in[k % PSLOTS], 16)
                    if k == 1:
                        load_params(l, GAIN_COLS, PARAM_COLS, params_in_s)
                    if k == V_PANEL:
                        e.dma_start(keys, keys_in[ds(l, 1)].rearrange("a p n -> p (a n)")).then_inc(keys_in_s, 16)
                    if k == BRANCH_PANEL + 1:
                        e.wait_ge(att_done, l * 6 + 4)
                        e.dma_start(mem_rows, mem_in.rearrange("a (b p) d -> p (a b) d", p=P)).then_inc(mem_in_s, 16)
            e.wait_ge(params_free, L + 1)
            e.dma_start(params[:, 0:D], g_final).then_inc(params_in_s, 16)
            e.wait_ge(xn_ready, 3 * L + 1)
            e.dma_start(out.rearrange("a (b p) d -> p (a b) d", p=P), xn[:, :, :]).then_inc(stored, 16)
            e.wait_ge(stored, 16)

        @block.tensor
        def _(e):
            def open_unit(l, unit):
                i = PROJ.index(unit)
                e.wait_ge(proj_out[i % 4], l * (PU // 4) + i // 4 + 1)
                return mm[i % 4]

            def open_tp(l, unit):
                i = TRANS.index(unit)
                e.wait_ge(tp_out[i % 2], l * (TU // 2) + i // 2 + 1)
                return tp[i % 2]

            def turn_rows(l, kind, src):
                for u in range(4):
                    ps = open_tp(l, f"{kind}{u}")
                    for c in range(2):
                        for b in range(NB):
                            o = c * T + b * P
                            ins = e.transpose(ps[:, o:o + P], src[:, b, (2 * u + c) * P:(2 * u + c + 1) * P], ident)
                    ins.then_inc(tp_done, 1)

            def piece(l, k, i):
                e.wait_ge(w_lo_ready, l * SPLITS + (SPLITS + k * PIECES + i + 1))
                n = (k * PIECES + i) % WSLOTS
                return w_hi[:, n, :], w_lo[:, n, :]

            def wait_turned(l, kind, c):
                if kind and c % 2 == 0:
                    unit = f"{kind}{c // 2}"
                    if unit in PROJ:
                        wait_proj_out(e, l, unit)
                    else:
                        wait_tp_out(e, l, unit)

            def rows_times(l, k, i0, n, units, hi, lo, turns=None):
                ps = None
                for c in range(n):
                    wait_turned(l, turns, c)
                    wh, wl = piece(l, k, i0 + c)
                    if c == 0:
                        ps = [open_unit(l, unit) for unit in units]
                    for b in range(NB):
                        s = slice(b * P, (b + 1) * P)
                        ins = e.matmul(ps[b][:, :], hi[:, c, s], wh, start=c == 0, stop=False)
                        if b == 0:
                            ins.then_inc(piece_started, 1)
                        e.matmul(ps[b][:, :], hi[:, c, s], wl, start=False, stop=False)
                        ins = e.matmul(ps[b][:, :], lo[:, c, s], wh, start=False, stop=c == n - 1)
                        if c == n - 1:
                            ins.then_inc(proj_done, 1)

            def full_panel(l, k, units, hi=act_hi, lo=act_lo, turns=None):
                rows_times(l, k, 0, KC, units, hi, lo, turns)

            def column_panel(l, k, units, hi=act_hi, lo=act_lo, turns=None, third=None):
                ps = None
                for c in range(KC):
                    if third and c == 2:
                        third()
                    wait_turned(l, turns, c)
                    wh, wl = piece(l, k, c)
                    if c == 0:
                        ps = [open_unit(l, unit) for unit in units]
                    for j in range(4):
                        o = ps[j // 2][:, (j % 2) * T:(j % 2 + 1) * T]
                        s = slice(j * P, (j + 1) * P)
                        ins = e.matmul(o, wh[:, s], hi[:, c, :], start=c == 0 and j % 2 == 0, stop=False,
                                       skip_group_check=True)
                        if j == 0:
                            ins.then_inc(piece_started, 1)
                        e.matmul(o, wh[:, s], lo[:, c, :], start=False, stop=False, skip_group_check=True)
                        ins = e.matmul(o, wl[:, s], hi[:, c, :], start=False, stop=c == KC - 1,
                                       skip_group_check=True)
                        if c == KC - 1 and j % 2 == 1:
                            ins.then_inc(proj_done, 1)

            def gate_panel(l, k):
                full_panel(l, GATE_PANEL + k, (f"g{k}0", f"g{k}1"))

            def scores_unit(l, u):
                b, h0 = u // 2, 2 * (u % 2)
                e.wait_ge(att_out, l * 6 + u + 1)
                for m in range(2):
                    for k in range(2):
                        o = (2 * m + k) * 256
                        ins = e.matmul(pair[:, o:o + P * (b + 1)],
                                       qkT[64 * m:64 * m + 64, 0, h0 + k, b * P:(b + 1) * P],
                                       qkT[64 * m:64 * m + 64, 1, h0 + k, 0:P * (b + 1)], start=True, stop=True)
                ins.then_inc(att_done, 1)

            def turn_probs(l, u):
                b = u // 2
                ps = open_tp(l, f"a{u}")
                e.wait_ge(probs_ready, l * 6 + u + 1)
                for k in range(2):
                    for kb in range(b + 1):
                        o = (k * (b + 1) + kb) * P
                        ins = e.transpose(ps[:, o:o + P], probs[:, u % 2, k, kb * P:(kb + 1) * P], ident)
                ins.then_inc(tp_done, 1)

            def probs_times_v(l, b):
                ps = open_unit(l, f"av{b}")
                for h in range(DA_HEADS):
                    for kb in range(b + 1):
                        ins = e.matmul(ps[:, h * P:(h + 1) * P], aT[:, b, h, kb, :],
                                       z[:, kb, 1024 + h * P:1024 + (h + 1) * P], start=kb == 0, stop=kb == b)
                ins.then_inc(proj_done, 1)

            e.wait_ge(zeros_ready, 1)
            e.wait_ge(consts_in_s, 16)
            e.sem_inc(proj_done, PU)
            e.sem_inc(tile_used, SLOTS)
            e.sem_inc(piece_started, AHEAD)

            with e.Fori(0, L) as l:
                e.wait_ge(xn_ready, l * 3 + 1)
                turn_rows(l, "nA", xn)
                for k in range(6):
                    full_panel(l, Z_PANEL + k, (f"z{k}0", f"z{k}1"), turns="nA" if k == 0 else None)
                e.wait_ge(rope_ready, l + 1)
                for u in range(4):
                    ps = open_tp(l, f"qk{u}")
                    for k in range(2):
                        for b in range(NB):
                            n = (u // 2) * BW + (2 * (u % 2) + k) * P
                            o = k * T + b * P
                            ins = e.transpose(ps[:, o:o + P], z[:, b, n:n + P], ident)
                    ins.then_inc(tp_done, 1)
                wait_tp_out(e, l, "qk2")
                wait_tp_out(e, l, "qk3")
                scores_unit(l, 0)
                e.wait_ge(wide_in_s, 16)
                wait_proj_out(e, l, "z31")
                for u in range(2):
                    ps = open_unit(l, f"pd{u}")
                    for k in range(2):
                        g = 2 * u + k
                        c = 1536 + g * P
                        e.matmul(ps[:, k * T:(k + 1) * T], z[:, 0, c:c + P], pool_m[:, g, 0:T], start=True, stop=False)
                        ins = e.matmul(ps[:, k * T + P:(k + 1) * T], z[:, 1, c:c + P], pool_m[:, g, T:T + P],
                                       start=False, stop=True)
                    ins.then_inc(proj_done, 1)
                gate_panel(l, 0)
                scores_unit(l, 1)
                turn_probs(l, 0)
                gate_panel(l, 1)
                scores_unit(l, 2)
                turn_probs(l, 1)
                gate_panel(l, 2)
                wait_tp_out(e, l, "a0")
                wait_tp_out(e, l, "a1")
                probs_times_v(l, 0)
                scores_unit(l, 3)
                turn_probs(l, 2)
                e.wait_ge(vn_ready, l + 1)
                for b in range(NB):
                    ps = open_unit(l, f"sm{b}")
                    for g in range(4):
                        ins = e.matmul(ps[:, g * P:(g + 1) * P], w_spatialT[:, g, :],
                                       z[:, b, 2560 + g * P:2560 + (g + 1) * P], start=True, stop=True)
                    ins.then_inc(proj_done, 1)
                gate_panel(l, 3)
                turn_probs(l, 3)
                gate_panel(l, 4)
                wait_tp_out(e, l, "a2")
                wait_tp_out(e, l, "a3")
                probs_times_v(l, 1)
                wait_proj_out(e, l, "pd0")
                wait_proj_out(e, l, "pd1")
                e.wait_ge(params_in_s, l * 16 + 16)
                for u in range(2):
                    ps = open_unit(l, f"py{u}")
                    for k in range(2):
                        ins = e.matmul(ps[:, k * T:(k + 1) * T], w_pool[:, 2 * u + k, :], poolT[:, 2 * u + k, :],
                                       start=True, stop=True)
                    ins.then_inc(proj_done, 1)
                gate_panel(l, 5)

                def turn_mixer(kind, c0):
                    for u in range(2):
                        ps = open_tp(l, f"{kind}{u}")
                        for k in range(2):
                            for b in range(NB):
                                n = c0 + (2 * u + k) * P
                                o = k * T + b * P
                                ins = e.transpose(ps[:, o:o + P], xn[:, b, n:n + P], ident)
                        ins.then_inc(tp_done, 1)

                def branch(p, n, turns):
                    for h in range(2):
                        rows_times(l, BRANCH_PANEL + p, 4 * h, 4, (f"br{n}{h}0", f"br{n}{h}1"),
                                   br_hi[:, 4 * n:4 * n + 4, :], br_lo[:, 4 * n:4 * n + 4, :],
                                   turns if h == 0 else None)

                wait_proj_out(e, l, "sm0")
                wait_proj_out(e, l, "sm1")
                turn_mixer("s", BW)
                branch(0, 1, "py")
                branch(1, 2, "s")
                e.wait_ge(on_ready, l + 1)
                turn_mixer("o", 0)
                branch(2, 0, "o")
                e.wait_ge(mem_ready, l + 1)
                turn_rows(l, "mT", mem_rows)
                for unit in ("br000", "br001", "br010", "br011"):
                    wait_proj_out(e, l, unit)
                turn_rows(l, "m", merged)
                for k in range(2):
                    full_panel(l, OUT_PANEL + k, (f"wo{2 * k}", f"wo{2 * k + 1}"), turns=None if k else "m")
                for k in range(2):
                    column_panel(l, K_PANEL + k, (f"km{2 * k}", f"km{2 * k + 1}"), br_hi, br_lo)
                e.wait_ge(xn_ready, l * 3 + 2)
                turn_rows(l, "nC", xn)
                for k in range(2):
                    column_panel(l, XQ_PANEL + k, (f"xq{2 * k}", f"xq{2 * k + 1}"), turns=None if k else "nC")
                for i in range(4):
                    wait_proj_out(e, l, f"xq{i}")
                    wait_proj_out(e, l, f"km{i}")
                for b in range(NB):
                    e.wait_ge(att_out, l * 6 + 4 + b + 1)
                    for h in range(X_HEADS):
                        for k in range(2):
                            ins = e.matmul(pair[:, h * T:(h + 1) * T], xqT[:, 2 * h + k, b * P:(b + 1) * P],
                                           kmT[:, 2 * h + k, :], start=k == 0, stop=k == 1)
                    ins.then_inc(att_done, 1)
                    full_panel(l, V_PANEL + b, (f"vm{2 * b}", f"vm{2 * b + 1}"), br_hi, br_lo)
                for u in range(4):
                    b, h0 = u // 2, 2 * (u % 2)
                    ps = open_tp(l, f"e{u}")
                    e.wait_ge(probs_ready, l * 6 + 4 + b + 1)
                    for k in range(2):
                        for m in range(NB):
                            o = (k * NB + m) * P
                            ins = e.transpose(ps[:, o:o + P], probs[:, b, h0 + k, m * P:(m + 1) * P], ident)
                    ins.then_inc(tp_done, 1)
                wait_tp_out(e, l, "e2")
                wait_tp_out(e, l, "e3")
                for i in range(4):
                    wait_proj_out(e, l, f"vm{i}")
                for u in range(4):
                    ps = open_unit(l, f"co{u}")
                    for k in range(2):
                        c = 2 * u + k
                        for m in range(NB):
                            ins = e.matmul(ps[:, k * T:(k + 1) * T], vm[:, m, c * P:(c + 1) * P], eT[:, c // 2, m, :],
                                           start=m == 0, stop=m == NB - 1)
                    ins.then_inc(proj_done, 1)
                for k in range(2):
                    full_panel(l, XO_PANEL + k, (f"xo{2 * k}", f"xo{2 * k + 1}"), turns=None if k else "co")
                e.wait_ge(xn_ready, l * 3 + 3)
                turn_rows(l, "nF", xn)
                def expert_scores(i):
                    ps = open_unit(l, f"sc{i}")
                    b, q = i // 4, i % 4
                    for k in range(4):
                        hp = 4 * q + k
                        ins = e.matmul(ps[:, k * NK:(k + 1) * NK], peer_qT[:, hp, b * P:(b + 1) * P],
                                       keys[:, hp * NK:(hp + 1) * NK], start=True, stop=True)
                    ins.then_inc(proj_done, 1)

                def first_scores():
                    wait_proj_out(e, l, "pq0")
                    wait_proj_out(e, l, "pq1")
                    e.wait_ge(keys_in_s, l * 16 + 16)
                    expert_scores(0)
                    expert_scores(4)

                column_panel(l, PQ_PANEL, ("pq0", "pq1"), turns="nF")
                column_panel(l, PQ_PANEL + 1, ("pq2", "pq3"), third=first_scores)
                column_panel(l, PQ_PANEL + 2, ("pq4", "pq5"))
                column_panel(l, PQ_PANEL + 3, ("pq6", "pq7"))
                for i in range(2, 8):
                    wait_proj_out(e, l, f"pq{i}")
                for i in LATE_SCORES:
                    expert_scores(i)
                with e.Fori(0, NB) as b:
                    e.wait_ge(acc_free, l * NB + b + 1)
                    for h in range(2):
                        e.matmul(pair[:, h * BW:(h + 1) * BW], zeros[:, 0:P], zeros[:, :], start=True, stop=False,
                                 skip_group_check=True)
                    with e.Fori(0, HEADS // 2) as hh:
                        for s in range(2):
                            for j in range(TOPK):
                                e.wait_ge(diag_ready, l * TILES + b * (TILES // NB) + hh * (2 * TOPK)
                                          + s * TOPK + j + 1)
                                for h in range(2):
                                    ins = e.matmul(pair[:, h * BW:(h + 1) * BW], diag[:, j % SLOTS, :],
                                                   tiles[j % SLOTS][:, D + h * BW:D + (h + 1) * BW],
                                                   start=False, stop=False, skip_group_check=True)
                                ins.then_inc(tile_used, 1)

        @block.vector
        def _(e):
            def norm(l, r):
                e.tensor_tensor_reduce(xn[:, 0, :], x[:, 0, :], x[:, 0, :], 1.0, 0.0, ALU.mult, ALU.add, sq[:, 0:1])
                e.drain()
                e.wait_ge(sq_ready, l * 3 + r + 1)
                e.tensor_scalar(var[:, r, 0:2], sq[:, :], 1.0 / D, EPS, ALU.mult, ALU.add).then_inc(var_ready, 1)
                e.wait_ge(rstd_ready, l * ROOTS + (0, 4, 5)[r] + 1)
                for b in range(NB):
                    ins = e.tensor_scalar(xn[:, b, :], x[:, b, :], rstd[:, r, b:b + 1], None, ALU.mult)
                return ins

            def rests(l, k, part, end=None):
                for i in range(part, end) if end else (range(0, AHEAD), range(AHEAD, PIECES))[part]:
                    n = k * PIECES + i
                    e.wait_ge(w_hi_ready, l * SPLITS + n + 1)
                    e.tensor_tensor(w_lo[:, n % WSLOTS, :], panels[:, k % PSLOTS, i * PIECE:(i + 1) * PIECE],
                                    w_hi[:, n % WSLOTS, :].bitcast(F32), ALU.subtract).then_inc(w_lo_ready, 1)

            def turn_rest(l, unit):
                e.wait_ge(hi_ready, l * HU + TURNED.index(unit) + 1)
                ps, free = source(e, l, unit)
                hi, lo = turned(unit)
                g = gains(unit)
                if isinstance(g, list):
                    for k in range(2):
                        ins = e.scalar_tensor_tensor(lo[:, k, :], ps[:, k * T:(k + 1) * T], g[k],
                                                     hi[:, k, :].bitcast(F32), ALU.mult, ALU.subtract)
                else:
                    ins = e.scalar_tensor_tensor(lo.rearrange("p c t -> p (c t)"), ps[:, :], 1.0 if g is None else g,
                                                 hi.rearrange("p c t -> p (c t)").bitcast(F32), ALU.mult,
                                                 ALU.subtract)
                ins.then_inc(free, 1)

            def turn_out(l, unit, dst):
                wait_tp_done(e, l, unit)
                e.tensor_copy(dst.rearrange("p c t -> p (c t)"), tbank(unit)[:, :]).then_inc(tfreed(unit), 1)

            def merge(l, n, h):
                for b in range(NB):
                    unit = f"br{n}{h}{b}"
                    wait_proj_done(e, l, unit)
                    g = gates[:, b, n * D + h * BW:n * D + (h + 1) * BW]
                    dst = merged[:, b, h * BW:(h + 1) * BW]
                    if n == BRANCH_ORDER[0]:
                        e.scalar_tensor_tensor(dst, g, 1.0, bank(unit)[:, :], ALU.add, ALU.mult) \
                            .then_inc(freed(unit), 1)
                    else:
                        e.scalar_tensor_tensor(gated[:, b, :], g, 1.0, bank(unit)[:, :], ALU.add, ALU.mult)
                        e.drain()
                        e.tensor_tensor(dst, dst, gated[:, b, :], ALU.add).then_inc(freed(unit), 1)

            def masked_max(l, u):
                b, n = u // 2, P * (u // 2 + 1)
                e.wait_ge(att_done, l * 6 + u + 1)
                mask = const("mask")[:, T - n:T].unsqueeze(1).broadcast_to([P, 4, n])
                src = pair[:, :].rearrange("p (i k) -> p i k", i=4)[:, :, 0:n]
                e.scalar_tensor_tensor(probs[:, u % 2, :, 0:n], src, DA_SCALE, mask, ALU.mult, ALU.add) \
                    .then_inc(att_out, 1)
                e.drain()
                e.tensor_reduce(neg_max[:, u % 2, :], probs[:, u % 2, :, 0:n], AX, ALU.max, negate=True) \
                    .then_inc(max_ready, 1)

            def difference(l, u):
                n = P * (u // 2 + 1)
                v = u % 2
                e.wait_ge(exp_done, l * 6 + u + 1)
                e.reciprocal(row_inv[:, v, :], row_sum[:, v, :])
                e.drain()
                e.tensor_scalar(row_inv[:, v, 2:4], row_inv[:, v, 2:4], lam[:, 0:1], None, ALU.mult)
                e.drain()
                for k in range(2):
                    e.tensor_scalar(probs[:, v, 2 + k, 0:n], probs[:, v, 2 + k, 0:n], row_inv[:, v, 2 + k:3 + k],
                                    None, ALU.mult)
                e.drain()
                for k in range(2):
                    ins = e.scalar_tensor_tensor(probs[:, v, k, 0:n], probs[:, v, k, 0:n], row_inv[:, v, k:k + 1],
                                                 probs[:, v, 2 + k, 0:n], ALU.mult, ALU.add)
                ins.then_inc(probs_ready, 1)

            def cross_max(l, b):
                e.wait_ge(att_done, l * 6 + 4 + b + 1)
                e.tensor_reduce(neg_max[:, b, :], pair[:, :].rearrange("p (i k) -> p i k", i=4), AX, ALU.max,
                                negate=True)
                e.drain()
                e.tensor_scalar(neg_max[:, b, :], neg_max[:, b, :], X_SCALE, None, ALU.mult).then_inc(max_ready, 1)

            def cross_probs(l, b):
                e.wait_ge(exp_done, l * 6 + 4 + b + 1)
                e.reciprocal(row_inv[:, b, :], row_sum[:, b, :])
                e.drain()
                e.tensor_tensor(probs[:, b, :, :], probs[:, b, :, :],
                                row_inv[:, b, :].unsqueeze(2).broadcast_to([P, 4, T]), ALU.mult) \
                    .then_inc(probs_ready, 1)

            def add_rows(l, unit, b, cols):
                wait_proj_done(e, l, unit)
                dst = x[:, b, cols * BW:(cols + 1) * BW]
                return e.tensor_tensor(dst, bank(unit)[:, :], dst, ALU.add)

            def top_halves(i):
                e.tensor_copy(head_sc[:, :, :], scores[:, ds(i, 1), :].rearrange("p a (h n) -> p (a h) n", h=2))
                e.drain()
                for a in range(2):
                    e.max(top[:, a, 0:8], head_sc[:, a, :])
                e.drain()

            def top_halves_rest():
                for a in range(2):
                    e.max_index(top_ix[:, a, 0:8], top[:, a, 0:8], head_sc[:, a, :])
                    e.match_replace(head_less[:, a, :], top[:, a, 0:8], head_sc[:, a, :], LOWEST)
                e.drain()

            def top_halves_second():
                for a in range(2):
                    e.max(top[:, a, 8:16], head_less[:, a, :])
                e.drain()
                for a in range(2):
                    e.max_index(top_ix[:, a, 8:16], top[:, a, 8:16], head_less[:, a, :])
                e.tensor_tensor(cand.rearrange("p (i j) -> p i j", i=TOPK),
                                top[:, 0, :].unsqueeze(2).broadcast_to([P, TOPK, TOPK]),
                                top[:, 1, :].unsqueeze(1).broadcast_to([P, TOPK, TOPK]), ALU.add)
                e.drain()

            def top_pairs(par_):
                e.tensor_copy(top_ixf[:, :, :], top_ix[:, :, :])
                e.max(best[:, par_, 0:8], cand)
                e.drain()
                e.max_index(pos[:, 0:8], best[:, par_, 0:8], cand)
                e.match_replace(cand_less, best[:, par_, 0:8], cand, LOWEST)
                e.tensor_scalar(best_neg[:, par_:par_ + 1], best[:, par_, 0:1], -1.0, None, ALU.mult)
                e.drain()

            def top_pairs_second(par_):
                e.max(best[:, par_, 8:16], cand_less).then_inc(best_ready, 1)
                e.drain()
                e.max_index(pos[:, 8:16], best[:, par_, 8:16], cand_less)
                e.drain()
                e.tensor_single_scalar(pos_ab[:, 0, :], pos[:, :], 4, ALU.logical_shift_right)
                e.tensor_single_scalar(pos_ab[:, 1, :], pos[:, :], TOPK - 1, ALU.bitwise_and)
                e.drain()

            def top_lookup():
                iota = const("iota").unsqueeze(1).unsqueeze(1).broadcast_to([P, 2, TOPK, TOPK])
                e.tensor_tensor(pick[:, :, :, :], pos_ab[:, :, :].unsqueeze(3).broadcast_to([P, 2, TOPK, TOPK]), iota,
                                ALU.is_equal)
                e.drain()
                e.tensor_tensor(pick[:, :, :, :], pick[:, :, :, :],
                                top_ixf[:, :, :].unsqueeze(2).broadcast_to([P, 2, TOPK, TOPK]), ALU.mult)
                e.drain()

            def top_experts(par_):
                e.tensor_reduce(chosen[:, :, :], pick[:, :, :, :], AX, ALU.add)
                e.drain()
                e.scalar_tensor_tensor(chosen[:, 0, :], chosen[:, 0, :], float(NK), chosen[:, 1, :], ALU.mult, ALU.add)
                e.drain()
                e.tensor_scalar(expert[:, par_, :], chosen[:, 0, :], base[:, :], None, ALU.add) \
                    .then_inc(expert_ready, 1)

            def head_gates(l, i, par_):
                e.wait_ge(gate_exp, l * TOPS + i + 1)
                e.reciprocal(gate_r[:, par_:par_ + 1], gate_s[:, par_:par_ + 1])
                e.drain()
                e.tensor_scalar(gate[:, par_, :], gate_e[:, par_, :], gate_r[:, par_:par_ + 1], None, ALU.mult) \
                    .then_inc(gate_ready, 1)

            def rotation_angles():
                e.wait_ge(consts_in_s, 16)
                e.wait_ge(pos_in_s, 16)
                e.tensor_copy(pos_f[:, :], pos_i[:, :])
                e.drain()
                e.tensor_tensor(ang[:, 0, :, :], pos_f[:, :].unsqueeze(2).broadcast_to([P, NB, HALF]),
                                const("inv").unsqueeze(1).broadcast_to([P, NB, HALF]), ALU.mult)
                e.drain()
                two_pi = 2 * np.pi
                parts, rest = [], two_pi
                for bits in (5, 14, 23):
                    v = np.floor(rest * 2.0 ** bits) / 2.0 ** bits
                    parts.append(float(v))
                    rest -= v
                parts.append(float(rest))
                nearest = 1.5 * 2.0 ** 23
                e.tensor_scalar(ang[:, 1, :, :], ang[:, 0, :, :], 1.0 / two_pi, nearest, ALU.mult, ALU.add)
                e.drain()
                e.tensor_scalar(ang[:, 1, :, :], ang[:, 1, :, :], nearest, None, ALU.subtract)
                e.drain()
                for v in parts:
                    e.scalar_tensor_tensor(ang[:, 0, :, :], ang[:, 1, :, :], -v, ang[:, 0, :, :], ALU.mult, ALU.add)
                    e.drain()
                e.tensor_scalar(ang[:, 3, :, :], ang[:, 0, :, :], 3.1415925, -3.1415925, ALU.min, ALU.max)
                e.drain()
                e.scalar_tensor_tensor(ang[:, 2, :, :], ang[:, 3, :, :], -1.0, ang[:, 3, :, :], ALU.mult, ALU.min)
                e.drain()
                e.tensor_scalar(ang[:, 2, :, :], ang[:, 2, :, :], float(np.pi / 2), None, ALU.add).then_inc(trig_in, 1)

            e.memset(zeros[:, :], 0.0).then_inc(zeros_ready, 1)
            e.memset(half[:, :], -0.5)
            for s in (*proj_out, *tp_out, att_out, acc_free, params_free):
                e.sem_inc(s, 1)
            e.sem_inc(w_lo_ready, SPLITS)
            rotation_angles()
            e.wait_ge(x_in_s, 16)
            e.sem_inc(x_ready, 1)

            with e.Fori(0, L) as l:
                rests(l, 0, 0)
                norm(l, 0).then_inc(xn_ready, 1)
                e.wait_ge(gains_in_s, l * 16 + 16)
                for u in range(4):
                    turn_rest(l, f"nA{u}")
                rests(l, 0, 1)
                for k in (1, 2):
                    rests(l, k, 0)
                    if k == 1:
                        e.wait_ge(params_in_s, l * 16 + 16)
                        lq = par("lam_qk")
                        for i in range(2):
                            e.tensor_tensor_reduce(rot[:, i, 0, 0:64], lq[:, 128 * i:128 * i + 64],
                                                   lq[:, 128 * i + 64:128 * i + 128], 1.0, 0.0, ALU.mult, ALU.add,
                                                   lam[:, i:i + 1])
                        e.drain()
                        e.sem_inc(lam_in, 1)
                    rests(l, k, 1)
                rests(l, 3, 0)
                e.wait_ge(trig_done, 1)
                wait_proj_out(e, l, "z10")
                wait_proj_out(e, l, "z11")
                heads = [z[:, b, 0:1024].rearrange("p (h d) -> p h d", d=DA_DIM) for b in range(NB)]
                r = [rot[:, k, :, :].rearrange("p b (h d) -> p b h d", d=HALF) for k in range(4)]
                for b in range(NB):
                    for k, (a, t) in enumerate(((0, 0), (HALF, 1), (0, 1), (HALF, 0))):
                        e.tensor_tensor(r[k][:, b], heads[b][:, :, a:a + HALF],
                                        trig[:, t, b, :].unsqueeze(1).broadcast_to([P, 16, HALF]), ALU.mult)
                e.drain()
                for b in range(NB):
                    e.tensor_tensor(heads[b][:, :, 0:HALF], r[0][:, b], r[1][:, b], ALU.subtract)
                    ins = e.tensor_tensor(heads[b][:, :, HALF:ROT], r[2][:, b], r[3][:, b], ALU.add)
                ins.then_inc(rope_ready, 1)
                rests(l, 3, 1)
                for k in (4, 5):
                    for half_ in range(2):
                        rests(l, k, half_)
                rests(l, GATE_PANEL, 0)
                turn_out(l, "qk0", qkT[:, 0, 0:2, :])
                turn_out(l, "qk2", qkT[:, 1, 0:2, :])
                wait_proj_out(e, l, "z50")
                wait_proj_out(e, l, "z51")
                e.wait_ge(wide_in_s, 16)
                for b in range(NB):
                    e.bn_stats(bn[:, b, :], z[:, b, 2560:3072])
                e.drain()
                for b in range(NB):
                    e.bn_aggr(mv[:, b, :], bn[:, b, :])
                e.drain()
                e.tensor_scalar(var[:, 3, 0:2], mv[:, :, 1], EPS, None, ALU.add).then_inc(var_ready, 1)
                e.wait_ge(lam_exp, l + 1)
                e.tensor_tensor(lam[:, 0:1], lam[:, 3:4], lam[:, 2:3], ALU.subtract)
                e.drain()
                e.tensor_tensor(lam[:, 0:1], lam[:, 0:1], par("lam_init"), ALU.subtract)
                masked_max(l, 0)
                rests(l, GATE_PANEL, 1)
                difference(l, 0)
                rests(l, GATE_PANEL + 1, 0)
                masked_max(l, 1)
                wait_tp_done(e, l, "a0")
                e.tensor_copy(aT[:, 0, 0:2, 0, :], tbank("a0")[:, 0:256].rearrange("p (h q) -> p h q", h=2)) \
                    .then_inc(tfreed("a0"), 1)
                rests(l, GATE_PANEL + 1, 1)
                difference(l, 1)
                e.wait_ge(rstd_ready, l * ROOTS + 2)
                for b in range(NB):
                    e.tensor_scalar(z[:, b, 2560:3072], z[:, b, 2560:3072], mv[:, b, 0:1], rstd[:, 3, b:b + 1],
                                    ALU.subtract, ALU.mult)
                e.drain()
                for b in range(NB):
                    e.tensor_tensor(z[:, b, 2560:3072], z[:, b, 2560:3072], par("sg_ln_g"), ALU.mult)
                rests(l, GATE_PANEL + 2, 0)
                masked_max(l, 2)
                for b in range(NB):
                    e.tensor_tensor(z[:, b, 2560:3072], z[:, b, 2560:3072], par("sg_ln_b"), ALU.add)
                e.tensor_tensor(w_spatialT, w_spatialT, const("triu").unsqueeze(1).broadcast_to([P, 4, P]),
                                ALU.mult).then_inc(vn_ready, 1)
                rests(l, GATE_PANEL + 2, 1)
                difference(l, 2)
                rests(l, GATE_PANEL + 3, 0)
                masked_max(l, 3)
                wait_tp_done(e, l, "a2")
                e.tensor_copy(aT[:, 1, 0:2, :, :].rearrange("p h k q -> p (h k q)"), tbank("a2")[:, :]) \
                    .then_inc(tfreed("a2"), 1)
                rests(l, GATE_PANEL + 3, 1)
                difference(l, 3)
                rests(l, GATE_PANEL + 4, 0)
                for b in range(NB):
                    wait_proj_done(e, l, f"sm{b}")
                    for g in range(4):
                        ins = e.scalar_tensor_tensor(xn[:, b, BW + g * P:BW + (g + 1) * P],
                                                     bank(f"sm{b}")[:, g * P:(g + 1) * P],
                                                     par("b_spatial")[:, g:g + 1],
                                                     z[:, b, 2048 + g * P:2048 + (g + 1) * P], ALU.add, ALU.mult)
                    ins.then_inc(freed(f"sm{b}"), 1)
                rests(l, GATE_PANEL + 4, 1)

                def head_squares(b):
                    wait_proj_out(e, l, f"av{b}")
                    if b == 0:
                        wait_tp_done(e, l, "a3")
                    e.tensor_tensor(gated[:, b, :], xn[:, b, 0:BW], xn[:, b, 0:BW], ALU.mult)
                    e.drain()
                    e.tensor_reduce(var[:, 4, 4 * b:4 * b + 4], gated[:, b, :].rearrange("p (h d) -> p h d", h=4), AX,
                                    ALU.add)

                head_squares(0)
                rests(l, GATE_PANEL + 5, 0)
                turn_rest(l, "py0")
                turn_rest(l, "py1")
                rests(l, GATE_PANEL + 5, 1)
                head_squares(1)
                e.drain()
                e.tensor_scalar(var[:, 4, :], var[:, 4, :], 1.0 / P, EPS, ALU.mult, ALU.add).then_inc(var_ready, 1)
                rests(l, BRANCH_PANEL, 0)
                turn_rest(l, "s0")
                turn_rest(l, "s1")
                e.wait_ge(rstd_ready, l * ROOTS + 3)
                e.tensor_scalar(rstd[:, 4, :], rstd[:, 4, :], par("one_less"), None, ALU.mult)
                e.drain()
                heads_o = [xn[:, b, 0:BW].rearrange("p (h d) -> p h d", h=4) for b in range(NB)]
                for b in range(NB):
                    e.tensor_tensor(heads_o[b], heads_o[b],
                                    rstd[:, 4, 4 * b:4 * b + 4].unsqueeze(2).broadcast_to([P, 4, P]), ALU.mult)
                e.drain()
                rests(l, BRANCH_PANEL, 1)
                for b in range(NB):
                    ins = e.tensor_tensor(heads_o[b], heads_o[b],
                                          par("subln_g").unsqueeze(1).broadcast_to([P, 4, P]), ALU.mult)
                ins.then_inc(on_ready, 1)
                n0, n1, n2 = BRANCH_ORDER
                merge(l, n0, 0)
                e.wait_ge(mem_sq_ready, l + 1)
                e.tensor_scalar(var[:, 5, 0:2], mem_sq[:, :], 1.0 / D, EPS, ALU.mult, ALU.add).then_inc(var_ready, 1)
                rests(l, BRANCH_PANEL + 1, 0)
                merge(l, n0, 1)
                e.wait_ge(mem_in_s, l * 16 + 16)
                e.wait_ge(rstd_ready, l * ROOTS + 4)
                for b in range(NB):
                    ins = e.tensor_scalar(mem_rows[:, b, :], mem_rows[:, b, :], rstd[:, 5, b:b + 1], None, ALU.mult)
                ins.then_inc(mem_ready, 1)
                rests(l, BRANCH_PANEL + 1, 1)
                merge(l, n1, 0)
                turn_rest(l, "o0")
                turn_rest(l, "o1")
                rests(l, BRANCH_PANEL + 2, 0)
                merge(l, n1, 1)
                rests(l, BRANCH_PANEL + 2, 1)
                merge(l, n2, 0)
                rests(l, OUT_PANEL, 0)
                merge(l, n2, 1)
                for u in range(4):
                    turn_rest(l, f"mT{u}")
                for u in range(4):
                    turn_rest(l, f"m{u}")
                rests(l, OUT_PANEL, 1)
                rests(l, OUT_PANEL + 1, 0)
                for b in range(NB):
                    add_rows(l, f"wo{b}", b, 0).then_inc(freed(f"wo{b}"), 1)
                rests(l, OUT_PANEL + 1, 1)
                rests(l, K_PANEL, 0)
                for b in range(NB):
                    add_rows(l, f"wo{2 + b}", b, 1).then_inc(freed(f"wo{2 + b}"), 1)
                e.drain()
                e.sem_inc(x_ready, 1)
                norm(l, 1).then_inc(xn_ready, 1)
                rests(l, K_PANEL, 1)
                rests(l, K_PANEL + 1, 0)
                rests(l, K_PANEL + 1, 1)
                rests(l, XQ_PANEL, 0)
                for u in range(4):
                    turn_rest(l, f"nC{u}")
                rests(l, XQ_PANEL, 1)
                rests(l, XQ_PANEL + 1, 0)
                rests(l, XQ_PANEL + 1, 1)
                rests(l, V_PANEL, 0)
                cross_max(l, 0)
                rests(l, V_PANEL, 1)
                cross_probs(l, 0)
                rests(l, V_PANEL + 1, 0)
                cross_max(l, 1)
                rests(l, V_PANEL + 1, 1)
                cross_probs(l, 1)
                rests(l, XO_PANEL, 0)
                for u in (0, 2):
                    wait_tp_done(e, l, f"e{u}")
                    b = u // 2
                    e.tensor_copy(eT[:, 0:2, :, b * P:(b + 1) * P],
                                  tbank(f"e{u}")[:, :].rearrange("p (h m t) -> p h m t", h=2, m=NB)) \
                        .then_inc(tfreed(f"e{u}"), 1)
                for u in range(4):
                    turn_rest(l, f"co{u}")
                rests(l, XO_PANEL, 1)
                rests(l, XO_PANEL + 1, 0)
                for b in range(NB):
                    add_rows(l, f"xo{b}", b, 0).then_inc(freed(f"xo{b}"), 1)
                rests(l, XO_PANEL + 1, 1)
                rests(l, PQ_PANEL, 0)
                for b in range(NB):
                    add_rows(l, f"xo{2 + b}", b, 1).then_inc(freed(f"xo{2 + b}"), 1)
                e.drain()
                e.sem_inc(x_ready, 1)
                norm(l, 2).then_inc(xn_ready, 1)
                for u in range(4):
                    turn_rest(l, f"nF{u}")
                rests(l, PQ_PANEL, 1)
                rests(l, PQ_PANEL + 1, 0, 5)
                wait_proj_out(e, l, "sc0")
                top_halves(0)
                rests(l, PQ_PANEL + 1, 5, 7)
                top_halves_rest()
                rests(l, PQ_PANEL + 1, 7, 8)
                rests(l, PQ_PANEL + 2, 0, 2)
                top_halves_second()
                rests(l, PQ_PANEL + 2, 2, 4)
                top_pairs(0)
                rests(l, PQ_PANEL + 2, 4, 6)
                top_pairs_second(0)
                e.tensor_copy(base[:, :], const("expert_base")[:, ds(l, 1)])
                rests(l, PQ_PANEL + 2, 6, 8)
                top_lookup()
                top_experts(0)
                rests(l, PQ_PANEL + 3, 0, 8)
                head_gates(l, 0, 0)
                for b in range(NB):
                    e.tensor_tensor(xn[:, b, :], xn[:, b, :], par("g_ffn_row"), ALU.mult)
                e.memset(scores[:, STEPS:TOPS, :], 0.0)
                e.drain()
                e.sem_inc(params_free, 1)
                with e.Fori(0, NB) as b:
                    e.tensor_copy(x_now.unsqueeze(1), xn[:, ds(b, 1), :])
                    e.drain()
                    with e.Fori(0, HEADS // 2) as hh:
                        for s in range(2):
                            i = b * HEADS + hh * 2 + s
                            for j in range(TOPK):
                                e.drain()
                                e.wait_ge(got[j % SLOTS], ((l * STEPS + i) * (TOPK // SLOTS) + j // SLOTS + 1) * 16)
                                ins = e.tensor_tensor_reduce(products, x_now, tiles[j % SLOTS][:, 0:D], 1.0, 0.0,
                                                             ALU.mult, ALU.add, dots[:, s, j:j + 1])
                                if j % GROUP == GROUP - 1:
                                    ins.then_inc(dots_ready, 1)
                                if j == 0:
                                    if s == 1:
                                        wait_proj_out(e, l, "sc7")
                                        e.nop(nofuse=True)
                                    top_halves(i + 1)
                                if j == 1:
                                    top_halves_rest()
                                if j == 2:
                                    top_halves_second()
                                if j == 3:
                                    top_pairs(1 - s)
                                if j == 4:
                                    top_pairs_second(1 - s)
                                if j == 5:
                                    top_lookup()
                                if j == 6:
                                    top_experts(1 - s)
                                if j == 14:
                                    head_gates(l, i + 1, 1 - s)
                    e.wait_ge(tile_used, SLOTS + l * TILES + b * (TILES // NB) + TILES // NB)
                    e.tensor_tensor(x[:, ds(b, 1), :], x[:, ds(b, 1), :], pair[:, :].unsqueeze(1), ALU.add)
                    e.drain()
                    e.sem_inc(x_ready, 1)
                    e.sem_inc(acc_free, 1)

            norm(L, 0)
            e.drain()
            e.wait_ge(params_in_s, L * 16 + 16)
            for b in range(NB):
                ins = e.tensor_tensor(xn[:, b, :], xn[:, b, :], params[:, 0:D], ALU.mult)
            ins.then_inc(xn_ready, 1)

        @block.scalar
        def _(e):
            def square(l, r):
                e.wait_ge(x_ready, l * 4 + r + 1)
                e.activation(xn[:, 1, :], x[:, 1, :], ACT.Square, accum_out=sq[:, 1:2]).then_inc(sq_ready, 1)

            def out_unit(l, unit, dst, func=ACT.Copy, scale=1.0):
                wait_proj_done(e, l, unit)
                e.activation(dst, bank(unit)[:, :], func, scale=scale).then_inc(freed(unit), 1)

            def highs(l, k, part, end=None):
                for i in range(part, end) if end else (range(0, AHEAD), range(AHEAD, PIECES))[part]:
                    n = k * PIECES + i
                    if i == 0:
                        wait_panel(e, l, k)
                    e.wait_ge(piece_started, l * SPLITS + n + 1)
                    e.activation(w_hi[:, n % WSLOTS, :], panels[:, k % PSLOTS, i * PIECE:(i + 1) * PIECE],
                                 ACT.Copy).then_inc(w_hi_ready, 1)

            def turn_high(l, unit):
                ps, _free = source(e, l, unit)
                hi, _lo = turned(unit)
                g = gains(unit)
                if isinstance(g, list):
                    for k in range(2):
                        ins = e.activation(hi[:, k, :], ps[:, k * T:(k + 1) * T], ACT.Copy, scale=g[k])
                else:
                    ins = e.activation(hi.rearrange("p c t -> p (c t)"), ps[:, :], ACT.Copy,
                                       scale=1.0 if g is None else g)
                ins.then_inc(hi_ready, 1)

            def turn_out(l, unit, dst):
                wait_tp_done(e, l, unit)
                e.activation(dst.rearrange("p c t -> p (c t)"), tbank(unit)[:, :], ACT.Copy) \
                    .then_inc(tfreed(unit), 1)

            def gates_out(l, k):
                for b in range(NB):
                    out_unit(l, f"g{k}{b}", gates[:, b, k * BW:(k + 1) * BW], ACT.Tanh, 0.5)

            def exps(l, u):
                n = P * (u // 2 + 1)
                e.wait_ge(max_ready, l * 6 + u + 1)
                for i in range(4):
                    ins = e.activation(probs[:, u % 2, i, 0:n], probs[:, u % 2, i, 0:n], ACT.Exp,
                                       bias=neg_max[:, u % 2, i:i + 1], accum_out=row_sum[:, u % 2, i:i + 1])
                ins.then_inc(exp_done, 1)

            def gate_exps(l, i, par_):
                e.wait_ge(best_ready, l * TOPS + i + 1)
                e.activation(gate_e[:, par_, :], best[:, par_, :], ACT.Exp, bias=best_neg[:, par_:par_ + 1],
                             accum_out=gate_s[:, par_:par_ + 1]).then_inc(gate_exp, 1)

            e.wait_ge(trig_in, 1)
            e.activation(trig[:, 0, :, :], ang[:, 2, :, :], ACT.Sin)
            e.activation(trig[:, 1, :, :], ang[:, 3, :, :], ACT.Sin).then_inc(trig_done, 1)
            e.dma_start(consts[:, SMALL_CONSTS:CONST_COLS], consts_in[:, SMALL_CONSTS:CONST_COLS]) \
                .then_inc(wide_in_s, 16)
            e.wait_ge(consts_in_s, 16)

            with e.Fori(0, L) as l:
                highs(l, 0, 0)
                square(l, 0)
                e.wait_ge(gains_in_s, l * 16 + 16)
                for u in range(4):
                    turn_high(l, f"nA{u}")
                highs(l, 0, 1)

                def z_out(k):
                    for b in range(NB):
                        out_unit(l, f"z{k}{b}", z[:, b, k * BW:(k + 1) * BW])

                for k in range(1, 6):
                    highs(l, k, 0)
                    z_out(k - 1)
                    highs(l, k, 1)
                highs(l, GATE_PANEL, 0)
                z_out(5)
                e.wait_ge(lam_in, l + 1)
                e.activation(lam[:, 2:4], lam[:, 0:2], ACT.Exp).then_inc(lam_exp, 1)
                turn_out(l, "qk1", qkT[:, 0, 2:4, :])
                turn_out(l, "qk3", qkT[:, 1, 2:4, :])
                exps(l, 0)
                for u in range(2):
                    out_unit(l, f"pd{u}", poolT[:, 2 * u:2 * u + 2, :].rearrange("p c t -> p (c t)"))
                highs(l, GATE_PANEL, 1)
                highs(l, GATE_PANEL + 1, 0)
                gates_out(l, 0)
                exps(l, 1)
                highs(l, GATE_PANEL + 1, 1)
                highs(l, GATE_PANEL + 2, 0)
                gates_out(l, 1)
                wait_tp_done(e, l, "a1")
                e.activation(aT[:, 0, 2:4, 0, :], tbank("a1")[:, 0:256].rearrange("p (h q) -> p h q", h=2), ACT.Copy) \
                    .then_inc(tfreed("a1"), 1)
                exps(l, 2)
                highs(l, GATE_PANEL + 2, 1)
                highs(l, GATE_PANEL + 3, 0)
                gates_out(l, 2)
                out_unit(l, "av0", xn[:, 0, 0:BW])
                exps(l, 3)
                highs(l, GATE_PANEL + 3, 1)
                highs(l, GATE_PANEL + 4, 0)
                gates_out(l, 3)
                wait_tp_done(e, l, "a3")
                e.activation(aT[:, 1, 2:4, :, :].rearrange("p h k q -> p (h k q)"), tbank("a3")[:, :], ACT.Copy) \
                    .then_inc(tfreed("a3"), 1)
                highs(l, GATE_PANEL + 4, 1)
                highs(l, GATE_PANEL + 5, 0)
                gates_out(l, 4)
                out_unit(l, "av1", xn[:, 1, 0:BW])
                turn_high(l, "py0")
                turn_high(l, "py1")
                highs(l, GATE_PANEL + 5, 1)
                highs(l, BRANCH_PANEL, 0)
                gates_out(l, 5)
                turn_high(l, "s0")
                turn_high(l, "s1")
                highs(l, BRANCH_PANEL, 1)
                highs(l, BRANCH_PANEL + 1, 0)
                e.wait_ge(mem_in_s, l * 16 + 16)
                for b in range(NB):
                    e.activation(z[:, 0, 0:D], mem_rows[:, b, :], ACT.Square, accum_out=mem_sq[:, b:b + 1])
                    e.drain()
                e.sem_inc(mem_sq_ready, 1)
                highs(l, BRANCH_PANEL + 1, 1)
                highs(l, BRANCH_PANEL + 2, 0)
                turn_high(l, "o0")
                turn_high(l, "o1")
                highs(l, BRANCH_PANEL + 2, 1)
                highs(l, OUT_PANEL, 0)
                for u in range(4):
                    turn_high(l, f"mT{u}")
                for u in range(4):
                    turn_high(l, f"m{u}")
                highs(l, OUT_PANEL, 1)
                highs(l, OUT_PANEL + 1, 0)
                highs(l, OUT_PANEL + 1, 1)
                highs(l, K_PANEL, 0)
                square(l, 1)
                highs(l, K_PANEL, 1)

                def columns_out(kind, i, dst):
                    out_unit(l, f"{kind}{i}", dst[:, 2 * i:2 * i + 2, :].rearrange("p c t -> p (c t)"))

                def values_out(i):
                    out_unit(l, f"vm{i}", vm[:, i % 2, (i // 2) * BW:(i // 2 + 1) * BW])

                highs(l, K_PANEL + 1, 0)
                columns_out("km", 0, kmT)
                columns_out("km", 1, kmT)
                highs(l, K_PANEL + 1, 1)
                highs(l, XQ_PANEL, 0)
                columns_out("km", 2, kmT)
                columns_out("km", 3, kmT)
                for u in range(4):
                    turn_high(l, f"nC{u}")
                highs(l, XQ_PANEL, 1)
                highs(l, XQ_PANEL + 1, 0)
                columns_out("xq", 0, xqT)
                columns_out("xq", 1, xqT)
                highs(l, XQ_PANEL + 1, 1)
                highs(l, V_PANEL, 0)
                columns_out("xq", 2, xqT)
                columns_out("xq", 3, xqT)
                highs(l, V_PANEL, 1)

                def cross_exps(b):
                    e.wait_ge(max_ready, l * 6 + 4 + b + 1)
                    for h in range(X_HEADS):
                        ins = e.activation(probs[:, b, h, :], pair[:, h * T:(h + 1) * T], ACT.Exp,
                                           bias=neg_max[:, b, h:h + 1], scale=X_SCALE,
                                           accum_out=row_sum[:, b, h:h + 1])
                    ins.then_inc(exp_done, 1)
                    e.drain()
                    e.sem_inc(att_out, 1)

                cross_exps(0)
                highs(l, V_PANEL + 1, 0)
                values_out(0)
                values_out(1)
                highs(l, V_PANEL + 1, 1)
                cross_exps(1)
                highs(l, XO_PANEL, 0)
                values_out(2)
                values_out(3)
                for u in (1, 3):
                    wait_tp_done(e, l, f"e{u}")
                    b = u // 2
                    e.activation(eT[:, 2:4, :, b * P:(b + 1) * P],
                                 tbank(f"e{u}")[:, :].rearrange("p (h m t) -> p h m t", h=2, m=NB), ACT.Copy) \
                        .then_inc(tfreed(f"e{u}"), 1)
                for u in range(4):
                    turn_high(l, f"co{u}")
                highs(l, XO_PANEL, 1)
                highs(l, XO_PANEL + 1, 0)
                highs(l, XO_PANEL + 1, 1)
                highs(l, PQ_PANEL, 0)
                square(l, 2)
                for u in range(4):
                    turn_high(l, f"nF{u}")
                highs(l, PQ_PANEL, 1)
                def scores_out(i):
                    out_unit(l, f"sc{i}", scores[:, 2 * i:2 * i + 2, :].rearrange("p h n -> p (h n)"))

                highs(l, PQ_PANEL + 1, 0)
                columns_out("pq", 0, peer_qT)
                columns_out("pq", 1, peer_qT)
                highs(l, PQ_PANEL + 1, AHEAD, AHEAD + 2)
                scores_out(0)
                scores_out(4)
                highs(l, PQ_PANEL + 1, AHEAD + 2, PIECES)
                highs(l, PQ_PANEL + 2, 0)
                columns_out("pq", 2, peer_qT)
                columns_out("pq", 3, peer_qT)
                highs(l, PQ_PANEL + 2, 1)
                highs(l, PQ_PANEL + 3, 0)
                columns_out("pq", 4, peer_qT)
                columns_out("pq", 5, peer_qT)
                highs(l, PQ_PANEL + 3, 1)
                gate_exps(l, 0, 0)
                columns_out("pq", 6, peer_qT)
                columns_out("pq", 7, peer_qT)
                for i in LATE_SCORES:
                    scores_out(i)
                with e.Fori(0, NB) as b:
                    with e.Fori(0, HEADS // 2) as hh:
                        for s in range(2):
                            i = b * HEADS + hh * 2 + s
                            e.wait_ge(gate_ready, l * TOPS + i + 1)
                            for g in range(TOPK // GROUP):
                                e.wait_ge(dots_ready, (l * STEPS + i) * (TOPK // GROUP) + g + 1)
                                e.activation(gelu[:, s, GROUP * g:GROUP * (g + 1)],
                                             dots[:, s, GROUP * g:GROUP * (g + 1)], ACT.Gelu)
                                e.drain()
                                for j in range(GROUP * g, GROUP * (g + 1)):
                                    e.activation(weight[:, s, j:j + 1], gelu[:, s, j:j + 1], ACT.Copy,
                                                 scale=gate[:, s, j:j + 1])
                                e.drain()
                                for j in range(GROUP * g, GROUP * (g + 1)):
                                    e.wait_ge(tile_used, (l * STEPS + i) * TOPK + j + 1)
                                    e.activation(diag[:, j % SLOTS, :], ident, ACT.Copy,
                                                 scale=weight[:, s, j:j + 1]).then_inc(diag_ready, 1)
                                if g == TOPK // GROUP - 3:
                                    gate_exps(l, i + 1, 1 - s)
            square(L, 0)

        @block.gpsimd
        def _(e):
            def root(k, r, n):
                e.wait_ge(var_ready, k)
                e.tensor_tensor(rstd[:, r, 0:n], var[:, r, 0:n], half[:, 0:n], ALU.pow).then_inc(rstd_ready, 1)

            with e.Fori(0, L) as l:
                for k, (r, n) in enumerate(((0, 2), (3, 2), (4, 8), (5, 2), (1, 2), (2, 2))):
                    root(l * ROOTS + k + 1, r, n)
                with e.Fori(0, NB) as b:
                    with e.Fori(0, HEADS // 2) as hh:
                        for s in range(2):
                            i = b * HEADS + hh * 2 + s
                            e.wait_ge(expert_ready, l * TOPS + i + 1)
                            e.nop(nofuse=True)
                            for j in range(TOPK):
                                e.wait_ge(tile_used, (l * STEPS + i) * TOPK + j + 1)
                                if s == 0 and j == 5:
                                    wait_proj_done(e, l, "pq7")
                                if s == 0 and j == 7:
                                    wait_proj_done(e, l, "sc7")
                                e.nop(nofuse=True)
                                e.indirect_dma_start(tiles[j % SLOTS], None, experts,
                                                     bass.IndirectOffsetOnAxis(expert[:, s, j:j + 1], 0)) \
                                    .then_inc(got[j % SLOTS], 16)
            root(L * ROOTS + 1, 0, 2)


def _constants():
    c = np.zeros((P, CONST_COLS), np.float32)

    def put(name, v):
        c[:, CONSTS[name][0]:CONSTS[name][1]] = v

    put("ident", np.eye(P))
    q, k = np.arange(P)[:, None], np.arange(P)[None, :]
    put("mask", np.concatenate([np.zeros((P, P)), np.where(k <= q, 0.0, MASKED)], 1))
    put("triu", q <= k)
    s, t = np.arange(T)[:, None], np.arange(T)[None, :]
    cols = []
    for w in WINDOWS:
        m = ((s <= t) & (s > t - w)) / np.minimum(t + 1, w) - (s == t)
        cols.append(np.concatenate([m[0:P, :], m[P:T, P:T]], 1))
    put("pool", np.concatenate(cols, 1))
    put("iota", np.arange(TOPK)[None, :])
    put("inv", (np.float32(ROPE_THETA) ** (-np.arange(0, ROT, 2, dtype=np.float32) / np.float32(ROT)))[None, :])
    put("expert_base", (np.arange(L) * NK * NK)[None, :])
    return c


def _panels(w):
    rows, cols = w.shape
    chunks = rows // P
    width = PANEL // chunks
    return w.reshape(chunks, P, cols // width, width).transpose(2, 1, 0, 3).reshape(cols // width, P, PANEL)


def _stream(a, l):
    branch = [a["w_branch"][l, n].reshape(4, P, 2, BW).transpose(1, 2, 0, 3).reshape(1, P, PANEL)
              for n in BRANCH_ORDER]
    kv = _panels(a["w_xkv"][l])
    return np.concatenate([_panels(a["w_in"][l]), *branch, _panels(a["w_out"][l]), kv[0:2], _panels(a["w_xq"][l]),
                           kv[2:4], _panels(a["w_xo"][l]), _panels(a["w_pq"][l].reshape(D, -1))])


def _params(a, l):
    p = np.zeros((P, PARAM_COLS), np.float32)

    def put(name, v):
        p[:, PARAMS[name][0]:PARAMS[name][1]] = v

    for name in ("g_mix", "g_cross", "g_mem", "g_ffn"):
        put(name, a[name][l].reshape(KC, P).T)
    put("pool_scale", a["pool_scale"][l].reshape(4, P).T)
    put("b_spatial", a["b_spatial"][l].T)
    start = 0.8 - 0.6 * np.exp(-0.3 * l)
    put("lam_init", start)
    put("one_less", 1.0 - start)
    put("lam_qk", a["lam_qk"][l].reshape(1, -1))
    for name in ("subln_g", "sg_ln_g", "sg_ln_b"):
        put(name, a[name][l][None, :])
    put("g_ffn_row", a["g_ffn"][l][None, :])
    put("w_spatial", a["w_spatial"][l].transpose(2, 0, 1).reshape(P, -1))
    put("w_pool", a["w_pool"][l].transpose(1, 0, 2).reshape(P, -1))
    return p


def kernel(**inputs):
    import concourse.bacc as _bacc
    from concourse.bass_utils import run_bass_kernel_spmd as _run

    a = {k: np.asarray(v) for k, v in inputs.items()}
    arrays = {
        "x_in": a["x"],
        "mem_in": a["mem"],
        "pos_in": a["positions"],
        "stream": np.concatenate([_stream(a, l) for l in range(L)]),
        "keys_in": np.stack([k.transpose(3, 0, 1, 2).reshape(P, 2 * HEADS * NK) for k in a["sub_keys"]]),
        "params_in": np.stack([_params(a, l) for l in range(L)]),
        "consts_in": _constants(),
        "g_final": np.broadcast_to(a["g_final"][None, :], (P, D)),
        "experts": np.concatenate([a["peer_u"], a["peer_v"]], 2).reshape(L * NK * NK, 2 * D),
    }
    arrays = {k: np.ascontiguousarray(v) for k, v in arrays.items()}
    nc = _bacc.Bacc("TRN2", target_bir_lowering=False, num_devices=1)
    args = [nc.dram_tensor(k, v.shape, mybir.dt.from_np(v.dtype), kind="ExternalInput").ap() for k, v in arrays.items()]
    out = nc.dram_tensor("out", a["x"].shape, F32, kind="ExternalOutput").ap()
    trunk(nc, *args, out)
    r = _run(nc, [arrays], core_ids=[0])
    return r.results[0]["out"]
```

```python
from contextlib import ExitStack

import numpy as np

import concourse.bass as bass
from concourse import mybir

F32 = mybir.dt.float32
F32R = mybir.dt.float32r
BF16 = mybir.dt.bfloat16
I32 = mybir.dt.int32
U32 = mybir.dt.uint32
ALU = mybir.AluOpType
ACT = mybir.ActivationFunctionType
AX = mybir.AxisListType.X
ds = bass.ds

P = 128
L = 2
D = 1024
T = 256
NB = T // P
KC = D // P
EPS = 1e-6
DA_HEADS = 4
DA_DIM = 64
ROT = 16
HALF = ROT // 2
ROPE_THETA = 500000.0
WINDOWS = (2, 4, 8, 16)
X_HEADS = 4
X_SCALE = float(D // X_HEADS) ** -0.5
DA_SCALE = float(DA_DIM) ** -0.5
HEADS = 8
NK = 128
TOPK = 16
BW = 512
MASKED = -1e30
LOWEST = -3e38

PANEL = 4096
Z_PANEL, GATE_PANEL, BRANCH_PANEL, OUT_PANEL, K_PANEL, XQ_PANEL, V_PANEL, XO_PANEL, PQ_PANEL = \
    0, 6, 12, 15, 17, 19, 21, 23, 25
PANELS = 29
PSLOTS = 2
PIECE = 512
PIECES = PANEL // PIECE
SPLITS = PANELS * PIECES
WSLOTS = 4
AHEAD = WSLOTS - 1
BRANCH_ORDER = (1, 2, 0)

PARAMS = {}
_at = 0
for _name, _n in (("g_mix", 8), ("g_cross", 8), ("g_mem", 8), ("g_ffn", 8), ("pool_scale", 4), ("b_spatial", 4),
                  ("lam_init", 1), ("one_less", 1), ("lam_qk", 256), ("subln_g", 128), ("sg_ln_g", 512),
                  ("sg_ln_b", 512), ("g_ffn_row", 1024), ("w_spatial", 512), ("w_pool", 512)):
    PARAMS[_name] = (_at, _at + _n)
    _at += _n
PARAM_COLS = _at
GAIN_COLS = PARAMS["lam_qk"][0]

CONSTS = {}
_at = 0
for _name, _n in (("ident", 128), ("iota", 16), ("inv", 8), ("expert_base", L), ("mask", 256),
                  ("pool", 4 * 384), ("triu", 128)):
    CONSTS[_name] = (_at, _at + _n)
    _at += _n
CONST_COLS = _at
SMALL_CONSTS = CONSTS["mask"][0]

PROJ = ([f"z{p}{b}" for p in range(6) for b in range(2)]
        + ["pd0", "pd1", "g00", "g01", "g10", "g11", "g20", "g21", "av0", "sm0", "sm1", "g30", "g31", "g40", "g41",
           "av1", "py0", "py1", "g50", "g51"]
        + [f"br{n}{h}{b}" for n in BRANCH_ORDER for h in range(2) for b in range(2)]
        + [f"wo{i}" for i in range(4)] + [f"km{i}" for i in range(4)] + [f"xq{i}" for i in range(4)]
        + [f"vm{i}" for i in range(4)] + [f"co{i}" for i in range(4)] + [f"xo{i}" for i in range(4)]
        + [f"{kind}{i}" for q in range(4) for kind, i in (("pq", 2 * q), ("pq", 2 * q + 1), ("sc", q), ("sc", 4 + q))])
TRANS = [k + str(i) for k, n in (("nA", 4), ("qk", 4), ("a", 4), ("s", 2), ("o", 2), ("mT", 4), ("m", 4),
                                 ("nC", 4), ("e", 4), ("nF", 4)) for i in range(n)]
TURNED = [k + str(i) for k, n in (("nA", 4), ("py", 2), ("s", 2), ("o", 2), ("mT", 4), ("m", 4), ("nC", 4),
                                  ("co", 4), ("nF", 4)) for i in range(n)]
PU, TU, HU = len(PROJ), len(TRANS), len(TURNED)
assert PU % 4 == 0 and TU % 2 == 0

ROOTS = 6
GROUP = 2
SLOTS = 8
STEPS = NB * HEADS
TILES = STEPS * TOPK
TOPS = STEPS + 1


def trunk(nc, x_in, mem_in, pos_in, stream, keys_in, params_in, consts_in, g_final, experts, out):
    ctx = ExitStack()
    with ctx:
        def sb(name, shape, dt=F32):
            return ctx.enter_context(nc.sbuf_tensor(name, shape, dt))

        def sem(name):
            return ctx.enter_context(nc.semaphore(name))

        x = sb("x", [P, NB, D])
        xn = sb("xn", [P, NB, D])
        params = sb("params", [P, PARAM_COLS])
        consts = sb("consts", [P, CONST_COLS])
        panels = sb("panels", [P, PSLOTS, PANEL])

        Z0, G0, W0, A0, S0, B0, END = 0, 6144, 12288, 19456, 23552, 27648, 33792
        base_bytes = nc.sbuf_base
        base_bytes += -base_bytes % 32
        arena = sb("arena", [P, END + 8])
        flat = arena[:, 0:END]

        def split_tensor(name, shape, column):
            return nc.alloc_sbuf_tensor_at(name, shape, F32R, offset=base_bytes + 4 * column)

        act_hi = split_tensor("act_hi", [P, KC, T], A0)
        act_lo = split_tensor("act_lo", [P, KC, T], A0 + 2048)
        w_hi = split_tensor("w_hi", [P, WSLOTS, PIECE], S0)
        w_lo = split_tensor("w_lo", [P, WSLOTS, PIECE], S0 + 2048)
        br_hi = split_tensor("br_hi", [P, 12, T], B0)
        br_lo = split_tensor("br_lo", [P, 12, T], B0 + 3072)

        mem_hi, mem_lo = br_hi[:, 4:12, :], br_lo[:, 4:12, :]

        def cols(start, n):
            return flat[:, start:start + n]

        z = cols(Z0, 6144).rearrange("p (b n) -> p b n", b=NB)
        kmT = cols(Z0, 2048).rearrange("p (c t) -> p c t", c=KC)
        vm = cols(Z0 + 2048, 2048).rearrange("p (b n) -> p b n", b=NB)
        gates = cols(G0, 6144).rearrange("p (b n) -> p b n", b=NB)
        qkT = cols(W0, 2048).rearrange("p (a h t) -> p a h t", a=2, h=4)
        mem_rows = cols(W0, 2048).rearrange("p (b n) -> p b n", b=NB)
        xqT = cols(W0, 2048).rearrange("p (c t) -> p c t", c=KC)
        poolT = cols(W0 + 2048, 1024).rearrange("p (c t) -> p c t", c=4)
        probsT = cols(W0 + 3072, 2048)
        merged = probsT.rearrange("p (b n) -> p b n", b=NB)
        aT = probsT.rearrange("p (b h k q) -> p b h k q", b=NB, h=4, k=NB)
        eT = probsT.rearrange("p (h m t) -> p h m t", h=X_HEADS, m=NB)
        probs = cols(W0 + 5120, 2048).rearrange("p (u i k) -> p u i k", u=2, i=4)
        rot = cols(W0 + 5120, 1024).rearrange("p (k b n) -> p k b n", k=4, b=NB)
        gated = cols(W0 + 5120, 1024).rearrange("p (k n) -> p k n", k=2)
        tiles = [cols(2048 * i, 2048) for i in range(5)] + [cols(A0 + 2048 * i, 2048) for i in range(2)] \
            + [cols(2048 * 5, 2048)]
        keys = cols(2048 * 5, 2048)
        peer_qT = cols(W0, 4096).rearrange("p (h t) -> p h t", h=2 * HEADS)
        products = cols(W0 + 4096, 1024)
        x_now = cols(W0 + 5120, 1024)
        diag = cols(W0 + 6144, 1024).rearrange("p (s n) -> p s n", s=SLOTS)
        scores = cols(B0, 4352).rearrange("p (h n) -> p h n", h=TOPS)
        head_sc = cols(B0 + 4352, 256).rearrange("p (a n) -> p a n", a=2)
        head_less = cols(B0 + 4608, 256).rearrange("p (a n) -> p a n", a=2)
        cand = cols(B0 + 4864, 256)
        cand_less = cols(B0 + 5120, 256)
        pick = cols(B0 + 5376, 512).rearrange("p (a k i) -> p a k i", a=2, k=TOPK)

        zeros = sb("zeros", [P, 512], BF16)
        half = sb("half", [P, 8])
        pos_i = sb("pos_i", [P, NB], I32)
        pos_f = sb("pos_f", [P, NB])
        ang = sb("ang", [P, 4, NB, HALF])
        trig = sb("trig", [P, 2, NB, HALF])
        sq = sb("sq", [P, 2])
        var = sb("var", [P, 6, 8])
        rstd = sb("rstd", [P, 6, 8])
        lam = sb("lam", [P, 4])
        mem_sq = sb("mem_sq", [P, NB])
        cross_scale = sb("cross_scale", [P, NB])
        bn = sb("bn", [P, NB, 6])
        mv = sb("mv", [P, NB, 2])
        neg_max = sb("neg_max", [P, 2, 4])
        row_sum = sb("row_sum", [P, 2, 4])
        row_inv = sb("row_inv", [P, 2, 4])
        top = sb("top", [P, 2, TOPK])
        top_ix = sb("top_ix", [P, 2, TOPK], U32)
        top_ixf = sb("top_ixf", [P, 2, TOPK])
        best = sb("best", [P, 2, TOPK])
        best_neg = sb("best_neg", [P, 2])
        pos = sb("pos", [P, TOPK], U32)
        pos_ab = sb("pos_ab", [P, 2, TOPK], U32)
        chosen = sb("chosen", [P, 2, TOPK])
        expert = sb("expert", [P, 2, TOPK], I32)
        base = sb("base", [P, 1])
        gate_e = sb("gate_e", [P, 2, TOPK])
        gate_s = sb("gate_s", [P, 2])
        gate_r = sb("gate_r", [P, 2])
        gate = sb("gate", [P, 2, TOPK])
        dots = sb("dots", [P, 2, TOPK])
        gelu = sb("gelu", [P, 2, TOPK])
        weight = sb("weight", [P, 2, TOPK])

        def par(name):
            a, b = PARAMS[name]
            return params[:, a:b]

        def const(name):
            a, b = CONSTS[name]
            return consts[:, a:b]

        ident = const("ident")
        pool_m = const("pool").rearrange("p (g n) -> p g n", g=4)
        w_spatialT = par("w_spatial").rearrange("p (g t) -> p g t", g=4)
        w_pool = par("w_pool").rearrange("p (g e) -> p g e", g=4)

        mm = [ctx.enter_context(nc.psum_tensor(f"mm{i}", [P, 512], F32)) for i in range(4)]
        pair = ctx.enter_context(nc.psum_tensor("pair", [P, 1024], F32))
        tp = [ctx.enter_context(nc.psum_tensor(f"tp{i}", [P, 512], F32)) for i in range(2)]

        x_in_s = sem("x_landed")
        pos_in_s = sem("pos_landed")
        consts_in_s = sem("consts_landed")
        wide_in_s = sem("wide_consts_landed")
        gains_in_s = sem("gains_landed")
        params_in_s = sem("params_landed")
        keys_in_s = sem("keys_landed")
        mem_sq_ready = sem("mem_sq_ready")
        params_free = sem("params_free")
        mem_in_s = sem("mem_landed")
        mem_ready = sem("mem_ready")
        w_hi_ready = sem("w_hi_ready")
        w_lo_ready = sem("w_lo_ready")
        piece_started = sem("piece_started")
        hi_ready = sem("hi_ready")
        half_panel_in = sem("half_panel_in")
        panel_in = [sem(f"panel_in{i}") for i in range(PSLOTS)]
        proj_done = sem("proj_done")
        proj_out = [sem(f"proj_out{i}") for i in range(4)]
        tp_done = sem("tp_done")
        tp_out = [sem(f"tp_out{i}") for i in range(2)]
        att_done = sem("att_done")
        att_out = sem("att_out")
        x_ready = sem("x_ready")
        xn_ready = sem("xn_ready")
        sq_ready = sem("sq_ready")
        var_ready = sem("var_ready")
        rstd_ready = sem("rstd_ready")
        trig_in = sem("trig_in")
        trig_done = sem("trig_done")
        lam_in = sem("lam_in")
        lam_exp = sem("lam_exp")
        rope_ready = sem("rope_ready")
        max_ready = sem("max_ready")
        exp_done = sem("exp_done")
        probs_ready = sem("probs_ready")
        vn_ready = sem("vn_ready")
        on_ready = sem("on_ready")
        zeros_ready = sem("zeros_ready")
        got = [sem(f"got{i}") for i in range(SLOTS)]
        tile_used = sem("tile_used")
        expert_ready = sem("expert_ready")
        best_ready = sem("best_ready")
        gate_exp = sem("gate_exp")
        gate_ready = sem("gate_ready")
        dots_ready = sem("dots_ready")
        diag_ready = sem("diag_ready")
        acc_free = sem("acc_free")
        stored = sem("stored")

        def wait_proj_done(e, l, unit):
            e.wait_ge(proj_done, l * PU + (PU + PROJ.index(unit) + 1))

        def wait_proj_out(e, l, unit):
            i = PROJ.index(unit)
            e.wait_ge(proj_out[i % 4], l * (PU // 4) + i // 4 + 2)

        def wait_tp_done(e, l, unit):
            e.wait_ge(tp_done, l * TU + TRANS.index(unit) + 1)

        def wait_tp_out(e, l, unit):
            i = TRANS.index(unit)
            e.wait_ge(tp_out[i % 2], l * (TU // 2) + i // 2 + 2)

        def wait_panel(e, l, k):
            e.wait_ge(panel_in[k % PSLOTS], (l * len(range(k % PSLOTS, PANELS, PSLOTS)) + k // PSLOTS + 1) * 16)

        def turned(unit):
            kind, i = unit[:-1], int(unit[-1])
            hi, lo = (act_hi, act_lo) if kind in ("nA", "m", "nC", "co", "nF") else (br_hi, br_lo)
            c = {"o": 0, "py": 4, "s": 8, "mT": 4}.get(kind, 0) + 2 * i
            return hi[:, c:c + 2, :], lo[:, c:c + 2, :]

        def gains(unit):
            kind, c = unit[:-1], 2 * int(unit[-1])
            name = {"nA": "g_mix", "nC": "g_cross", "nF": "g_ffn", "mT": "g_mem", "py": "pool_scale"}.get(kind)
            if name is None:
                return 0.5 if kind == "m" else None
            return [par(name)[:, c + k:c + k + 1] for k in range(2)]

        def source(e, l, unit):
            if unit in PROJ:
                wait_proj_done(e, l, unit)
                return bank(unit), freed(unit)
            wait_tp_done(e, l, unit)
            return tbank(unit), tfreed(unit)

        def bank(unit):
            return mm[PROJ.index(unit) % 4]

        def tbank(unit):
            return tp[TRANS.index(unit) % 2]

        def freed(unit):
            return proj_out[PROJ.index(unit) % 4]

        def tfreed(unit):
            return tp_out[TRANS.index(unit) % 2]

        block = ctx.enter_context(nc.Block())

        @block.sync
        def _(e):
            e.dma_start(consts[:, 0:SMALL_CONSTS], consts_in[:, 0:SMALL_CONSTS]).then_inc(consts_in_s, 16)
            e.dma_start(pos_i[:, :], pos_in.rearrange("a (b p) -> p (a b)", p=P),
                        allow_slow_non_contiguous=True).then_inc(pos_in_s, 16)
            e.dma_start(x[:, :, :], x_in.rearrange("a (b p) d -> p (a b) d", p=P)).then_inc(x_in_s, 16)

            def load_params(l, a, b, landed):
                e.dma_start(params[:, a:b], params_in[ds(l, 1), :, a:b].rearrange("a p n -> p (a n)")) \
                    .then_inc(landed, 16)

            with e.Fori(0, L) as l:
                e.wait_ge(params_free, l + 1)
                e.wait_ge(tile_used, l * TILES + SLOTS - 4)
                load_params(l, 0, GAIN_COLS, gains_in_s)
                for k in range(PANELS):
                    e.wait_ge(w_lo_ready, l * SPLITS + (SPLITS + PIECES * max(k - 1, 0)))
                    if k == 0:
                        e.dma_start(panels[:, 0, 0:PANEL // 2], stream[ds(l * PANELS, 1), :, 0:PANEL // 2]
                                    .rearrange("a p n -> p (a n)")).then_inc(half_panel_in, 16)
                        e.dma_start(panels[:, 0, PANEL // 2:PANEL], stream[ds(l * PANELS, 1), :, PANEL // 2:PANEL]
                                    .rearrange("a p n -> p (a n)")).then_inc(panel_in[0], 16)
                        continue
                    e.dma_start(panels[:, k % PSLOTS, :], stream[ds(l * PANELS + k, 1)]
                                .rearrange("a p n -> p (a n)")).then_inc(panel_in[k % PSLOTS], 16)
                    if k == 1:
                        load_params(l, GAIN_COLS, PARAM_COLS, params_in_s)
                    if k == V_PANEL:
                        e.dma_start(keys, keys_in[ds(l, 1)].rearrange("a p n -> p (a n)")).then_inc(keys_in_s, 16)
                    if k == BRANCH_PANEL - 1:
                        e.wait_ge(att_done, l * 6 + 4)
                        e.dma_start(mem_rows, mem_in.rearrange("a (b p) d -> p (a b) d", p=P)).then_inc(mem_in_s, 16)
            e.wait_ge(params_free, L + 1)
            e.dma_start(params[:, 0:D], g_final).then_inc(params_in_s, 16)
            for b in range(NB):
                e.wait_ge(xn_ready, b + 1)
                e.dma_start(out.rearrange("a (b p) d -> b p (a d)", p=P)[b], xn[:, b, :]).then_inc(stored, 16)
            e.wait_ge(stored, 16 * NB)

        @block.tensor
        def _(e):
            def open_unit(l, unit):
                i = PROJ.index(unit)
                e.wait_ge(proj_out[i % 4], l * (PU // 4) + i // 4 + 1)
                return mm[i % 4]

            def open_tp(l, unit):
                i = TRANS.index(unit)
                e.wait_ge(tp_out[i % 2], l * (TU // 2) + i // 2 + 1)
                return tp[i % 2]

            def turn_rows(l, kind, src, units=range(4)):
                for u in units:
                    ps = open_tp(l, f"{kind}{u}")
                    for c in range(2):
                        for b in range(NB):
                            o = c * T + b * P
                            ins = e.transpose(ps[:, o:o + P], src[:, b, (2 * u + c) * P:(2 * u + c + 1) * P], ident)
                    ins.then_inc(tp_done, 1)

            def piece(l, k, i):
                e.wait_ge(w_lo_ready, l * SPLITS + (SPLITS + k * PIECES + i + 1))
                n = (k * PIECES + i) % WSLOTS
                return w_hi[:, n, :], w_lo[:, n, :]

            def wait_turned(l, kind, c):
                if kind and c % 2 == 0:
                    unit = f"{kind}{c // 2}"
                    if unit in PROJ:
                        wait_proj_out(e, l, unit)
                    else:
                        wait_tp_out(e, l, unit)

            def rows_times(l, k, i0, n, units, hi, lo, turns=None):
                ps = {}
                for c in range(n):
                    wait_turned(l, turns, c)
                    wh, wl = piece(l, k, i0 + c)
                    for b in range(NB):
                        if c == 0:
                            ps[b] = open_unit(l, units[b])
                        s = slice(b * P, (b + 1) * P)
                        ins = e.matmul(ps[b][:, :], hi[:, c, s], wh, start=c == 0, stop=False)
                        if b == 0:
                            ins.then_inc(piece_started, 1)
                        e.matmul(ps[b][:, :], hi[:, c, s], wl, start=False, stop=False)
                        ins = e.matmul(ps[b][:, :], lo[:, c, s], wh, start=False, stop=c == n - 1)
                        if c == n - 1:
                            ins.then_inc(proj_done, 1)

            def full_panel(l, k, units, hi=act_hi, lo=act_lo, turns=None):
                rows_times(l, k, 0, KC, units, hi, lo, turns)

            def column_panel(l, k, units, hi=act_hi, lo=act_lo, turns=None, second=None):
                ps = {}
                for c in range(KC):
                    if second and c == 1:
                        second()
                    wait_turned(l, turns, c)
                    wh, wl = piece(l, k, c)
                    for j in range(4):
                        if c == 0 and j % 2 == 0:
                            ps[j // 2] = open_unit(l, units[j // 2])
                        o = ps[j // 2][:, (j % 2) * T:(j % 2 + 1) * T]
                        s = slice(j * P, (j + 1) * P)
                        ins = e.matmul(o, wh[:, s], hi[:, c, :], start=c == 0 and j % 2 == 0, stop=False,
                                       skip_group_check=True)
                        if j == 0:
                            ins.then_inc(piece_started, 1)
                        e.matmul(o, wh[:, s], lo[:, c, :], start=False, stop=False, skip_group_check=True)
                        ins = e.matmul(o, wl[:, s], hi[:, c, :], start=False, stop=c == KC - 1,
                                       skip_group_check=True)
                        if c == KC - 1 and j % 2 == 1:
                            ins.then_inc(proj_done, 1)

            def gate_panel(l, k):
                full_panel(l, GATE_PANEL + k, (f"g{k}0", f"g{k}1"))

            def scores_unit(l, u):
                b, h0 = u // 2, 2 * (u % 2)
                e.wait_ge(att_out, l * 6 + u + 1)
                for m in range(2):
                    for k in range(2):
                        o = (2 * m + k) * 256
                        ins = e.matmul(pair[:, o:o + P * (b + 1)],
                                       qkT[64 * m:64 * m + 64, 0, h0 + k, b * P:(b + 1) * P],
                                       qkT[64 * m:64 * m + 64, 1, h0 + k, 0:P * (b + 1)], start=True, stop=True)
                ins.then_inc(att_done, 1)

            def turn_probs(l, u):
                b = u // 2
                ps = open_tp(l, f"a{u}")
                e.wait_ge(probs_ready, l * 6 + u + 1)
                for k in range(2):
                    for kb in range(b + 1):
                        o = (k * (b + 1) + kb) * P
                        ins = e.transpose(ps[:, o:o + P], probs[:, u % 2, k, kb * P:(kb + 1) * P], ident)
                ins.then_inc(tp_done, 1)

            def probs_times_v(l, b):
                ps = open_unit(l, f"av{b}")
                for h in range(DA_HEADS):
                    for kb in range(b + 1):
                        ins = e.matmul(ps[:, h * P:(h + 1) * P], aT[:, b, h, kb, :],
                                       z[:, kb, 1024 + h * P:1024 + (h + 1) * P], start=kb == 0, stop=kb == b)
                ins.then_inc(proj_done, 1)

            e.wait_ge(zeros_ready, 1)
            e.wait_ge(consts_in_s, 16)
            e.sem_inc(proj_done, PU)
            e.sem_inc(tile_used, SLOTS)
            e.sem_inc(piece_started, AHEAD)

            with e.Fori(0, L) as l:
                e.wait_ge(x_ready, l * 4 + 1)
                turn_rows(l, "nA", x)
                for k in range(6):
                    full_panel(l, Z_PANEL + k, (f"z{k}0", f"z{k}1"), turns="nA" if k == 0 else None)
                e.wait_ge(rope_ready, l + 1)
                for u in range(4):
                    ps = open_tp(l, f"qk{u}")
                    for k in range(2):
                        for b in range(NB):
                            n = (u // 2) * BW + (2 * (u % 2) + k) * P
                            o = k * T + b * P
                            ins = e.transpose(ps[:, o:o + P], z[:, b, n:n + P], ident)
                    ins.then_inc(tp_done, 1)
                wait_tp_out(e, l, "qk2")
                wait_tp_out(e, l, "qk3")
                scores_unit(l, 0)
                e.wait_ge(wide_in_s, 16)
                wait_proj_out(e, l, "z31")
                for u in range(2):
                    ps = open_unit(l, f"pd{u}")
                    for k in range(2):
                        g = 2 * u + k
                        c = 1536 + g * P
                        e.matmul(ps[:, k * T:(k + 1) * T], z[:, 0, c:c + P], pool_m[:, g, 0:T], start=True, stop=False)
                        ins = e.matmul(ps[:, k * T + P:(k + 1) * T], z[:, 1, c:c + P], pool_m[:, g, T:T + P],
                                       start=False, stop=True)
                    ins.then_inc(proj_done, 1)
                gate_panel(l, 0)
                scores_unit(l, 1)
                turn_probs(l, 0)
                gate_panel(l, 1)
                scores_unit(l, 2)
                turn_probs(l, 1)
                gate_panel(l, 2)
                wait_tp_out(e, l, "a0")
                wait_tp_out(e, l, "a1")
                probs_times_v(l, 0)
                scores_unit(l, 3)
                turn_probs(l, 2)
                e.wait_ge(vn_ready, l + 1)
                for b in range(NB):
                    ps = open_unit(l, f"sm{b}")
                    for g in range(4):
                        ins = e.matmul(ps[:, g * P:(g + 1) * P], w_spatialT[:, g, :],
                                       z[:, b, 2560 + g * P:2560 + (g + 1) * P], start=True, stop=True)
                    ins.then_inc(proj_done, 1)
                gate_panel(l, 3)
                turn_probs(l, 3)
                gate_panel(l, 4)
                wait_tp_out(e, l, "a2")
                wait_tp_out(e, l, "a3")
                probs_times_v(l, 1)
                wait_proj_out(e, l, "pd0")
                wait_proj_out(e, l, "pd1")
                e.wait_ge(params_in_s, l * 16 + 16)
                for u in range(2):
                    ps = open_unit(l, f"py{u}")
                    for k in range(2):
                        ins = e.matmul(ps[:, k * T:(k + 1) * T], w_pool[:, 2 * u + k, :], poolT[:, 2 * u + k, :],
                                       start=True, stop=True)
                    ins.then_inc(proj_done, 1)
                gate_panel(l, 5)

                def turn_mixer(kind, c0):
                    for u in range(2):
                        ps = open_tp(l, f"{kind}{u}")
                        for k in range(2):
                            for b in range(NB):
                                n = c0 + (2 * u + k) * P
                                o = k * T + b * P
                                ins = e.transpose(ps[:, o:o + P], xn[:, b, n:n + P], ident)
                        ins.then_inc(tp_done, 1)

                def branch(p, n, turns, between=None):
                    for h in range(2):
                        if h and between:
                            between()
                        rows_times(l, BRANCH_PANEL + p, 4 * h, 4, (f"br{n}{h}0", f"br{n}{h}1"),
                                   br_hi[:, 4 * n:4 * n + 4, :], br_lo[:, 4 * n:4 * n + 4, :],
                                   turns if h == 0 else None)

                wait_proj_out(e, l, "sm0")
                wait_proj_out(e, l, "sm1")
                turn_mixer("s", BW)
                branch(0, 1, "py")
                e.wait_ge(on_ready, l + 1)
                turn_mixer("o", 0)
                branch(1, 2, "s")
                e.wait_ge(mem_ready, l + 1)
                turn_rows(l, "mT", mem_rows, (0, 1))
                branch(2, 0, "o", between=lambda: turn_rows(l, "mT", mem_rows, (2, 3)))
                for h in range(2):
                    wait_proj_out(e, l, f"br0{h}0")
                    wait_proj_out(e, l, f"br0{h}1")
                    turn_rows(l, "m", merged, (2 * h, 2 * h + 1))
                for k in range(2):
                    full_panel(l, OUT_PANEL + k, (f"wo{2 * k}", f"wo{2 * k + 1}"), turns=None if k else "m")
                column_panel(l, K_PANEL, ("km0", "km1"), mem_hi, mem_lo)
                e.wait_ge(x_ready, l * 4 + 2)
                turn_rows(l, "nC", x, (0, 1))
                column_panel(l, K_PANEL + 1, ("km2", "km3"), mem_hi, mem_lo)
                turn_rows(l, "nC", x, (2, 3))
                for k in range(2):
                    column_panel(l, XQ_PANEL + k, (f"xq{2 * k}", f"xq{2 * k + 1}"), turns=None if k else "nC")
                for i in range(4):
                    wait_proj_out(e, l, f"xq{i}")
                    wait_proj_out(e, l, f"km{i}")
                for b in range(NB):
                    e.wait_ge(att_out, l * 6 + 4 + b + 1)
                    for h in range(X_HEADS):
                        for k in range(2):
                            ins = e.matmul(pair[:, h * T:(h + 1) * T], xqT[:, 2 * h + k, b * P:(b + 1) * P],
                                           kmT[:, 2 * h + k, :], start=k == 0, stop=k == 1)
                    ins.then_inc(att_done, 1)
                    full_panel(l, V_PANEL + b, (f"vm{2 * b}", f"vm{2 * b + 1}"), mem_hi, mem_lo)
                for u in range(4):
                    b, h0 = u // 2, 2 * (u % 2)
                    ps = open_tp(l, f"e{u}")
                    e.wait_ge(probs_ready, l * 6 + 4 + b + 1)
                    for k in range(2):
                        for m in range(NB):
                            o = (k * NB + m) * P
                            ins = e.transpose(ps[:, o:o + P], probs[:, b, h0 + k, m * P:(m + 1) * P], ident)
                    ins.then_inc(tp_done, 1)
                wait_tp_out(e, l, "e2")
                wait_tp_out(e, l, "e3")
                for i in range(4):
                    wait_proj_out(e, l, f"vm{i}")
                for u in range(4):
                    ps = open_unit(l, f"co{u}")
                    for k in range(2):
                        c = 2 * u + k
                        for m in range(NB):
                            ins = e.matmul(ps[:, k * T:(k + 1) * T], vm[:, m, c * P:(c + 1) * P], eT[:, c // 2, m, :],
                                           start=m == 0, stop=m == NB - 1)
                    ins.then_inc(proj_done, 1)
                for k in range(2):
                    full_panel(l, XO_PANEL + k, (f"xo{2 * k}", f"xo{2 * k + 1}"), turns=None if k else "co")
                wait_proj_out(e, l, "xo0")
                wait_proj_out(e, l, "xo1")
                turn_rows(l, "nF", x, (0, 1))
                e.wait_ge(x_ready, l * 4 + 3)
                turn_rows(l, "nF", x, (2, 3))

                def expert_scores(i):
                    ps = open_unit(l, f"sc{i}")
                    b, q = i // 4, i % 4
                    for k in range(4):
                        if k % 2 == 0:
                            wait_proj_out(e, l, f"pq{2 * q + k // 2}")
                        hp = 4 * q + k
                        ins = e.matmul(ps[:, k * NK:(k + 1) * NK], peer_qT[:, hp, b * P:(b + 1) * P],
                                       keys[:, hp * NK:(hp + 1) * NK], start=True, stop=True)
                    ins.then_inc(proj_done, 1)

                def both_scores(q):
                    if q == 0:
                        e.wait_ge(keys_in_s, l * 16 + 16)
                    expert_scores(q)
                    expert_scores(4 + q)

                for q in range(4):
                    column_panel(l, PQ_PANEL + q, (f"pq{2 * q}", f"pq{2 * q + 1}"), turns=None if q else "nF",
                                 second=(lambda: both_scores(q - 1)) if q else None)
                both_scores(3)

                with e.Fori(0, NB) as b:
                    e.wait_ge(acc_free, l * NB + b + 1)
                    for h in range(2):
                        e.matmul(pair[:, h * BW:(h + 1) * BW], zeros[:, 0:P], zeros[:, :], start=True, stop=False,
                                 skip_group_check=True)
                    with e.Fori(0, HEADS // 2) as hh:
                        for s in range(2):
                            for j in range(TOPK):
                                e.wait_ge(diag_ready, l * TILES + b * (TILES // NB) + hh * (2 * TOPK)
                                          + s * TOPK + j + 1)
                                for h in range(2):
                                    ins = e.matmul(pair[:, h * BW:(h + 1) * BW], diag[:, j % SLOTS, :],
                                                   tiles[j % SLOTS][:, D + h * BW:D + (h + 1) * BW],
                                                   start=False, stop=False, skip_group_check=True)
                                ins.then_inc(tile_used, 1)

        @block.vector
        def _(e):
            def square(x_rows):
                e.tensor_tensor_reduce(x_rows, x[:, 0, :], x[:, 0, :], 1.0, 0.0, ALU.mult, ALU.add, sq[:, 0:1])

            def norm_factors(l, r):
                e.drain()
                e.wait_ge(sq_ready, l * 3 + r + 1)
                if r == 0:
                    e.tensor_scalar(var[:, r, 2:4], sq[:, :], 4.0 / D, 4 * EPS, ALU.mult, ALU.add)
                e.tensor_scalar(var[:, r, 0:2], sq[:, :], 1.0 / D, EPS, ALU.mult, ALU.add).then_inc(var_ready, 1)

            def rests(l, k, part, end=None):
                for i in range(part, end) if end else (range(0, AHEAD), range(AHEAD, PIECES))[part]:
                    n = k * PIECES + i
                    e.wait_ge(w_hi_ready, l * SPLITS + n + 1)
                    e.tensor_tensor(w_lo[:, n % WSLOTS, :], panels[:, k % PSLOTS, i * PIECE:(i + 1) * PIECE],
                                    w_hi[:, n % WSLOTS, :].bitcast(F32), ALU.subtract).then_inc(w_lo_ready, 1)

            def turn_rest(l, unit):
                e.wait_ge(hi_ready, l * HU + TURNED.index(unit) + 1)
                ps, free = source(e, l, unit)
                hi, lo = turned(unit)
                g = gains(unit)
                if isinstance(g, list):
                    for k in range(2):
                        ins = e.scalar_tensor_tensor(lo[:, k, :], ps[:, k * T:(k + 1) * T], g[k],
                                                     hi[:, k, :].bitcast(F32), ALU.mult, ALU.subtract)
                else:
                    ins = e.scalar_tensor_tensor(lo.rearrange("p c t -> p (c t)"), ps[:, :], 1.0 if g is None else g,
                                                 hi.rearrange("p c t -> p (c t)").bitcast(F32), ALU.mult,
                                                 ALU.subtract)
                ins.then_inc(free, 1)

            def turn_out(l, unit, dst):
                wait_tp_done(e, l, unit)
                e.tensor_copy(dst.rearrange("p c t -> p (c t)"), tbank(unit)[:, :]).then_inc(tfreed(unit), 1)

            def merge(l, n, h):
                for b in range(NB):
                    unit = f"br{n}{h}{b}"
                    wait_proj_done(e, l, unit)
                    g = gates[:, b, n * D + h * BW:n * D + (h + 1) * BW]
                    dst = merged[:, b, h * BW:(h + 1) * BW]
                    if n == BRANCH_ORDER[0]:
                        e.scalar_tensor_tensor(dst, g, 1.0, bank(unit)[:, :], ALU.add, ALU.mult) \
                            .then_inc(freed(unit), 1)
                    else:
                        e.scalar_tensor_tensor(gated[:, b, :], g, 1.0, bank(unit)[:, :], ALU.add, ALU.mult)
                        e.drain()
                        e.tensor_tensor(dst, dst, gated[:, b, :], ALU.add).then_inc(freed(unit), 1)

            def masked_max(l, u):
                b, n = u // 2, P * (u // 2 + 1)
                e.wait_ge(att_done, l * 6 + u + 1)
                mask = const("mask")[:, T - n:T].unsqueeze(1).broadcast_to([P, 4, n])
                src = pair[:, :].rearrange("p (i k) -> p i k", i=4)[:, :, 0:n]
                e.scalar_tensor_tensor(probs[:, u % 2, :, 0:n], src, DA_SCALE, mask, ALU.mult, ALU.add) \
                    .then_inc(att_out, 1)
                e.drain()
                e.tensor_reduce(neg_max[:, u % 2, :], probs[:, u % 2, :, 0:n], AX, ALU.max, negate=True) \
                    .then_inc(max_ready, 1)

            def difference(l, u):
                n = P * (u // 2 + 1)
                v = u % 2
                e.wait_ge(exp_done, l * 6 + u + 1)
                e.reciprocal(row_inv[:, v, :], row_sum[:, v, :])
                e.drain()
                e.tensor_scalar(row_inv[:, v, 2:4], row_inv[:, v, 2:4], lam[:, 0:1], None, ALU.mult)
                e.drain()
                for k in range(2):
                    e.tensor_scalar(probs[:, v, 2 + k, 0:n], probs[:, v, 2 + k, 0:n], row_inv[:, v, 2 + k:3 + k],
                                    None, ALU.mult)
                e.drain()
                for k in range(2):
                    ins = e.scalar_tensor_tensor(probs[:, v, k, 0:n], probs[:, v, k, 0:n], row_inv[:, v, k:k + 1],
                                                 probs[:, v, 2 + k, 0:n], ALU.mult, ALU.add)
                ins.then_inc(probs_ready, 1)

            def cross_max(l, b):
                e.wait_ge(att_done, l * 6 + 4 + b + 1)
                e.tensor_reduce(neg_max[:, b, :], pair[:, :].rearrange("p (i k) -> p i k", i=4), AX, ALU.max,
                                negate=True)
                if b == 0:
                    e.wait_ge(rstd_ready, l * ROOTS + 5)
                e.tensor_scalar(cross_scale[:, b:b + 1], rstd[:, 1, b:b + 1], X_SCALE, None, ALU.mult)
                e.drain()
                e.tensor_scalar(neg_max[:, b, :], neg_max[:, b, :], cross_scale[:, b:b + 1], None, ALU.mult) \
                    .then_inc(max_ready, 1)

            def cross_probs(l, b):
                e.wait_ge(exp_done, l * 6 + 4 + b + 1)
                e.reciprocal(row_inv[:, b, :], row_sum[:, b, :])
                e.drain()
                e.tensor_tensor(probs[:, b, :, :], probs[:, b, :, :],
                                row_inv[:, b, :].unsqueeze(2).broadcast_to([P, 4, T]), ALU.mult) \
                    .then_inc(probs_ready, 1)

            def add_rows(l, unit, b, cols):
                wait_proj_done(e, l, unit)
                dst = x[:, b, cols * BW:(cols + 1) * BW]
                return e.tensor_tensor(dst, bank(unit)[:, :], dst, ALU.add)

            def top_halves(i):
                e.tensor_copy(head_sc[:, :, :], scores[:, ds(i, 1), :].rearrange("p a (h n) -> p (a h) n", h=2))
                e.drain()
                for a in range(2):
                    e.max(top[:, a, 0:8], head_sc[:, a, :])
                e.drain()

            def top_halves_rest():
                for a in range(2):
                    e.max_index(top_ix[:, a, 0:8], top[:, a, 0:8], head_sc[:, a, :])
                    e.match_replace(head_less[:, a, :], top[:, a, 0:8], head_sc[:, a, :], LOWEST)
                e.drain()

            def top_halves_second():
                for a in range(2):
                    e.max(top[:, a, 8:16], head_less[:, a, :])
                e.drain()
                for a in range(2):
                    e.max_index(top_ix[:, a, 8:16], top[:, a, 8:16], head_less[:, a, :])
                e.tensor_tensor(cand.rearrange("p (i j) -> p i j", i=TOPK),
                                top[:, 0, :].unsqueeze(2).broadcast_to([P, TOPK, TOPK]),
                                top[:, 1, :].unsqueeze(1).broadcast_to([P, TOPK, TOPK]), ALU.add)
                e.drain()

            def top_pairs(par_):
                e.tensor_copy(top_ixf[:, :, :], top_ix[:, :, :])
                e.max(best[:, par_, 0:8], cand)
                e.drain()
                e.max_index(pos[:, 0:8], best[:, par_, 0:8], cand)
                e.match_replace(cand_less, best[:, par_, 0:8], cand, LOWEST)
                e.tensor_scalar(best_neg[:, par_:par_ + 1], best[:, par_, 0:1], -1.0, None, ALU.mult)
                e.drain()

            def top_pairs_second(par_):
                e.max(best[:, par_, 8:16], cand_less).then_inc(best_ready, 1)
                e.drain()
                e.max_index(pos[:, 8:16], best[:, par_, 8:16], cand_less)
                e.drain()
                e.tensor_single_scalar(pos_ab[:, 0, :], pos[:, :], 4, ALU.logical_shift_right)
                e.tensor_single_scalar(pos_ab[:, 1, :], pos[:, :], TOPK - 1, ALU.bitwise_and)
                e.drain()

            def top_lookup():
                iota = const("iota").unsqueeze(1).unsqueeze(1).broadcast_to([P, 2, TOPK, TOPK])
                e.tensor_tensor(pick[:, :, :, :], pos_ab[:, :, :].unsqueeze(3).broadcast_to([P, 2, TOPK, TOPK]), iota,
                                ALU.is_equal)
                e.drain()
                e.tensor_tensor(pick[:, :, :, :], pick[:, :, :, :],
                                top_ixf[:, :, :].unsqueeze(2).broadcast_to([P, 2, TOPK, TOPK]), ALU.mult)
                e.drain()

            def top_experts(par_):
                e.tensor_reduce(chosen[:, :, :], pick[:, :, :, :], AX, ALU.add)
                e.drain()
                e.scalar_tensor_tensor(chosen[:, 0, :], chosen[:, 0, :], float(NK), chosen[:, 1, :], ALU.mult, ALU.add)
                e.drain()
                e.tensor_scalar(expert[:, par_, :], chosen[:, 0, :], base[:, :], None, ALU.add) \
                    .then_inc(expert_ready, 1)

            def head_gates(l, i, par_):
                e.wait_ge(gate_exp, l * TOPS + i + 1)
                e.reciprocal(gate_r[:, par_:par_ + 1], gate_s[:, par_:par_ + 1])
                e.drain()
                e.tensor_scalar(gate[:, par_, :], gate_e[:, par_, :], gate_r[:, par_:par_ + 1], None, ALU.mult) \
                    .then_inc(gate_ready, 1)

            def rotation_angles():
                e.wait_ge(consts_in_s, 16)
                e.wait_ge(pos_in_s, 16)
                e.tensor_copy(pos_f[:, :], pos_i[:, :])
                e.drain()
                e.tensor_tensor(ang[:, 0, :, :], pos_f[:, :].unsqueeze(2).broadcast_to([P, NB, HALF]),
                                const("inv").unsqueeze(1).broadcast_to([P, NB, HALF]), ALU.mult)
                e.drain()
                two_pi = 2 * np.pi
                parts, rest = [], two_pi
                for bits in (5, 14, 23):
                    v = np.floor(rest * 2.0 ** bits) / 2.0 ** bits
                    parts.append(float(v))
                    rest -= v
                parts.append(float(rest))
                nearest = 1.5 * 2.0 ** 23
                e.tensor_scalar(ang[:, 1, :, :], ang[:, 0, :, :], 1.0 / two_pi, nearest, ALU.mult, ALU.add)
                e.drain()
                e.tensor_scalar(ang[:, 1, :, :], ang[:, 1, :, :], nearest, None, ALU.subtract)
                e.drain()
                for v in parts:
                    e.scalar_tensor_tensor(ang[:, 0, :, :], ang[:, 1, :, :], -v, ang[:, 0, :, :], ALU.mult, ALU.add)
                    e.drain()
                e.tensor_scalar(ang[:, 3, :, :], ang[:, 0, :, :], 3.1415925, -3.1415925, ALU.min, ALU.max)
                e.drain()
                e.scalar_tensor_tensor(ang[:, 2, :, :], ang[:, 3, :, :], -1.0, ang[:, 3, :, :], ALU.mult, ALU.min)
                e.drain()
                e.tensor_scalar(ang[:, 2, :, :], ang[:, 2, :, :], float(np.pi / 2), None, ALU.add).then_inc(trig_in, 1)

            e.memset(zeros[:, :], 0.0).then_inc(zeros_ready, 1)
            e.memset(half[:, :], -0.5)
            for s in (*proj_out, *tp_out, att_out, acc_free, params_free):
                e.sem_inc(s, 1)
            e.sem_inc(w_lo_ready, SPLITS)
            rotation_angles()
            e.wait_ge(x_in_s, 16)
            e.sem_inc(x_ready, 1)

            with e.Fori(0, L) as l:
                square(xn[:, 0, :])
                e.wait_ge(gains_in_s, l * 16 + 16)
                turn_rest(l, "nA0")
                turn_rest(l, "nA1")
                rests(l, 0, 0)
                turn_rest(l, "nA2")
                turn_rest(l, "nA3")
                rests(l, 0, 1)
                norm_factors(l, 0)
                for k in (1, 2):
                    rests(l, k, 0)
                    if k == 1:
                        e.wait_ge(params_in_s, l * 16 + 16)
                        lq = par("lam_qk")
                        for i in range(2):
                            e.tensor_tensor_reduce(rot[:, i, 0, 0:64], lq[:, 128 * i:128 * i + 64],
                                                   lq[:, 128 * i + 64:128 * i + 128], 1.0, 0.0, ALU.mult, ALU.add,
                                                   lam[:, i:i + 1])
                        e.drain()
                        e.sem_inc(lam_in, 1)
                    rests(l, k, 1)
                rests(l, 3, 0)
                e.wait_ge(trig_done, 1)
                wait_proj_out(e, l, "z10")
                wait_proj_out(e, l, "z11")
                heads = [z[:, b, 0:1024].rearrange("p (h d) -> p h d", d=DA_DIM) for b in range(NB)]
                r = [rot[:, k, :, :].rearrange("p b (h d) -> p b h d", d=HALF) for k in range(4)]
                for b in range(NB):
                    for k, (a, t) in enumerate(((0, 0), (HALF, 1), (0, 1), (HALF, 0))):
                        e.tensor_tensor(r[k][:, b], heads[b][:, :, a:a + HALF],
                                        trig[:, t, b, :].unsqueeze(1).broadcast_to([P, 16, HALF]), ALU.mult)
                e.drain()
                for b in range(NB):
                    e.tensor_tensor(heads[b][:, :, 0:HALF], r[0][:, b], r[1][:, b], ALU.subtract)
                    ins = e.tensor_tensor(heads[b][:, :, HALF:ROT], r[2][:, b], r[3][:, b], ALU.add)
                ins.then_inc(rope_ready, 1)
                rests(l, 3, 1)
                for k in (4, 5):
                    for half_ in range(2):
                        rests(l, k, half_)
                rests(l, GATE_PANEL, 0)
                turn_out(l, "qk0", qkT[:, 0, 0:2, :])
                turn_out(l, "qk2", qkT[:, 1, 0:2, :])
                wait_proj_out(e, l, "z50")
                wait_proj_out(e, l, "z51")
                e.wait_ge(wide_in_s, 16)
                for b in range(NB):
                    e.bn_stats(bn[:, b, :], z[:, b, 2560:3072])
                e.drain()
                for b in range(NB):
                    e.bn_aggr(mv[:, b, :], bn[:, b, :])
                e.drain()
                e.tensor_scalar(var[:, 3, 0:2], mv[:, :, 1], EPS, None, ALU.add).then_inc(var_ready, 1)
                e.wait_ge(lam_exp, l + 1)
                e.tensor_tensor(lam[:, 0:1], lam[:, 3:4], lam[:, 2:3], ALU.subtract)
                e.drain()
                e.tensor_tensor(lam[:, 0:1], lam[:, 0:1], par("lam_init"), ALU.subtract)
                masked_max(l, 0)
                rests(l, GATE_PANEL, 1)
                difference(l, 0)
                rests(l, GATE_PANEL + 1, 0)
                masked_max(l, 1)
                wait_tp_done(e, l, "a0")
                e.tensor_copy(aT[:, 0, 0:2, 0, :], tbank("a0")[:, 0:256].rearrange("p (h q) -> p h q", h=2)) \
                    .then_inc(tfreed("a0"), 1)
                rests(l, GATE_PANEL + 1, 1)
                difference(l, 1)
                e.wait_ge(rstd_ready, l * ROOTS + 2)
                for b in range(NB):
                    e.tensor_scalar(z[:, b, 2560:3072], z[:, b, 2560:3072], mv[:, b, 0:1], rstd[:, 3, b:b + 1],
                                    ALU.subtract, ALU.mult)
                e.drain()
                for b in range(NB):
                    e.tensor_tensor(z[:, b, 2560:3072], z[:, b, 2560:3072], par("sg_ln_g"), ALU.mult)
                rests(l, GATE_PANEL + 2, 0)
                masked_max(l, 2)
                rests(l, GATE_PANEL + 2, AHEAD, 6)
                for b in range(NB):
                    e.tensor_tensor(z[:, b, 2560:3072], z[:, b, 2560:3072], par("sg_ln_b"), ALU.add)
                e.tensor_tensor(w_spatialT, w_spatialT, const("triu").unsqueeze(1).broadcast_to([P, 4, P]),
                                ALU.mult).then_inc(vn_ready, 1)
                rests(l, GATE_PANEL + 2, 6, 8)
                difference(l, 2)
                rests(l, GATE_PANEL + 3, 0)
                masked_max(l, 3)
                wait_tp_done(e, l, "a2")
                e.tensor_copy(aT[:, 1, 0:2, :, :].rearrange("p h k q -> p (h k q)"), tbank("a2")[:, :]) \
                    .then_inc(tfreed("a2"), 1)
                rests(l, GATE_PANEL + 3, AHEAD, 6)
                for b in range(NB):
                    wait_proj_done(e, l, f"sm{b}")
                    for g in range(4):
                        ins = e.scalar_tensor_tensor(xn[:, b, BW + g * P:BW + (g + 1) * P],
                                                     bank(f"sm{b}")[:, g * P:(g + 1) * P],
                                                     par("b_spatial")[:, g:g + 1],
                                                     z[:, b, 2048 + g * P:2048 + (g + 1) * P], ALU.add, ALU.mult)
                    ins.then_inc(freed(f"sm{b}"), 1)
                rests(l, GATE_PANEL + 3, 6, 8)
                difference(l, 3)
                rests(l, GATE_PANEL + 4, 0)
                rests(l, GATE_PANEL + 4, 1)

                def head_squares(b):
                    wait_proj_out(e, l, f"av{b}")
                    if b == 0:
                        wait_tp_done(e, l, "a3")
                    e.tensor_tensor(gated[:, b, :], xn[:, b, 0:BW], xn[:, b, 0:BW], ALU.mult)
                    e.drain()
                    e.tensor_reduce(var[:, 4, 4 * b:4 * b + 4], gated[:, b, :].rearrange("p (h d) -> p h d", h=4), AX,
                                    ALU.add)

                head_squares(0)
                rests(l, GATE_PANEL + 5, 0)
                turn_rest(l, "py0")
                turn_rest(l, "py1")
                rests(l, GATE_PANEL + 5, 1)
                head_squares(1)
                e.drain()
                e.tensor_scalar(var[:, 4, :], var[:, 4, :], 1.0 / P, EPS, ALU.mult, ALU.add).then_inc(var_ready, 1)
                rests(l, BRANCH_PANEL, 0)
                e.wait_ge(mem_sq_ready, l + 1)
                e.tensor_scalar(var[:, 5, 0:2], mem_sq[:, :], 1.0 / D, EPS, ALU.mult, ALU.add).then_inc(var_ready, 1)
                turn_rest(l, "s0")
                turn_rest(l, "s1")
                e.wait_ge(rstd_ready, l * ROOTS + 3)
                e.tensor_scalar(rstd[:, 4, :], rstd[:, 4, :], par("one_less"), None, ALU.mult)
                e.drain()
                heads_o = [xn[:, b, 0:BW].rearrange("p (h d) -> p h d", h=4) for b in range(NB)]
                for b in range(NB):
                    e.tensor_tensor(heads_o[b], heads_o[b],
                                    rstd[:, 4, 4 * b:4 * b + 4].unsqueeze(2).broadcast_to([P, 4, P]), ALU.mult)
                e.drain()
                rests(l, BRANCH_PANEL, 1)
                for b in range(NB):
                    ins = e.tensor_tensor(heads_o[b], heads_o[b],
                                          par("subln_g").unsqueeze(1).broadcast_to([P, 4, P]), ALU.mult)
                ins.then_inc(on_ready, 1)
                n0, n1, n2 = BRANCH_ORDER
                merge(l, n0, 0)
                rests(l, BRANCH_PANEL + 1, 0)
                turn_rest(l, "o0")
                turn_rest(l, "o1")
                merge(l, n0, 1)
                rests(l, BRANCH_PANEL + 1, AHEAD, 6)
                e.wait_ge(rstd_ready, l * ROOTS + 4)
                for b in range(NB):
                    ins = e.tensor_scalar(mem_rows[:, b, :], mem_rows[:, b, :], rstd[:, 5, b:b + 1], None, ALU.mult)
                ins.then_inc(mem_ready, 1)
                rests(l, BRANCH_PANEL + 1, 6, 8)
                merge(l, n1, 0)
                rests(l, BRANCH_PANEL + 2, 0)
                turn_rest(l, "mT0")
                turn_rest(l, "mT1")
                rests(l, BRANCH_PANEL + 2, AHEAD, 5)
                merge(l, n1, 1)
                rests(l, BRANCH_PANEL + 2, 5, 7)
                turn_rest(l, "mT2")
                turn_rest(l, "mT3")
                rests(l, BRANCH_PANEL + 2, 7, 8)
                merge(l, n2, 0)
                merge(l, n2, 1)
                turn_rest(l, "m0")
                turn_rest(l, "m1")
                rests(l, OUT_PANEL, 0)
                turn_rest(l, "m2")
                turn_rest(l, "m3")
                rests(l, OUT_PANEL, 1)
                rests(l, OUT_PANEL + 1, 0)
                for b in range(NB):
                    add_rows(l, f"wo{b}", b, 0).then_inc(freed(f"wo{b}"), 1)
                rests(l, OUT_PANEL + 1, 1)
                rests(l, K_PANEL, 0)
                for b in range(NB):
                    add_rows(l, f"wo{2 + b}", b, 1).then_inc(freed(f"wo{2 + b}"), 1)
                e.drain()
                e.sem_inc(x_ready, 1)
                rests(l, K_PANEL, 1)
                square(xn[:, 0, :])
                norm_factors(l, 1)
                rests(l, K_PANEL + 1, 0)
                turn_rest(l, "nC0")
                turn_rest(l, "nC1")
                rests(l, K_PANEL + 1, 1)
                rests(l, XQ_PANEL, 0)
                turn_rest(l, "nC2")
                turn_rest(l, "nC3")
                rests(l, XQ_PANEL, 1)
                rests(l, XQ_PANEL + 1, 0)
                rests(l, XQ_PANEL + 1, 1)
                rests(l, V_PANEL, 0)
                cross_max(l, 0)
                rests(l, V_PANEL, 1)
                cross_probs(l, 0)
                rests(l, V_PANEL + 1, 0)
                cross_max(l, 1)
                rests(l, V_PANEL + 1, 1)
                cross_probs(l, 1)
                rests(l, XO_PANEL, 0)
                for u in (0, 2):
                    wait_tp_done(e, l, f"e{u}")
                    b = u // 2
                    e.tensor_copy(eT[:, 0:2, :, b * P:(b + 1) * P],
                                  tbank(f"e{u}")[:, :].rearrange("p (h m t) -> p h m t", h=2, m=NB)) \
                        .then_inc(tfreed(f"e{u}"), 1)
                for u in range(4):
                    turn_rest(l, f"co{u}")
                rests(l, XO_PANEL, 1)
                rests(l, XO_PANEL + 1, 0)
                for b in range(NB):
                    add_rows(l, f"xo{b}", b, 0).then_inc(freed(f"xo{b}"), 1)
                rests(l, XO_PANEL + 1, 1)
                rests(l, PQ_PANEL, 0)
                for b in range(NB):
                    add_rows(l, f"xo{2 + b}", b, 1).then_inc(freed(f"xo{2 + b}"), 1)
                e.drain()
                e.sem_inc(x_ready, 1)
                for u in range(4):
                    turn_rest(l, f"nF{u}")
                square(xn[:, 0, :])
                rests(l, PQ_PANEL, AHEAD, 7)
                norm_factors(l, 2)
                rests(l, PQ_PANEL, 7, 8)
                rests(l, PQ_PANEL + 1, 0, 4)
                wait_proj_out(e, l, "sc0")
                top_halves(0)
                rests(l, PQ_PANEL + 1, 4, 6)
                top_halves_rest()
                rests(l, PQ_PANEL + 1, 6, 8)
                top_halves_second()
                rests(l, PQ_PANEL + 2, 0, 2)
                top_pairs(0)
                rests(l, PQ_PANEL + 2, 2, 4)
                top_pairs_second(0)
                e.tensor_copy(base[:, :], const("expert_base")[:, ds(l, 1)])
                rests(l, PQ_PANEL + 2, 4, 6)
                top_lookup()
                rests(l, PQ_PANEL + 2, 6, 7)
                top_experts(0)
                rests(l, PQ_PANEL + 2, 7, 8)
                rests(l, PQ_PANEL + 3, 0, 8)
                head_gates(l, 0, 0)
                e.wait_ge(rstd_ready, l * ROOTS + 6)
                for b in range(NB):
                    e.scalar_tensor_tensor(xn[:, b, :], x[:, b, :], rstd[:, 2, b:b + 1], par("g_ffn_row"), ALU.mult,
                                           ALU.mult)
                e.memset(scores[:, STEPS:TOPS, :], 0.0)
                e.drain()
                e.sem_inc(params_free, 1)
                e.tensor_copy(x_now, xn[:, 0, :])
                with e.Fori(0, NB) as b:
                    with e.Fori(0, HEADS // 2) as hh:
                        for s in range(2):
                            i = b * HEADS + hh * 2 + s
                            for j in range(TOPK):
                                e.drain()
                                e.wait_ge(got[j % SLOTS], ((l * STEPS + i) * (TOPK // SLOTS) + j // SLOTS + 1) * 16)
                                ins = e.tensor_tensor_reduce(products, x_now, tiles[j % SLOTS][:, 0:D], 1.0, 0.0,
                                                             ALU.mult, ALU.add, dots[:, s, j:j + 1])
                                if j % GROUP == GROUP - 1:
                                    ins.then_inc(dots_ready, 1)
                                if j == 2:
                                    if s == 1:
                                        wait_proj_out(e, l, "sc7")
                                        e.nop(nofuse=True)
                                    top_halves(i + 1)
                                if j == 3:
                                    top_halves_rest()
                                if j == 4:
                                    top_halves_second()
                                if j == 5:
                                    top_pairs(1 - s)
                                if j == 6:
                                    top_pairs_second(1 - s)
                                if j == 7:
                                    top_lookup()
                                if j == 8:
                                    top_experts(1 - s)
                                if j == 14:
                                    head_gates(l, i + 1, 1 - s)
                    e.drain()
                    e.tensor_copy(x_now.unsqueeze(1), xn[:, ds(1 - b, 1), :])
                    e.wait_ge(tile_used, SLOTS + l * TILES + b * (TILES // NB) + TILES // NB)
                    e.tensor_tensor(x[:, ds(b, 1), :], x[:, ds(b, 1), :], pair[:, :].unsqueeze(1), ALU.add)
                    e.drain()
                    e.sem_inc(x_ready, 1)
                    e.sem_inc(acc_free, 1)

            square(xn[:, 0, :])
            norm_factors(L, 0)
            e.wait_ge(rstd_ready, L * ROOTS + 1)
            e.wait_ge(params_in_s, L * 16 + 16)
            for b in range(NB):
                e.scalar_tensor_tensor(xn[:, b, :], x[:, b, :], rstd[:, 0, b:b + 1], params[:, 0:D], ALU.mult,
                                       ALU.mult).then_inc(xn_ready, 1)

        @block.scalar
        def _(e):
            def square(l, r):
                e.wait_ge(x_ready, l * 4 + r + 1)
                e.activation(xn[:, 1, :], x[:, 1, :], ACT.Square, accum_out=sq[:, 1:2]).then_inc(sq_ready, 1)

            def out_unit(l, unit, dst, func=ACT.Copy, scale=1.0):
                wait_proj_done(e, l, unit)
                e.activation(dst, bank(unit)[:, :], func, scale=scale).then_inc(freed(unit), 1)

            def highs(l, k, part, end=None):
                for i in range(part, end) if end else (range(0, AHEAD), range(AHEAD, PIECES))[part]:
                    n = k * PIECES + i
                    if k == 0 and i == 0:
                        e.wait_ge(half_panel_in, l * 16 + 16)
                    if i == (PIECES // 2 if k == 0 else 0):
                        wait_panel(e, l, k)
                    e.wait_ge(piece_started, l * SPLITS + n + 1)
                    e.activation(w_hi[:, n % WSLOTS, :], panels[:, k % PSLOTS, i * PIECE:(i + 1) * PIECE],
                                 ACT.Copy).then_inc(w_hi_ready, 1)

            def turn_high(l, unit):
                ps, _free = source(e, l, unit)
                hi, _lo = turned(unit)
                g = gains(unit)
                if isinstance(g, list):
                    for k in range(2):
                        ins = e.activation(hi[:, k, :], ps[:, k * T:(k + 1) * T], ACT.Copy, scale=g[k])
                else:
                    ins = e.activation(hi.rearrange("p c t -> p (c t)"), ps[:, :], ACT.Copy,
                                       scale=1.0 if g is None else g)
                ins.then_inc(hi_ready, 1)

            def turn_out(l, unit, dst):
                wait_tp_done(e, l, unit)
                e.activation(dst.rearrange("p c t -> p (c t)"), tbank(unit)[:, :], ACT.Copy) \
                    .then_inc(tfreed(unit), 1)

            def gates_out(l, k):
                for b in range(NB):
                    out_unit(l, f"g{k}{b}", gates[:, b, k * BW:(k + 1) * BW], ACT.Tanh,
                             rstd[:, 0, 2 + b:3 + b])

            def exps(l, u):
                n = P * (u // 2 + 1)
                e.wait_ge(max_ready, l * 6 + u + 1)
                for i in range(4):
                    ins = e.activation(probs[:, u % 2, i, 0:n], probs[:, u % 2, i, 0:n], ACT.Exp,
                                       bias=neg_max[:, u % 2, i:i + 1], accum_out=row_sum[:, u % 2, i:i + 1])
                ins.then_inc(exp_done, 1)

            def gate_exps(l, i, par_):
                e.wait_ge(best_ready, l * TOPS + i + 1)
                e.activation(gate_e[:, par_, :], best[:, par_, :], ACT.Exp, bias=best_neg[:, par_:par_ + 1],
                             accum_out=gate_s[:, par_:par_ + 1]).then_inc(gate_exp, 1)

            e.wait_ge(trig_in, 1)
            e.activation(trig[:, 0, :, :], ang[:, 2, :, :], ACT.Sin)
            e.activation(trig[:, 1, :, :], ang[:, 3, :, :], ACT.Sin).then_inc(trig_done, 1)
            e.dma_start(consts[:, SMALL_CONSTS:CONST_COLS], consts_in[:, SMALL_CONSTS:CONST_COLS]) \
                .then_inc(wide_in_s, 16)
            e.wait_ge(consts_in_s, 16)

            with e.Fori(0, L) as l:
                e.wait_ge(gains_in_s, l * 16 + 16)
                turn_high(l, "nA0")
                turn_high(l, "nA1")
                highs(l, 0, 0)
                turn_high(l, "nA2")
                turn_high(l, "nA3")
                highs(l, 0, AHEAD, 5)
                square(l, 0)
                highs(l, 0, 5, 8)

                def z_out(k):
                    if k == 0:
                        e.wait_ge(rstd_ready, l * ROOTS + 1)
                    for b in range(NB):
                        out_unit(l, f"z{k}{b}", z[:, b, k * BW:(k + 1) * BW], scale=rstd[:, 0, b:b + 1])

                for k in range(1, 6):
                    highs(l, k, 0)
                    z_out(k - 1)
                    highs(l, k, 1)
                highs(l, GATE_PANEL, 0)
                z_out(5)
                e.wait_ge(lam_in, l + 1)
                e.activation(lam[:, 2:4], lam[:, 0:2], ACT.Exp).then_inc(lam_exp, 1)
                turn_out(l, "qk1", qkT[:, 0, 2:4, :])
                turn_out(l, "qk3", qkT[:, 1, 2:4, :])
                for u in range(2):
                    out_unit(l, f"pd{u}", poolT[:, 2 * u:2 * u + 2, :].rearrange("p c t -> p (c t)"))
                highs(l, GATE_PANEL, AHEAD, 6)
                exps(l, 0)
                highs(l, GATE_PANEL, 6, 8)
                highs(l, GATE_PANEL + 1, 0)
                gates_out(l, 0)
                highs(l, GATE_PANEL + 1, AHEAD, 6)
                exps(l, 1)
                highs(l, GATE_PANEL + 1, 6, 8)
                highs(l, GATE_PANEL + 2, 0)
                gates_out(l, 1)
                wait_tp_done(e, l, "a1")
                e.activation(aT[:, 0, 2:4, 0, :], tbank("a1")[:, 0:256].rearrange("p (h q) -> p h q", h=2), ACT.Copy) \
                    .then_inc(tfreed("a1"), 1)
                highs(l, GATE_PANEL + 2, AHEAD, 6)
                exps(l, 2)
                highs(l, GATE_PANEL + 2, 6, 8)
                highs(l, GATE_PANEL + 3, 0)
                gates_out(l, 2)
                out_unit(l, "av0", xn[:, 0, 0:BW])
                highs(l, GATE_PANEL + 3, AHEAD, 6)
                exps(l, 3)
                highs(l, GATE_PANEL + 3, 6, 8)
                highs(l, GATE_PANEL + 4, 0)
                gates_out(l, 3)
                wait_tp_done(e, l, "a3")
                e.activation(aT[:, 1, 2:4, :, :].rearrange("p h k q -> p (h k q)"), tbank("a3")[:, :], ACT.Copy) \
                    .then_inc(tfreed("a3"), 1)
                highs(l, GATE_PANEL + 4, 1)
                highs(l, GATE_PANEL + 5, 0)
                gates_out(l, 4)
                out_unit(l, "av1", xn[:, 1, 0:BW])
                turn_high(l, "py0")
                turn_high(l, "py1")
                highs(l, GATE_PANEL + 5, 1)
                e.wait_ge(mem_in_s, l * 16 + 16)
                for b in range(NB):
                    e.activation(z[:, 0, 0:D], mem_rows[:, b, :], ACT.Square, accum_out=mem_sq[:, b:b + 1])
                    e.drain()
                e.sem_inc(mem_sq_ready, 1)
                highs(l, BRANCH_PANEL, 0)
                gates_out(l, 5)
                turn_high(l, "s0")
                turn_high(l, "s1")
                highs(l, BRANCH_PANEL, 1)
                highs(l, BRANCH_PANEL + 1, 0)
                turn_high(l, "o0")
                turn_high(l, "o1")
                highs(l, BRANCH_PANEL + 1, 1)
                highs(l, BRANCH_PANEL + 2, 0)
                turn_high(l, "mT0")
                turn_high(l, "mT1")
                highs(l, BRANCH_PANEL + 2, AHEAD, 7)
                turn_high(l, "mT2")
                turn_high(l, "mT3")
                highs(l, BRANCH_PANEL + 2, 7, 8)
                highs(l, OUT_PANEL, 0)
                for u in range(4):
                    turn_high(l, f"m{u}")
                highs(l, OUT_PANEL, 1)
                highs(l, OUT_PANEL + 1, 0)
                highs(l, OUT_PANEL + 1, 1)
                highs(l, K_PANEL, 0)
                highs(l, K_PANEL, AHEAD, 5)
                square(l, 1)
                highs(l, K_PANEL, 5, 8)

                def columns_out(kind, i, dst):
                    out_unit(l, f"{kind}{i}", dst[:, 2 * i:2 * i + 2, :].rearrange("p c t -> p (c t)"))

                def values_out(i):
                    out_unit(l, f"vm{i}", vm[:, i % 2, (i // 2) * BW:(i // 2 + 1) * BW])

                highs(l, K_PANEL + 1, 0)
                columns_out("km", 0, kmT)
                columns_out("km", 1, kmT)
                turn_high(l, "nC0")
                turn_high(l, "nC1")
                highs(l, K_PANEL + 1, 1)
                highs(l, XQ_PANEL, 0)
                columns_out("km", 2, kmT)
                columns_out("km", 3, kmT)
                turn_high(l, "nC2")
                turn_high(l, "nC3")
                highs(l, XQ_PANEL, 1)
                highs(l, XQ_PANEL + 1, 0)
                columns_out("xq", 0, xqT)
                columns_out("xq", 1, xqT)
                highs(l, XQ_PANEL + 1, 1)
                highs(l, V_PANEL, 0)
                columns_out("xq", 2, xqT)
                columns_out("xq", 3, xqT)
                highs(l, V_PANEL, 1)

                def cross_exps(b):
                    e.wait_ge(max_ready, l * 6 + 4 + b + 1)
                    for h in range(X_HEADS):
                        ins = e.activation(probs[:, b, h, :], pair[:, h * T:(h + 1) * T], ACT.Exp,
                                           bias=neg_max[:, b, h:h + 1], scale=cross_scale[:, b:b + 1],
                                           accum_out=row_sum[:, b, h:h + 1])
                    ins.then_inc(exp_done, 1)
                    e.drain()
                    e.sem_inc(att_out, 1)

                cross_exps(0)
                highs(l, V_PANEL + 1, 0)
                values_out(0)
                values_out(1)
                highs(l, V_PANEL + 1, 1)
                cross_exps(1)
                highs(l, XO_PANEL, 0)
                values_out(2)
                values_out(3)
                for u in (1, 3):
                    wait_tp_done(e, l, f"e{u}")
                    b = u // 2
                    e.activation(eT[:, 2:4, :, b * P:(b + 1) * P],
                                 tbank(f"e{u}")[:, :].rearrange("p (h m t) -> p h m t", h=2, m=NB), ACT.Copy) \
                        .then_inc(tfreed(f"e{u}"), 1)
                for u in range(4):
                    turn_high(l, f"co{u}")
                highs(l, XO_PANEL, 1)
                highs(l, XO_PANEL + 1, 0)
                highs(l, XO_PANEL + 1, 1)
                highs(l, PQ_PANEL, 0)
                for u in range(4):
                    turn_high(l, f"nF{u}")
                highs(l, PQ_PANEL, AHEAD, 5)
                square(l, 2)
                highs(l, PQ_PANEL, 5, 8)
                def scores_out(i):
                    if i == 0:
                        e.wait_ge(rstd_ready, l * ROOTS + 6)
                    out_unit(l, f"sc{i}", scores[:, 2 * i:2 * i + 2, :].rearrange("p h n -> p (h n)"),
                             scale=rstd[:, 2, i // 4:i // 4 + 1])

                for q in range(4):
                    if q < 3:
                        highs(l, PQ_PANEL + q + 1, 0)
                    columns_out("pq", 2 * q, peer_qT)
                    columns_out("pq", 2 * q + 1, peer_qT)
                    if q < 3:
                        highs(l, PQ_PANEL + q + 1, AHEAD, AHEAD + 1)
                    scores_out(q)
                    scores_out(4 + q)
                    if q < 3:
                        highs(l, PQ_PANEL + q + 1, AHEAD + 1, PIECES)
                    if q == 2:
                        gate_exps(l, 0, 0)
                with e.Fori(0, NB) as b:
                    with e.Fori(0, HEADS // 2) as hh:
                        for s in range(2):
                            i = b * HEADS + hh * 2 + s
                            e.wait_ge(gate_ready, l * TOPS + i + 1)
                            for g in range(TOPK // GROUP):
                                e.wait_ge(dots_ready, (l * STEPS + i) * (TOPK // GROUP) + g + 1)
                                e.activation(gelu[:, s, GROUP * g:GROUP * (g + 1)],
                                             dots[:, s, GROUP * g:GROUP * (g + 1)], ACT.Gelu)
                                e.drain()
                                for j in range(GROUP * g, GROUP * (g + 1)):
                                    e.activation(weight[:, s, j:j + 1], gelu[:, s, j:j + 1], ACT.Copy,
                                                 scale=gate[:, s, j:j + 1])
                                e.drain()
                                for j in range(GROUP * g, GROUP * (g + 1)):
                                    e.wait_ge(tile_used, (l * STEPS + i) * TOPK + j + 1)
                                    e.activation(diag[:, j % SLOTS, :], ident, ACT.Copy,
                                                 scale=weight[:, s, j:j + 1]).then_inc(diag_ready, 1)
                                if g == TOPK // GROUP - 3:
                                    gate_exps(l, i + 1, 1 - s)
            square(L, 0)

        @block.gpsimd
        def _(e):
            def root(k, r, n):
                e.wait_ge(var_ready, k)
                e.tensor_tensor(rstd[:, r, 0:n], var[:, r, 0:n], half[:, 0:n], ALU.pow).then_inc(rstd_ready, 1)

            with e.Fori(0, L) as l:
                for k, (r, n) in enumerate(((0, 4), (3, 2), (4, 8), (5, 2), (1, 2), (2, 2))):
                    root(l * ROOTS + k + 1, r, n)
                with e.Fori(0, NB) as b:
                    with e.Fori(0, HEADS // 2) as hh:
                        for s in range(2):
                            i = b * HEADS + hh * 2 + s
                            e.wait_ge(expert_ready, l * TOPS + i + 1)
                            e.nop(nofuse=True)
                            for j in range(TOPK):
                                e.wait_ge(tile_used, (l * STEPS + i) * TOPK + j + 1)
                                if s == 0 and j == 5:
                                    wait_proj_done(e, l, "pq7")
                                if s == 0 and j == 7:
                                    wait_proj_done(e, l, "sc7")
                                e.nop(nofuse=True)
                                e.indirect_dma_start(tiles[j % SLOTS], None, experts,
                                                     bass.IndirectOffsetOnAxis(expert[:, s, j:j + 1], 0)) \
                                    .then_inc(got[j % SLOTS], 16)
            root(L * ROOTS + 1, 0, 4)


def _constants():
    c = np.zeros((P, CONST_COLS), np.float32)

    def put(name, v):
        c[:, CONSTS[name][0]:CONSTS[name][1]] = v

    put("ident", np.eye(P))
    q, k = np.arange(P)[:, None], np.arange(P)[None, :]
    put("mask", np.concatenate([np.zeros((P, P)), np.where(k <= q, 0.0, MASKED)], 1))
    put("triu", q <= k)
    s, t = np.arange(T)[:, None], np.arange(T)[None, :]
    cols = []
    for w in WINDOWS:
        m = ((s <= t) & (s > t - w)) / np.minimum(t + 1, w) - (s == t)
        cols.append(np.concatenate([m[0:P, :], m[P:T, P:T]], 1))
    put("pool", np.concatenate(cols, 1))
    put("iota", np.arange(TOPK)[None, :])
    put("inv", (np.float32(ROPE_THETA) ** (-np.arange(0, ROT, 2, dtype=np.float32) / np.float32(ROT)))[None, :])
    put("expert_base", (np.arange(L) * NK * NK)[None, :])
    return c


def _panels(w):
    rows, cols = w.shape
    chunks = rows // P
    width = PANEL // chunks
    return w.reshape(chunks, P, cols // width, width).transpose(2, 1, 0, 3).reshape(cols // width, P, PANEL)


def _stream(a, l):
    branch = [a["w_branch"][l, n].reshape(4, P, 2, BW).transpose(1, 2, 0, 3).reshape(1, P, PANEL)
              for n in BRANCH_ORDER]
    kv = _panels(a["w_xkv"][l])
    return np.concatenate([_panels(a["w_in"][l]), *branch, _panels(a["w_out"][l]), kv[0:2], _panels(a["w_xq"][l]),
                           kv[2:4], _panels(a["w_xo"][l]), _panels(a["w_pq"][l].reshape(D, -1))])


def _params(a, l):
    p = np.zeros((P, PARAM_COLS), np.float32)

    def put(name, v):
        p[:, PARAMS[name][0]:PARAMS[name][1]] = v

    for name in ("g_mix", "g_cross", "g_mem", "g_ffn"):
        put(name, a[name][l].reshape(KC, P).T)
    put("pool_scale", a["pool_scale"][l].reshape(4, P).T)
    put("b_spatial", a["b_spatial"][l].T)
    start = 0.8 - 0.6 * np.exp(-0.3 * l)
    put("lam_init", start)
    put("one_less", 1.0 - start)
    put("lam_qk", a["lam_qk"][l].reshape(1, -1))
    for name in ("subln_g", "sg_ln_g", "sg_ln_b"):
        put(name, a[name][l][None, :])
    put("g_ffn_row", a["g_ffn"][l][None, :])
    put("w_spatial", a["w_spatial"][l].transpose(2, 0, 1).reshape(P, -1))
    put("w_pool", a["w_pool"][l].transpose(1, 0, 2).reshape(P, -1))
    return p


def kernel(**inputs):
    import concourse.bacc as _bacc
    from concourse.bass_utils import run_bass_kernel_spmd as _run

    a = {k: np.asarray(v) for k, v in inputs.items()}
    arrays = {
        "x_in": a["x"],
        "mem_in": a["mem"],
        "pos_in": a["positions"],
        "stream": np.concatenate([_stream(a, l) for l in range(L)]),
        "keys_in": np.stack([k.transpose(3, 0, 1, 2).reshape(P, 2 * HEADS * NK) for k in a["sub_keys"]]),
        "params_in": np.stack([_params(a, l) for l in range(L)]),
        "consts_in": _constants(),
        "g_final": np.broadcast_to(a["g_final"][None, :], (P, D)),
        "experts": np.concatenate([a["peer_u"], a["peer_v"]], 2).reshape(L * NK * NK, 2 * D),
    }
    arrays = {k: np.ascontiguousarray(v) for k, v in arrays.items()}
    nc = _bacc.Bacc("TRN2", target_bir_lowering=False, num_devices=1)
    args = [nc.dram_tensor(k, v.shape, mybir.dt.from_np(v.dtype), kind="ExternalInput").ap() for k, v in arrays.items()]
    out = nc.dram_tensor("out", a["x"].shape, F32, kind="ExternalOutput").ap()
    trunk(nc, *args, out)
    r = _run(nc, [arrays], core_ids=[0])
    return r.results[0]["out"]
```
